# Optimizing a Trainium2 kernel written in Bass

```python
import jax, jax.numpy as jnp
from jax import lax
import numpy as np

D_MODEL = 1024
BATCH = 1
SEQ = 1024
DEPTH = 2

CHUNK = 64
N_MEM = 256
N_HEADS = 4
HEAD_DIM = 64
BRANCH_W = N_HEADS * HEAD_DIM
N_BRANCH = 4
Q_BLOCK = 128
ROPE_BASE = 10000.0
N_EXPERTS = 16
N_GROUPS = 4
EXPERTS_PER_GROUP = N_EXPERTS // N_GROUPS
TOP_K = 2
D_EXPERT = 512
DEEPNORM_ALPHA = (2.0 * DEPTH) ** 0.25
DEEPNORM_BETA = (8.0 * DEPTH) ** -0.25
LN_EPS = 1e-5
GN_EPS = 1e-6
MASK_VALUE = -1e30
FOX_FORGET_BIAS = 2.0

COL_SIZES = (
    BRANCH_W, BRANCH_W, BRANCH_W, N_HEADS,
    BRANCH_W, BRANCH_W, BRANCH_W, BRANCH_W,
    BRANCH_W, BRANCH_W, BRANCH_W, BRANCH_W,
    BRANCH_W,
    N_BRANCH * D_MODEL,
)
SPLIT_POINTS = tuple(int(v) for v in np.cumsum(COL_SIZES)[:-1])
N_IN = int(sum(COL_SIZES))
FOX_F_COL = 3 * BRANCH_W

kernel_name = 'hybrid_fox_retnet_hgrn2_mem_moe_deepnorm'

def _heads(t):
    return t.reshape(t.shape[:-1] + (N_HEADS, t.shape[-1] // N_HEADS))

def _layer_norm(x, g, b):
    xf = x.astype(jnp.float32)
    mu = jnp.mean(xf, axis=-1, keepdims=True)
    var = jnp.mean(jnp.square(xf - mu), axis=-1, keepdims=True)
    y = (xf - mu) * lax.rsqrt(var + LN_EPS)
    return (y * g + b).astype(x.dtype)

def _rope(t, pos):
    half = HEAD_DIM // 2
    inv = ROPE_BASE ** (-2.0 * jnp.arange(half, dtype=jnp.float32) / HEAD_DIM)
    ang = pos[:, None] * inv[None, :]
    cos = jnp.cos(ang)[:, None, :]
    sin = jnp.sin(ang)[:, None, :]
    t1, t2 = t[..., :half], t[..., half:]
    return jnp.concatenate([t1 * cos - t2 * sin, t1 * sin + t2 * cos], axis=-1)

def forgetting_attention(q, k, v, zf):
    S = q.shape[1]
    q = q.astype(jnp.float32)
    k = k.astype(jnp.float32)
    v = v.astype(jnp.float32)
    c = jnp.cumsum(jax.nn.log_sigmoid(zf.astype(jnp.float32)), axis=1).transpose(0, 2, 1)
    scale = HEAD_DIM ** -0.5
    pos = jnp.arange(S)
    outs = []
    for qs in range(0, S, Q_BLOCK):
        qe = qs + Q_BLOCK
        s = jnp.einsum('bqhd,bkhd->bhqk', q[:, qs:qe], k[:, :qe]) * scale
        s = s + c[:, :, qs:qe, None] - c[:, :, None, :qe]
        mask = pos[qs:qe, None] >= pos[None, :qe]
        p = jax.nn.softmax(jnp.where(mask, s, MASK_VALUE), axis=-1)
        outs.append(jnp.einsum('bhqk,bkhd->bqhd', p, v[:, :qe]))
    return jnp.concatenate(outs, axis=1)

def retention(q, k, v, g):
    B, S = q.shape[:2]
    n_chunks = S // CHUNK
    pos = jnp.arange(S, dtype=jnp.float32)
    q = _rope(q.astype(jnp.float32), pos)
    k = _rope(k.astype(jnp.float32), pos) * (HEAD_DIM ** -0.5)
    v = v.astype(jnp.float32)
    log_gamma = jnp.log1p(-jnp.exp2(-5.0 - jnp.arange(N_HEADS, dtype=jnp.float32)))
    idx = jnp.arange(CHUNK, dtype=jnp.float32)
    intra_decay = jnp.exp(log_gamma[:, None, None] * jnp.abs(idx[:, None] - idx[None, :]))
    key_decay = jnp.exp(log_gamma[:, None] * (CHUNK - 1.0 - idx[None, :]))
    query_decay = jnp.exp(log_gamma[:, None] * (idx[None, :] + 1.0))
    chunk_decay = jnp.exp(log_gamma * CHUNK)
    qc = q.reshape(B, n_chunks, CHUNK, N_HEADS, HEAD_DIM)
    kc = k.reshape(B, n_chunks, CHUNK, N_HEADS, HEAD_DIM)
    vc = v.reshape(B, n_chunks, CHUNK, N_HEADS, HEAD_DIM)
    scores = jnp.einsum('bnihd,bnjhd->bnhij', qc, kc) * intra_decay
    o = jnp.einsum('bnhij,bnjhv->bnihv', scores, vc)
    kv = jnp.einsum('bnjhd,hj,bnjhv->nbhdv', kc, key_decay, vc)

    def step(state, kv_n):
        return chunk_decay[None, :, None, None] * state + kv_n, state

    _, states = lax.scan(step, jnp.zeros((B, N_HEADS, HEAD_DIM, HEAD_DIM), jnp.float32), kv)
    o = o + jnp.einsum('bnihd,hi,nbhdv->bnihv', qc, query_decay, states)
    o = o.reshape(B, S, N_HEADS, HEAD_DIM)
    mu = jnp.mean(o, axis=-1, keepdims=True)
    var = jnp.mean(jnp.square(o - mu), axis=-1, keepdims=True)
    o = (o - mu) * lax.rsqrt(var + GN_EPS)
    return o * jax.nn.silu(g.astype(jnp.float32))

def _to_chunks(t):
    B, S, H, K = t.shape
    return t.reshape(B, S // CHUNK, CHUNK, H, K).transpose(1, 0, 3, 2, 4)

def hgrn2(q, i, zf, g, lb, norm_g):
    B, S = q.shape[:2]
    lb = lb.reshape(N_HEADS, HEAD_DIM)
    kf = (1.0 - lb) * jax.nn.sigmoid(-zf.astype(jnp.float32))
    logf = jnp.log1p(-kf)
    xs = (_to_chunks(q.astype(jnp.float32)), _to_chunks(kf), _to_chunks(i.astype(jnp.float32)), _to_chunks(logf))
    causal = jnp.tril(jnp.ones((CHUNK, CHUNK), dtype=bool))[:, :, None]

    def step(state, chunk):
        qn, kn, vn, lfn = chunk
        b = jnp.cumsum(lfn, axis=2)
        rel = b[:, :, :, None, :] - b[:, :, None, :, :]
        decay = jnp.where(causal, jnp.exp(jnp.where(causal, rel, 0.0)), 0.0)
        a = jnp.einsum('bhik,bhjk,bhijk->bhij', qn, kn, decay)
        o = jnp.einsum('bhij,bhjv->bhiv', a, vn) + jnp.einsum('bhik,bhkv->bhiv', qn * jnp.exp(b), state)
        b_last = b[:, :, -1:, :]
        new_state = jnp.exp(b_last[:, :, 0, :])[..., None] * state + jnp.einsum('bhjk,bhjv->bhkv', kn * jnp.exp(b_last - b), vn)
        return new_state, o

    _, o = lax.scan(step, jnp.zeros((B, N_HEADS, HEAD_DIM, HEAD_DIM), jnp.float32), xs)
    o = o.transpose(1, 0, 3, 2, 4).reshape(B, S, N_HEADS, HEAD_DIM)
    o = o * lax.rsqrt(jnp.mean(jnp.square(o), axis=-1, keepdims=True) + GN_EPS) * norm_g.astype(jnp.float32)
    return o * jax.nn.silu(g.astype(jnp.float32))

def memory_attention(q, mk, mv):
    s = jnp.einsum('bshd,bmhd->bhsm', q.astype(jnp.float32), mk.astype(jnp.float32)) * (HEAD_DIM ** -0.5)
    p = jax.nn.softmax(s, axis=-1)
    return jnp.einsum('bhsm,bmhd->bshd', p, mv.astype(jnp.float32))

def grouped_moe(x, w_router, b_router, w_e_in, w_e_out):
    B, S, D = x.shape
    T = B * S
    xt = x.reshape(T, D)
    probs = jax.nn.softmax((xt @ w_router + b_router).astype(jnp.float32), axis=-1)
    grouped = probs.reshape(T, N_GROUPS, EXPERTS_PER_GROUP)
    g_sel = jnp.argmax(jnp.max(grouped, axis=-1), axis=-1)
    in_group = jnp.take_along_axis(grouped, g_sel[:, None, None], axis=1)[:, 0]
    top_p, top_i = lax.top_k(in_group, TOP_K)
    expert = g_sel[:, None] * EXPERTS_PER_GROUP + top_i
    weight = top_p / jnp.sum(top_p, axis=-1, keepdims=True)
    flat_e = expert.reshape(-1)
    order = jnp.argsort(flat_e)
    tok = order // TOP_K
    xs = xt[tok]
    group_sizes = jnp.bincount(flat_e, length=N_EXPERTS).astype(jnp.int32)
    h = lax.ragged_dot(xs, w_e_in, group_sizes)
    h_gate, h_up = jnp.split(h, 2, axis=-1)
    y = lax.ragged_dot(jax.nn.silu(h_gate) * h_up, w_e_out, group_sizes)
    y = y * weight.reshape(-1)[order][:, None].astype(y.dtype)
    out = jnp.zeros_like(xt).at[tok].add(y.astype(xt.dtype))
    return out.reshape(B, S, D)

def setup_inputs(seed: int = 0) -> dict:
    key = jax.random.key(seed)
    ks = jax.random.split(key, 16)
    nrm = jax.random.normal
    f32 = jnp.float32
    x = nrm(ks[0], (BATCH, SEQ, D_MODEL), f32)
    mem = nrm(ks[1], (BATCH, N_MEM, D_MODEL), f32)
    w_in = nrm(ks[2], (DEPTH, D_MODEL, N_IN), f32) * D_MODEL ** -0.5
    b_in = 0.02 * nrm(ks[3], (DEPTH, N_IN), f32)
    b_in = b_in.at[:, FOX_F_COL:FOX_F_COL + N_HEADS].add(FOX_FORGET_BIAS)
    w_mem_kv = nrm(ks[4], (DEPTH, D_MODEL, 2 * BRANCH_W), f32) * D_MODEL ** -0.5
    hgrn_lb = 1.0 + 0.1 * nrm(ks[5], (DEPTH, BRANCH_W), f32)
    hgrn_norm_g = 1.0 + 0.1 * nrm(ks[6], (DEPTH, HEAD_DIM), f32)
    w_branch = nrm(ks[7], (DEPTH, N_BRANCH, BRANCH_W, D_MODEL), f32) * (BRANCH_W ** -0.5) * DEEPNORM_BETA
    w_out = nrm(ks[8], (DEPTH, D_MODEL, D_MODEL), f32) * (D_MODEL ** -0.5) * DEEPNORM_BETA
    ln_g = 1.0 + 0.1 * nrm(ks[9], (DEPTH, 2, D_MODEL), f32)
    ln_b = 0.02 * nrm(ks[10], (DEPTH, 2, D_MODEL), f32)
    w_router = nrm(ks[11], (D_MODEL, N_EXPERTS), f32) * D_MODEL ** -0.5
    b_router = 0.01 * nrm(ks[12], (N_EXPERTS,), f32)
    w_e_in = nrm(ks[13], (DEPTH, N_EXPERTS, D_MODEL, 2 * D_EXPERT), f32) * D_MODEL ** -0.5
    w_e_out = nrm(ks[14], (DEPTH, N_EXPERTS, D_EXPERT, D_MODEL), f32) * (D_EXPERT ** -0.5) * DEEPNORM_BETA
    return {'x': x, 'mem': mem, 'w_in': w_in, 'b_in': b_in, 'w_mem_kv': w_mem_kv,
            'hgrn_lb': hgrn_lb, 'hgrn_norm_g': hgrn_norm_g, 'w_branch': w_branch, 'w_out': w_out,
            'ln_g': ln_g, 'ln_b': ln_b, 'w_router': w_router, 'b_router': b_router,
            'w_e_in': w_e_in, 'w_e_out': w_e_out}

def reference(x, mem, w_in, b_in, w_mem_kv, hgrn_lb, hgrn_norm_g, w_branch, w_out,
              ln_g, ln_b, w_router, b_router, w_e_in, w_e_out):
    B, S, D = x.shape
    lb_all = jax.nn.softmax(hgrn_lb.astype(jnp.float32), axis=0)
    lb_all = jnp.cumsum(lb_all, axis=0) - lb_all[0:1]
    for l in range(DEPTH):
        proj = x @ w_in[l] + b_in[l]
        (fq, fk, fv, ff, rq, rk, rv, rg, hf, hi, hq, hg, mq, gate) = jnp.split(proj, SPLIT_POINTS, axis=-1)
        o_fox = forgetting_attention(_heads(fq), _heads(fk), _heads(fv), ff)
        o_ret = retention(_heads(rq), _heads(rk), _heads(rv), _heads(rg))
        o_hg = hgrn2(_heads(hq), _heads(hi), _heads(hf), _heads(hg), lb_all[l], hgrn_norm_g[l])
        mk, mv = jnp.split(mem @ w_mem_kv[l], 2, axis=-1)
        o_mem = memory_attention(_heads(mq), _heads(mk), _heads(mv))
        branches = jnp.stack([o_fox, o_ret, o_hg, o_mem], axis=2).reshape(B, S, N_BRANCH, BRANCH_W).astype(x.dtype)
        up = jnp.einsum('bsnc,ncd->bsnd', branches, w_branch[l])
        gates = jax.nn.sigmoid(gate.reshape(B, S, N_BRANCH, D))
        mixed = jnp.sum(gates * up, axis=2) @ w_out[l]
        x = _layer_norm(DEEPNORM_ALPHA * x + mixed, ln_g[l, 0], ln_b[l, 0])
        x = _layer_norm(DEEPNORM_ALPHA * x + grouped_moe(x, w_router, b_router, w_e_in[l], w_e_out[l]), ln_g[l, 1], ln_b[l, 1])
    return x


_drawn_inputs = setup_inputs


def setup_inputs(seed=0):
    import zlib

    import numpy as np

    out = dict(_drawn_inputs(seed))
    spreads = {}
    factors = {'hgrn_lb': 3.127}
    for name, (base, spread) in spreads.items():
        noise = np.random.default_rng([zlib.crc32(name.encode()), seed]).standard_normal(out[name].shape)
        drawn = base * np.exp(spread * noise) if base else spread * noise
        out[name] = __import__('jax').numpy.asarray(drawn.astype(out[name].dtype))
    for name, factor in factors.items():
        out[name] = (out[name] * factor).astype(out[name].dtype)
    return out
```

```python
from contextlib import ExitStack

import concourse.bass as bass
from concourse import mybir

F32 = mybir.dt.float32
I32 = mybir.dt.int32
U32 = mybir.dt.uint32
ALU = mybir.AluOpType
ACT = mybir.ActivationFunctionType
AX = mybir.AxisListType

P = 128
LAYERS = 2
T = 1024
D = 1024
NT = T // P
KD = D // P
H = 4
HD = 64
BW = H * HD
NBR = 4
N_MEM = 256
MT = N_MEM // P
CH = 64
E = 16
NG = 4
EPG = E // NG
FE = 512
KF = FE // P
HALF = 512
ALPHA = (2.0 * LAYERS) ** 0.25
LN_EPS = 1e-5
GN_EPS = 1e-6
QK_SCALE = HD ** -0.5
NEG = -1e30

C_FQ, C_FK, C_FV, C_FF = 0, BW, 2 * BW, 3 * BW
C_RQ = 3 * BW + H
C_HF = C_RQ + 4 * BW
C_MQ = C_HF + 4 * BW
C_GATE = C_MQ + BW
N_IN = C_GATE + NBR * D
N_NAT = C_MQ - C_FV

TILES = 2 * T // P + E
UNITS = 18
GATE_U, OUT_U = 8, 16
ATT = H + 1

CONST = {}
_at = 0
for _name, _width in (("ident", 128), ("causal", 128), ("rmask", 512), ("qdec", 256), ("kdec", 4), ("gtile", 2),
                      ("cos", 256), ("sin", 512), ("c_mid", 128), ("c_cum", 128), ("c_rest", 128), ("c_end", 2),
                      ("before", 128), ("ones", 128), ("iota4", 4), ("iota16", 16), ("iota32", 32), ("thr", 8)):
    CONST[_name] = (_at, _at + _width)
    _at += _width
N_CONST = _at


def trunk(nc, x, mem, w_in, b_in, w_mem_kv, hgrn_lb, hgrn_norm_g, w_branch, w_out, ln_g, ln_b,
          w_router, b_router, w_e_in, w_e_out, consts, chunk_mask, out):
    with ExitStack() as ctx:
        def sb(name, shape, dt=F32):
            return ctx.enter_context(nc.sbuf_tensor(name, shape, dt))

        def pb(name):
            return ctx.enter_context(nc.psum_tensor(name, [P, 2, HALF], F32))

        per = {}

        def sem(name, per_layer=0):
            s = ctx.enter_context(nc.semaphore(name))
            per[name] = per_layer
            return s

        def dram(name, shape):
            return nc.dram_tensor(name, shape, F32, kind="Internal").ap()

        x_all = dram("x_all", [LAYERS + 1, T, D])
        rows = dram("rows", [TILES * P, D])
        keep_rate = dram("keep_rate", [LAYERS, BW])

        XT = sb("XT", [P, KD * T])
        OT = sb("OT", [P, 8 * T])
        RA = sb("RA", [P, 8 * T])
        RC = sb("RC", [P, 8 * T])
        W = [sb(f"W{i}", [P, 8, HALF]) for i in range(2)]
        WK = sb("WK", [P, 4096])
        BR = sb("BR", [P, N_NAT])
        MKV = sb("MKV", [P, 4, BW])
        CO = sb("CO", [P, N_CONST])
        hmask = sb("hmask", [P, P], I32)
        bT = sb("bT", [P, 6 + NBR * KD])
        omlb = sb("omlb", [P, BW])
        ngain = sb("ngain", [P, HD])
        wr = sb("wr", [P, KD, E])
        brt = sb("brt", [P, E])
        ON = sb("ON", [P, 2, BW])
        ZF = sb("ZF", [P, 4, NT * H])
        nm = sb("nm", [P, 2, 8])
        rs = sb("rs", [P, 2, 4])
        rstate = sb("rstate", [P, 2, HD])
        hstate = sb("hstate", [P, 2, 2, 2, HD])
        hdec = sb("hdec", [P, 2, 2])
        st = sb("st", [P, 32])
        m12 = sb("m12", [P, 4, NT])
        slots = sb("slots", [P, 2, NT], U32)
        tab = sb("tab", [1, TILES + 2], U32)
        tabf = sb("tabf", [P, TILES + 2])

        PA, PB, PC, PD = pb("PA"), pb("PB"), pb("PC"), pb("PD")

        def co(name):
            a, b = CONST[name]
            return CO[:, a:b]

        ident = co("ident")
        XTk = XT[:, :].rearrange("p (k t) -> p k t", k=KD)
        OTk = OT[:, :].rearrange("p (c t) -> p c t", c=8)
        memT = RA[:, 0:KD * N_MEM].rearrange("p (k m) -> p k m", k=KD)
        qkT = RC[:, 0:6 * T].rearrange("p (c t) -> p c t", c=6)
        FV = RC[:, 6 * T:8 * T].rearrange("p (t c) -> p t c", t=NT)
        RN = RA[:, :].rearrange("p (t c) -> p t c", t=NT)
        HN = RC[:, :].rearrange("p (t c) -> p t c", t=NT)
        MIXT = RA[:, :].rearrange("p (k t) -> p k t", k=KD)
        X1 = RC[:, :].rearrange("p (t c) -> p t c", t=NT)
        cb = OT[:, 2 * T:6 * T].rearrange("p (h t) -> p h t", h=H)
        WBR = [BR[:, i * T:(i + 1) * T].rearrange("p (c m) -> p c m", c=8) for i in range(2)]
        lnp = [XT[:, i * D:(i + 1) * D] for i in range(4)]
        xres = [XT[:, (4 + i) * D:(5 + i) * D] for i in range(2)]
        WEI = OTk
        WEO = RA[:, 0:4 * T].rearrange("p (k n) -> p k n", k=KF)
        ROW = RA[:, 4 * T:5 * T]
        ROWT = RA[:, 6 * T:7 * T]

        b_rows = WK[0:6 + NBR * KD, 2 * T:2 * T + P]

        def flat(psum, n=2 * HALF):
            return psum[:, :, :].rearrange("p a b -> p (a b)")[:, 0:n]

        def heads(ap, n=H):
            return ap.rearrange("p (h d) -> p h d", h=n)

        def by_bank(psum, n):
            return psum[:, :, 0:2 * n].rearrange("p a (j d) -> p j a d", j=2)

        def over4(ap):
            return ap.rearrange("p (j a) -> p j a", j=2).unsqueeze(3).to_broadcast([P, 2, 2, HD])

        def paired(ap):
            return ap.rearrange("p (j a d) -> p j a d", j=2, a=2)

        def perm(h):
            return (h % 2) * 2 + h // 2

        def over(ap, n):
            return ap.unsqueeze(2).to_broadcast([ap.shape[0], ap.shape[1], n])

        c_ld = sem("c_ld")
        x0_ld = sem("x0_ld")
        zero_ok = sem("zero_ok")
        zero_st = sem("zero_st")
        lb_ld = sem("lb_ld")
        lb_v = sem("lb_v")
        lb_a = sem("lb_a")
        lb_st = sem("lb_st")
        par_ld = sem("par_ld", 6 * 16)
        nat_ld = [sem(f"nat_ld{i}", 5 * 16) for i in range(2)]
        bt_tr = sem("bt_tr", 1)
        nat_tr = sem("nat_tr", NT + MT)
        nat_a = sem("nat_a", NT + MT)
        nat_v = sem("nat_v", NT + MT)
        w_ld = [sem(f"w_ld{i}", UNITS // 2 * 64) for i in range(2)]
        w_used = sem("w_used", UNITS)
        pj = sem("pj", 56)
        pj_a = sem("pj_a", 16)
        pj_v = sem("pj_v", 40)
        z_v = sem("z_v", 1)
        z_a = sem("z_a", 1)
        lf_tr = sem("lf_tr", 1)
        c_row = sem("c_row", 1)
        cb_mm = sem("cb_mm", H)
        cb_cp = sem("cb_cp", H)
        s_mm = sem("s_mm", NT * ATT)
        s_rd = sem("s_rd", NT * H)
        mx_ok = sem("mx_ok", NT * ATT)
        p_ok = sem("p_ok", NT * ATT)
        pt_tr = sem("pt_tr", NT * ATT)
        pt_cp = sem("pt_cp", NT * ATT)
        pv_mm = sem("pv_mm", NT * ATT)
        o_ev = sem("o_ev", NT * ATT)
        ot_tr = sem("ot_tr", 4 * NT)
        ot_cp = sem("ot_cp", 4 * NT)
        r_sil = sem("r_sil", 1)
        r_rot = sem("r_rot", NT)
        r_tr = sem("r_tr", NT)
        r_qk = sem("r_qk", NT)
        r_sc = sem("r_sc", NT)
        r_mk = sem("r_mk", NT)
        r_o = sem("r_o", NT)
        r_var = sem("r_var", NT)
        r_rstd = sem("r_rstd", NT)
        r_on = sem("r_on", NT)
        h_sig = sem("h_sig", 1)
        h_kf = sem("h_kf", 1)
        h_sil = sem("h_sil", 1)
        h_lf = sem("h_lf", NT)
        h_b = sem("h_b", NT)
        h_e = sem("h_e", NT)
        h_pr = sem("h_pr", NT)
        h_kv = sem("h_kv", NT)
        h_tr = sem("h_tr", NT)
        h_tc = sem("h_tc", NT)
        h_a = sem("h_a", NT)
        h_st = sem("h_st", NT)
        h_am = sem("h_am", NT)
        h_o = sem("h_o", NT)
        h_sq = sem("h_sq", NT)
        h_var = sem("h_var", NT)
        h_rstd = sem("h_rstd", NT)
        h_on = sem("h_on", NT)
        wbr_ld = [sem(f"wbr_ld{i}", 4 * 16) for i in range(2)]
        wbr_used = sem("wbr_used", KD)
        g_mm = sem("g_mm", 64)
        g_sig = sem("g_sig", 64)
        g_mul = sem("g_mul", 64)
        mix_ok = sem("mix_ok", 16)
        lnp_ld = sem("lnp_ld", 4 * 16)
        xr_ld = [sem(f"xr_ld{i}", 4 * 16) for i in range(2)]
        o_mm = sem("o_mm", NT)
        o_rd = sem("o_rd", NT)
        o_var = sem("o_var", NT)
        o_rstd = sem("o_rstd", NT)
        o_nrm = sem("o_nrm", NT)
        o_x1 = sem("o_x1", NT)
        x1_tr = sem("x1_tr", NT)
        x1_cp = sem("x1_cp", NT)
        lg_mm = sem("lg_mm", NT)
        rt_v = sem("rt_v", 1)
        rt_a = sem("rt_a", 1)
        sel_ok = sem("sel_ok", 1)
        rank_mm = sem("rank_mm", 1)
        tab_ok = sem("tab_ok", 1)
        disp = sem("disp", 2 * NT * 16)
        row_ld = sem("row_ld")
        row_tr = sem("row_tr")
        row_cp = sem("row_cp")
        wei_ld = [sem(f"wei_ld{k}") for k in range(KD)]
        wei_used = sem("wei_used")
        weo_ld = [sem(f"weo_ld{k}") for k in range(KF)]
        weo_used = sem("weo_used")
        hid_sil = sem("hid_sil")
        hid_ok = sem("hid_ok")
        hid_tr = sem("hid_tr")
        hid_cp = sem("hid_cp")
        y_ev = sem("y_ev")
        y_st = sem("y_st")
        y_ld = [sem(f"y_ld{i}", 8 * 16) for i in range(2)]
        y_used = sem("y_used", NT)
        f_var = sem("f_var", NT)
        f_rstd = sem("f_rstd", NT)
        f_nrm = sem("f_nrm", NT)
        f_x2 = sem("f_x2", NT)
        x2_st = [sem(f"x2_st{i}", 4 * 32) for i in range(2)]
        passed = sem("passed")

        def att_units():
            return [(t, i) for t in range(NT) for i in range(ATT)]

        block = ctx.enter_context(nc.Block())

        @block.sync
        def _(sp):
            sp.dma_start(CO[:, :], consts).then_inc(c_ld, 16)
            sp.dma_start(hmask[:, :], chunk_mask).then_inc(c_ld, 16)
            sp.dma_start(wr[:, :, :], w_router.rearrange("(k p) e -> p k e", p=P)).then_inc(c_ld, 16)
            sp.dma_start(brt[:, :], b_router.unsqueeze(0).to_broadcast([P, E])).then_inc(c_ld, 16)
            with sp.Fori(0, LAYERS) as l:
                at = lambda s, n: l * per[s.name] + n

                def load_unit(u):
                    slot = u % 2
                    sp.wait_ge(w_used, at(w_used, u + 1))
                    if u == 0:
                        c0, n, src = 0, 2 * BW, w_mem_kv
                    elif u in (1, 2, 3):
                        c0, n = {1: (C_FQ, 2 * BW), 2: (C_MQ, BW), 3: (C_FV, BW + H)}[u]
                        src = w_in
                    elif u < GATE_U:
                        c0, n, src = C_RQ + (u - 4) * HALF, HALF, w_in
                    else:
                        c0, n, src = (u - OUT_U) * HALF, HALF, w_out
                    for q in range(4):
                        sp.dma_start(W[slot][:, 2 * q:2 * q + 2, 0:n],
                                     src[l, 256 * q:256 * q + 256, c0:c0 + n].rearrange("(k p) n -> p k n", p=P)
                                     ).then_inc(w_ld[slot], 16)

                load_unit(0)
                load_unit(1)
                sp.wait_ge(x0_ld, 16)
                sp.wait_ge(x2_st[0], at(x2_st[0], 32))
                sp.wait_ge(x2_st[1], at(x2_st[1], 32))
                for t in range(NT + MT):
                    sp.wait_ge(nat_tr, at(nat_tr, t + 1))
                    src = x_all[l, t * P:(t + 1) * P, :] if t < NT else mem[0, (t - NT) * P:(t - NT + 1) * P, :]
                    sp.dma_start(WK[:, (t % 2) * D:(t % 2 + 1) * D], src).then_inc(nat_ld[t % 2], 16)
                for u in range(2, GATE_U):
                    load_unit(u)
                sp.wait_ge(pj_v, at(pj_v, 40))
                sp.sem_inc(passed, 1)
                with sp.Fori(0, KD // 2) as dd:
                    for b in range(2):
                        d = dd * 2 + b
                        sp.wait_ge(w_used, at(w_used, GATE_U + 1) + d)
                        for n in range(NBR):
                            sp.dma_start(W[b][:, :, n * P:(n + 1) * P],
                                         w_in[l, :, bass.ds(C_GATE + n * D + d * P, P)].rearrange(
                                             "(k p) c -> p k c", p=P)).then_inc(w_ld[b], 16)
                        sp.wait_ge(wbr_used, at(wbr_used, 1) + d)
                        sp.dma_start(WBR[b], w_branch[l, :, :, bass.ds(d * P, P)].rearrange(
                            "n (j p) c -> p (n j) c", p=P)).then_inc(wbr_ld[b], 16)
                load_unit(OUT_U)
                load_unit(OUT_U + 1)
                sp.wait_ge(g_mm, at(g_mm, 64))
                for i, src in enumerate((ln_g, ln_b, ln_g, ln_b)):
                    sp.dma_start(lnp[i], src[l, i // 2:i // 2 + 1, :].to_broadcast([P, D])).then_inc(lnp_ld, 16)
                for t in range(NT):
                    sp.wait_ge(o_rd, at(o_rd, t + 1))
                    sp.dma_start(xres[t % 2], x_all[l, t * P:(t + 1) * P, :]).then_inc(xr_ld[t % 2], 16)

                sp.wait_ge(tab_ok, at(tab_ok, 1))
                sp.sem_inc(passed, 1)
                n_tiles = sp.value_load(tab[0:1, TILES:TILES + 1], min_val=E, max_val=TILES - 1)
                g0 = sp.value_load(tab[0:1, TILES + 1:TILES + 2], min_val=0, max_val=TILES)
                sp.wait_ge(zero_st, 16)
                sp.wait_ge(disp, at(disp, 2 * NT * 16))
                sp.dma_start(ROW, rows[0:P, :]).then_inc(row_ld, 16)
                with sp.Fori(0, n_tiles) as i:
                    g = g0 + i
                    e = sp.value_load(tab[0:1, bass.ds(i, 1)], min_val=0, max_val=E - 1)
                    for k in range(KD):
                        sp.wait_ge(wei_used, g * KD + (k + 1))
                        sp.dma_start(WEI[:, k, :], w_e_in[l, e, k * P:(k + 1) * P, :]).then_inc(wei_ld[k], 16)
                    sp.wait_ge(row_tr, g + l + 1)
                    sp.dma_start(ROW, rows[bass.ds(i * P + P, P), :]).then_inc(row_ld, 16)
                    for k in range(KF):
                        sp.wait_ge(weo_used, g * KF + (k + 1))
                        sp.dma_start(WEO[:, k, :], w_e_out[l, e, k * P:(k + 1) * P, :]).then_inc(weo_ld[k], 16)
                sp.sem_inc(passed, 1)
            for i in range(2):
                sp.wait_ge(x2_st[i], LAYERS * per[x2_st[i].name] + 32)

        def gain(pool, l, t):
            pool.wait_ge(f_nrm, l * NT + t + 1)
            r = OT[:, (4 + t % 2) * D:(5 + t % 2) * D]
            nc.gpsimd.tensor_tensor(r, r, lnp[2], ALU.mult)
            pool.drain()
            nc.gpsimd.tensor_tensor(r, r, lnp[3], ALU.add).then_inc(f_x2, 1)

        @block.gpsimd
        def _(pool):
            pool.dma_start(x_all[0], x[0]).then_inc(x0_ld, 16)
            pool.dma_start(WK[0:1, 2048:2048 + 2 * BW], hgrn_lb.rearrange("l (a c) -> a (l c)", a=1)
                           ).then_inc(lb_ld, 16)
            pool.wait_ge(lb_v, 2)
            pool.dma_start(keep_rate.rearrange("l (a c) -> a (l c)", a=1), WK[0:1, 3072:3072 + 2 * BW]
                           ).then_inc(lb_st, 16)
            pool.wait_ge(lb_st, 16)
            with pool.Fori(0, LAYERS) as l:
                at = lambda s, n: l * per[s.name] + n
                pool.dma_start(BR[:, :], b_in[bass.ds(l, 1), C_FV:C_MQ].to_broadcast([P, N_NAT])).then_inc(par_ld, 16)
                for a, c0, n in ((0, C_FQ, 4), (4, C_MQ, 2), (6, C_GATE, NBR * KD)):
                    pool.dma_start(b_rows[a:a + n, :], b_in[l, c0:c0 + n * P].rearrange("(c p) -> c p", p=P)
                                   ).then_inc(par_ld, 16)
                pool.dma_start(ngain[:, :], hgrn_norm_g[bass.ds(l, 1), :].to_broadcast([P, HD])).then_inc(par_ld, 16)
                pool.dma_start(omlb[:, :], keep_rate[bass.ds(l, 1), :].to_broadcast([P, BW])).then_inc(par_ld, 16)
                for t in range(NT):
                    if t == 0:
                        pool.wait_ge(lnp_ld, at(lnp_ld, 64))
                    pool.wait_ge(o_nrm, at(o_nrm, t + 1))
                    r = WK[:, (t % 2) * D:(t % 2 + 1) * D]
                    nc.gpsimd.tensor_tensor(r, r, lnp[0], ALU.mult)
                    pool.drain()
                    nc.gpsimd.tensor_tensor(X1[:, t, :], r, lnp[1], ALU.add).then_inc(o_x1, 1)
                pool.wait_ge(tab_ok, at(tab_ok, 1))
                pool.wait_ge(zero_st, 16)
                pool.wait_ge(o_x1, at(o_x1, NT))
                pool.sem_inc(passed, 1)
                for t in range(NT):
                    for j in range(2):
                        nc.gpsimd.indirect_dma_start(
                            rows, bass.IndirectOffsetOnAxis(slots[:, j, t:t + 1], 0), X1[:, t, :], None
                        ).then_inc(disp, 16)
                n_tiles = pool.value_load(tab[0:1, TILES:TILES + 1], min_val=E, max_val=TILES - 1)
                g0 = pool.value_load(tab[0:1, TILES + 1:TILES + 2], min_val=0, max_val=TILES)
                pool.wait_ge(y_st, (g0 + n_tiles + 1) * 16)
                for t in range(NT):
                    pool.wait_ge(y_used, at(y_used, t + 1))
                    pool.sem_inc(passed, 1)
                    for j in range(2):
                        nc.gpsimd.indirect_dma_start(
                            OT[:, (2 * (t % 2) + j) * D:(2 * (t % 2) + j + 1) * D], None,
                            rows, bass.IndirectOffsetOnAxis(slots[:, j, t:t + 1], 0)
                        ).then_inc(y_ld[t % 2], 16)
                    if t >= 1:
                        gain(pool, l, t - 1)
                gain(pool, l, NT - 1)

        @block.scalar
        def _(act):
            act.wait_ge(zero_ok, 1)
            act.dma_start(rows.rearrange("(n p) d -> p n d", p=P),
                          XT[:, 0:D].unsqueeze(1).to_broadcast([P, TILES, D])).then_inc(zero_st, 16)
            act.preload_act_table_set("natural_log_exp_and_others")
            act.wait_ge(lb_v, 1)
            nc.scalar.activation(WK[0:1, 3072:3072 + 2 * BW], WK[0:1, 2048:2048 + 2 * BW], ACT.Exp).then_inc(lb_a, 1)
            with act.Fori(0, LAYERS) as l:
                at = lambda s, n: l * per[s.name] + n
                act.preload_act_table_set("natural_log_exp_and_others")
                for t in range(NT + MT):
                    act.wait_ge(nat_tr, at(nat_tr, t + 3))
                    if t == 0:
                        act.wait_ge(zero_st, 16)
                    dst = XTk[:, 0:4, t * P:(t + 1) * P] if t < NT else memT[:, 0:4, (t - NT) * P:(t - NT + 1) * P]
                    nc.scalar.copy(dst, [PA, PB][t % 2][:, 0, :].rearrange("p (k q) -> p k q", k=4)).then_inc(nat_a, 1)
                act.wait_ge(bt_tr, at(bt_tr, 1))
                nc.scalar.copy(bT[:, :], PD[:, 0, 0:6 + NBR * KD])
                act.drain()
                for j in range(16):
                    act.wait_ge(pj, at(pj, j + 1))
                    src = PA[:, j % 2, :]
                    if j < 4:
                        nc.scalar.copy(MKV[:, j, :], src[:, 0:BW]).then_inc(pj_a, 1)
                    else:
                        c, half = (j - 4) // 2, j % 2
                        nc.scalar.activation(qkT[:, c, half * HALF:(half + 1) * HALF], src, ACT.Identity,
                                             bias=bT[:, c:c + 1]).then_inc(pj_a, 1)
                act.wait_ge(pj_v, at(pj_v, NT))
                nc.scalar.activation(ZF[:, 1, :], ZF[:, 0, :], ACT.Abs)
                act.drain()
                nc.scalar.activation(ZF[:, 2, :], ZF[:, 1, :], ACT.Exp, scale=-1.0)
                act.drain()
                nc.scalar.activation(ZF[:, 3, :], ZF[:, 2, :], ACT.Ln, bias=1.0).then_inc(z_a, 1)

                units = att_units()
                N = len(units)

                def softmax_exp(n):
                    t, i = units[n]
                    act.wait_ge(mx_ok, at(mx_ok, n + 1))
                    s = WK[:, (n % 2) * T:(n % 2 + 1) * T]
                    if i < H:
                        w = (t + 1) * P
                        nc.scalar.activation(s[:, 0:w], s[:, 0:w], ACT.Exp, bias=nm[:, n % 2, 4:5],
                                             accum_out=rs[:, n % 2, 0:1]).then_inc(p_ok, 1)
                    else:
                        act.wait_ge(pt_tr, at(pt_tr, n))
                        for h in range(H):
                            q = nc.scalar.activation(s[:, h * N_MEM:(h + 1) * N_MEM],
                                                     flat(PB)[:, perm(h) * N_MEM:(perm(h) + 1) * N_MEM], ACT.Exp,
                                                     bias=nm[:, n % 2, 4 + perm(h):5 + perm(h)], scale=QK_SCALE,
                                                     accum_out=rs[:, n % 2, h:h + 1])
                        q.then_inc(p_ok, 1)

                def copy_pt(n):
                    t, i = units[n]
                    w = (t + 1) * P if i < H else T
                    act.wait_ge(pt_tr, at(pt_tr, n + 2))
                    act.wait_ge(pv_mm, at(pv_mm, n + 1))
                    nc.scalar.copy(WK[:, (2 + n % 2) * T:(2 + n % 2) * T + w], flat(PC, w)).then_inc(pt_cp, 1)

                def copy_ot(c, branch, t):
                    act.wait_ge(ot_tr, at(ot_tr, c + 1))
                    nc.scalar.copy(OTk[:, 2 * branch:2 * branch + 2, t * P:(t + 1) * P],
                                   PD[:, 1, 0:BW].rearrange("p (j q) -> p j q", j=2)).then_inc(ot_cp, 1)

                for n in range(N + 2):
                    if n < N:
                        softmax_exp(n)
                    if 1 <= n <= N:
                        copy_pt(n - 1)
                    if n >= 2 and units[n - 2][1] >= H - 1:
                        t, i = units[n - 2]
                        copy_ot(2 * t + (i == H), 0 if i < H else 3, t)

                act.wait_ge(pj_v, at(pj_v, 24))
                nc.scalar.activation(RN[:, :, 3 * BW:4 * BW], RN[:, :, 3 * BW:4 * BW], ACT.Silu).then_inc(r_sil, 1)
                act.preload_act_table_set("natural_log_exp_and_others")
                for t in range(NT):
                    if t >= 1:
                        copy_ot(2 * NT + t - 1, 1, t - 1)
                    act.wait_ge(r_tr, at(r_tr, t + 1))
                    nc.scalar.copy(WK[:, 1792:2304], PB[:, 0, :]).then_inc(r_qk, 1)
                    act.wait_ge(r_var, at(r_var, t + 1))
                    nc.scalar.activation(st[:, 8:12], st[:, 4:8], ACT.Ln)
                    act.drain()
                    nc.scalar.activation(st[:, 8:12], st[:, 8:12], ACT.Exp, scale=-0.5).then_inc(r_rstd, 1)
                copy_ot(3 * NT - 1, 1, NT - 1)

                act.wait_ge(pj_v, at(pj_v, 40))
                nc.scalar.activation(HN[:, :, 0:BW], HN[:, :, 0:BW], ACT.Sigmoid, scale=-1.0).then_inc(h_sig, 1)
                nc.scalar.activation(HN[:, :, 3 * BW:4 * BW], HN[:, :, 3 * BW:4 * BW], ACT.Silu).then_inc(h_sil, 1)
                act.preload_act_table_set("natural_log_exp_and_others")
                act.wait_ge(h_kf, at(h_kf, 1))
                for t in range(NT):
                    nc.scalar.activation(WK[:, 0:BW], HN[:, t, 0:BW], ACT.Ln, bias=1.0, scale=-1.0).then_inc(h_lf, 1)
                    act.wait_ge(h_b, at(h_b, t + 1))
                    nc.scalar.activation(WK[:, 256:1024], flat(PB, 768), ACT.Exp)
                    nc.scalar.activation(WK[:, 1024:1280], PB[:, 0, 0:BW], ACT.Exp, scale=-1.0)
                    nc.scalar.activation(hdec[:, :, :], PB[:, 1, BW:BW + 4].rearrange("p (a b) -> p a b", a=2),
                                         ACT.Exp).then_inc(h_e, 1)
                    if t >= 1:
                        copy_ot(3 * NT + t - 1, 2, t - 1)
                    act.wait_ge(h_tr, at(h_tr, t + 1))
                    nc.scalar.copy(WK[:, 2304:3072], flat(PC, 768)).then_inc(h_tc, 1)
                    act.wait_ge(h_o, at(h_o, t + 1))
                    nc.scalar.activation(paired(WK[:, 3840:4096]), by_bank(PC, HD), ACT.Square).then_inc(h_sq, 1)
                    act.wait_ge(h_var, at(h_var, t + 1))
                    nc.scalar.activation(st[:, 8:12], st[:, 4:8], ACT.Ln)
                    act.drain()
                    nc.scalar.activation(st[:, 8:12], st[:, 8:12], ACT.Exp, scale=-0.5).then_inc(h_rstd, 1)
                copy_ot(4 * NT - 1, 2, NT - 1)

                with act.Fori(0, KD // 2) as dd:
                    for q in range(16):
                        b, n = q // 8, q % 4
                        act.wait_ge(g_mm, at(g_mm, q + 1) + dd * 16)
                        act.wait_ge(g_mul, at(g_mul, q + 1) + dd * 16)
                        act.sem_inc(passed, 1)
                        bank = [PA, PB][(q % 4) // 2][:, q % 2, :]
                        nc.scalar.activation(WK[:, (q % 4) * HALF:(q % 4 + 1) * HALF], bank, ACT.Sigmoid,
                                             bias=bT[:, bass.ds(dd * 2 + (6 + n * KD + b), 1)]).then_inc(g_sig, 1)

                act.preload_act_table_set("natural_log_exp_and_others")
                for t in range(NT + 1):
                    if t < NT:
                        act.wait_ge(o_var, at(o_var, t + 1))
                        nc.scalar.activation(st[:, 2:3], st[:, 1:2], ACT.Ln)
                        act.drain()
                        nc.scalar.activation(st[:, 2:3], st[:, 2:3], ACT.Exp, scale=-0.5).then_inc(o_rstd, 1)
                    if t >= 1:
                        act.wait_ge(x1_tr, at(x1_tr, t))
                        nc.scalar.copy(WK[:, 2048:3072], flat(PC)).then_inc(x1_cp, 1)
                act.wait_ge(rt_v, at(rt_v, 1))
                nc.scalar.activation(WK[:, 0:NT * E], WK[:, 0:NT * E], ACT.Exp).then_inc(rt_a, 1)

                act.wait_ge(tab_ok, at(tab_ok, 1))
                act.sem_inc(passed, 1)
                n_tiles = act.value_load(tab[0:1, TILES:TILES + 1], min_val=E, max_val=TILES - 1)
                g0 = act.value_load(tab[0:1, TILES + 1:TILES + 2], min_val=0, max_val=TILES)
                act.wait_ge(row_tr, g0 + l + 1)
                nc.scalar.copy(ROWT, flat(PC)).then_inc(row_cp, 1)
                with act.Fori(0, n_tiles) as i:
                    g = g0 + i
                    act.wait_ge(wei_used, g * KD + 2 * KD)
                    nc.scalar.activation(WK[:, 0:FE], PA[:, 0, :], ACT.Silu).then_inc(hid_sil, 1)
                    act.wait_ge(row_tr, g + l + 2)
                    nc.scalar.copy(ROWT, flat(PC)).then_inc(row_cp, 1)
                    act.wait_ge(y_ev, g + 2)
                    act.dma_start(rows[bass.ds(i * P, P), :], WK[:, 2048:3072]).then_inc(y_st, 16)
                    act.sem_inc(passed, 1)

                act.preload_act_table_set("natural_log_exp_and_others")
                for t in range(NT + 2):
                    if t >= 2:
                        act.wait_ge(f_x2, at(f_x2, t - 1))
                        r = OT[:, (4 + t % 2) * D:(5 + t % 2) * D]
                        act.dma_start(x_all[l + 1, (t - 2) * P:(t - 1) * P, :], r).then_inc(x2_st[t % 2], 16)
                        act.dma_start(out[0, (t - 2) * P:(t - 1) * P, :], r).then_inc(x2_st[t % 2], 16)
                    if t < NT:
                        act.wait_ge(f_var, at(f_var, t + 1))
                        nc.scalar.activation(st[:, 2:3], st[:, 1:2], ACT.Ln)
                        act.drain()
                        nc.scalar.activation(st[:, 2:3], st[:, 2:3], ACT.Exp, scale=-0.5).then_inc(f_rstd, 1)

        @block.vector
        def _(v):
            tt, ts, stt = nc.vector.tensor_tensor, nc.vector.tensor_scalar, nc.vector.scalar_tensor_tensor
            v.memset(XT[:, 0:D], 0.0).then_inc(zero_ok, 1)
            for s, n in ((w_used, 2), (nat_tr, 2), (pv_mm, 1), (pt_tr, 1), (pt_cp, 1), (o_ev, 1), (ot_cp, 1),
                         (wbr_used, 2), (g_mul, 4), (g_sig, 4), (o_rd, 2), (wei_used, KD), (weo_used, KF),
                         (y_ev, 1), (y_st, 16), (y_used, 2), (x2_st[0], 32), (x2_st[1], 32), (hid_ok, 1)):
                v.sem_inc(s, n)
            v.memset(tabf[:, :], 0.0)
            lb = WK[0:1, 2048:2048 + 2 * BW]
            ex = WK[0:1, 3072:3072 + 2 * BW]
            v.wait_ge(lb_ld, 16)
            tt(WK[0:1, 2560:2560 + BW], lb[:, 0:BW], lb[:, BW:2 * BW], ALU.max)
            v.drain()
            tt(lb[:, 0:BW], lb[:, 0:BW], WK[0:1, 2560:2560 + BW], ALU.subtract)
            tt(lb[:, BW:2 * BW], lb[:, BW:2 * BW], WK[0:1, 2560:2560 + BW], ALU.subtract).then_inc(lb_v, 1)
            v.wait_ge(lb_a, 1)
            tt(WK[0:1, 2560:2560 + BW], ex[:, 0:BW], ex[:, BW:2 * BW], ALU.add)
            v.drain()
            nc.vector.reciprocal(WK[0:1, 2560:2560 + BW], WK[0:1, 2560:2560 + BW])
            v.drain()
            tt(ex[:, BW:2 * BW], ex[:, BW:2 * BW], WK[0:1, 2560:2560 + BW], ALU.mult)
            v.drain()
            ts(ex[:, BW:2 * BW], ex[:, BW:2 * BW], -1.0, 1.0, ALU.mult, ALU.add)
            v.memset(ex[:, 0:BW], 1.0)
            v.drain().then_inc(lb_v, 1)
            v.wait_ge(c_ld, 64)
            v.wait_ge(lb_st, 16)

            with v.Fori(0, LAYERS) as l:
                at = lambda s, n: l * per[s.name] + n
                for t in range(NT + MT):
                    v.wait_ge(nat_tr, at(nat_tr, t + 3))
                    dst = XTk[:, 4:8, t * P:(t + 1) * P] if t < NT else memT[:, 4:8, (t - NT) * P:(t - NT + 1) * P]
                    nc.vector.tensor_copy(dst, [PA, PB][t % 2][:, 1, :].rearrange("p (k q) -> p k q", k=4)
                                          ).then_inc(nat_v, 1)
                v.memset(rstate[:, :, :], 0.0)
                v.memset(hstate[:, 0, 0, :, :], 0.0)
                v.wait_ge(par_ld, at(par_ld, 96))
                for t in range(NT):
                    v.wait_ge(pj, at(pj, 17 + t))
                    src = PA[:, t % 2, :]
                    tt(FV[:, t, :], src[:, 0:BW], BR[:, 0:BW], ALU.add)
                    tt(ZF[:, 0, t * H:(t + 1) * H], src[:, BW:BW + H], BR[:, BW:BW + H], ALU.add).then_inc(pj_v, 1)
                v.wait_ge(z_a, at(z_a, 1))
                stt(ZF[:, 0, :], ZF[:, 0, :], 0.0, ZF[:, 3, :], ALU.min, ALU.subtract).then_inc(z_v, 1)

                def evict_proj(j, dst, c0):
                    v.wait_ge(pj, at(pj, j + 1))
                    tt(dst, PA[:, j % 2, :], BR[:, c0 - C_FV:c0 - C_FV + HALF], ALU.add).then_inc(pj_v, 1)

                lf_row, c_sum = WK[0:H, 2 * T:3 * T], WK[0:H, 3 * T:4 * T]
                v.wait_ge(lf_tr, at(lf_tr, 1))
                nc.vector.tensor_copy(lf_row, flat(PC)[0:H, :])
                v.drain()
                nc.vector.tensor_tensor_scan(c_sum, co("ones")[0:H, 0:1].to_broadcast([H, T]), lf_row, 0.0,
                                             ALU.mult, ALU.add).then_inc(c_row, 1)
                evict_proj(24, RN[:, 0, 0:HALF], C_RQ)
                evict_proj(25, RN[:, 0, HALF:2 * HALF], C_RQ + HALF)
                for h in range(H):
                    v.wait_ge(cb_mm, at(cb_mm, h + 1))
                    ts(cb[:, h, :], flat(PC), -1.0 / QK_SCALE, None, ALU.mult).then_inc(cb_cp, 1)

                units = att_units()
                N = len(units)

                def softmax_max(n):
                    t, i = units[n]
                    b = n % 2
                    s = WK[:, b * T:(b + 1) * T]
                    v.wait_ge(s_mm, at(s_mm, n + 1))
                    if i < H:
                        w = (t + 1) * P
                        v.wait_ge(pt_tr, at(pt_tr, n))
                        v.sem_inc(passed, 1)
                        nc.vector.tensor_tensor_reduce(s[:, 0:w], flat(PB, w), cb[:, i, 0:w], QK_SCALE, 2 * NEG,
                                                       ALU.add, ALU.max, nm[:, b, 0:1]).then_inc(s_rd, 1)
                        v.drain()
                        ts(nm[:, b, 4:5], nm[:, b, 0:1], -1.0, None, ALU.mult).then_inc(mx_ok, 1)
                    else:
                        nc.vector.tensor_reduce(nm[:, b, 0:H], flat(PB).rearrange("p (h m) -> p h m", h=H), AX.X, ALU.max)
                        v.drain()
                        ts(nm[:, b, 4:8], nm[:, b, 0:4], -QK_SCALE, None, ALU.mult).then_inc(mx_ok, 1)

                def normalize(n):
                    t, i = units[n]
                    v.wait_ge(pv_mm, at(pv_mm, n + 2))
                    if i < H:
                        nc.vector.reciprocal(rs[:, n % 2, 0:1], rs[:, n % 2, 0:1])
                        v.drain()
                        ts(ON[:, 0, i * HD:(i + 1) * HD], PD[:, 0, 0:HD], rs[:, n % 2, 0:1], None,
                           ALU.mult).then_inc(o_ev, 1)
                    else:
                        nc.vector.reciprocal(rs[:, n % 2, :], rs[:, n % 2, :])
                        v.drain()
                        tt(heads(ON[:, 1, :]), heads(PD[:, 0, 0:BW]), over(rs[:, n % 2, :], HD), ALU.mult
                           ).then_inc(o_ev, 1)

                for n in range(N + 1):
                    if n < N:
                        if units[n][1] == 0 and units[n][0] > 0:
                            t = units[n][0]
                            evict_proj(24 + 2 * t, RN[:, t, 0:HALF], C_RQ)
                            evict_proj(25 + 2 * t, RN[:, t, HALF:2 * HALF], C_RQ + HALF)
                        softmax_max(n)
                    if n >= 1:
                        normalize(n - 1)

                v.wait_ge(r_sil, at(r_sil, 1))
                A4, B4, ROT = WK[:, 0:512], WK[:, 512:1024], WK[:, 1024:1536]
                KDC, QKT, QDT, STM = WK[:, 1536:1792], WK[:, 1792:2304], WK[:, 2304:2560], WK[:, 2560:3072]
                CEN, SQ = WK[:, 3072:3328], WK[:, 3328:3584]

                def group_norm_stats(o, done):
                    nc.vector.tensor_reduce(st[:, 0:4].rearrange("p (j a) -> p j a", j=2), o, AX.X, ALU.add)
                    v.drain()
                    ts(st[:, 0:4], st[:, 0:4], 1.0 / HD, None, ALU.mult)
                    v.drain()
                    tt(paired(CEN), o, over4(st[:, 0:4]), ALU.subtract)
                    v.drain()
                    tt(SQ, CEN, CEN, ALU.mult)
                    v.drain()
                    nc.vector.tensor_reduce(st[:, 4:8], heads(SQ), AX.X, ALU.add)
                    v.drain()
                    ts(st[:, 4:8], st[:, 4:8], 1.0 / HD, GN_EPS, ALU.mult, ALU.add).then_inc(done, 1)

                for t in range(NT):
                    X8 = RN[:, t, 0:HALF].rearrange("p (h d) -> p h d", h=8)
                    cs = co("cos")[:, t * 32:(t + 1) * 32].unsqueeze(1).to_broadcast([P, 16, 32])
                    tt(A4.rearrange("p (h d) -> p h d", h=16),
                       RN[:, t, 0:HALF].rearrange("p (h d) -> p h d", h=16), cs, ALU.mult)
                    for a in range(2):
                        sn = co("sin")[:, t * HD + 32 * a:t * HD + 32 * a + 32].unsqueeze(1).to_broadcast([P, 8, 32])
                        tt(B4.rearrange("p (h d) -> p h d", h=8)[:, :, 32 * a:32 * a + 32],
                           X8[:, :, 32 - 32 * a:64 - 32 * a], sn, ALU.mult)
                    v.drain()
                    tt(ROT, A4, B4, ALU.add)
                    v.drain()
                    tt(heads(KDC), heads(ROT[:, BW:2 * BW]), over(co("kdec"), HD), ALU.mult).then_inc(r_rot, 1)
                    evict_proj(40 + 2 * t, HN[:, t, 0:HALF], C_HF)
                    v.wait_ge(r_qk, at(r_qk, t + 1))
                    tt(QDT, QKT[:, 0:BW], co("qdec"), ALU.mult)
                    v.wait_ge(r_sc, at(r_sc, t + 1))
                    tt(paired(STM), by_bank(PC, P), paired(co("rmask")), ALU.mult).then_inc(r_mk, 1)
                    evict_proj(41 + 2 * t, HN[:, t, HALF:2 * HALF], C_HF + HALF)
                    v.wait_ge(r_o, at(r_o, t + 1))
                    tt(rstate[:, :, :], rstate[:, :, :], over(co("gtile"), HD), ALU.mult)
                    v.drain()
                    tt(rstate[:, :, :], rstate[:, :, :], PD[:, 0, 0:2 * HD].rearrange("p (j d) -> p j d", j=2), ALU.add)
                    group_norm_stats(by_bank(PB, HD), r_var)
                    v.wait_ge(r_rstd, at(r_rstd, t + 1))
                    tt(heads(CEN), heads(CEN), over(st[:, 8:12], HD), ALU.mult)
                    v.drain()
                    tt(ON[:, t % 2, :], CEN, RN[:, t, 3 * BW:4 * BW], ALU.mult).then_inc(r_on, 1)

                v.wait_ge(h_sig, at(h_sig, 1))
                tt(HN[:, :, 0:BW], HN[:, :, 0:BW], omlb[:, :].unsqueeze(1).to_broadcast([P, NT, BW]), ALU.mult
                   ).then_inc(h_kf, 1)
                v.wait_ge(h_sil, at(h_sil, 1))
                AT = WK[:, 3072:3584]
                E1, E2, E3, E1N = (WK[:, 256 + 256 * i:512 + 256 * i] for i in range(4))
                QM, Q2, KM, K3 = (WK[:, 1280 + 256 * i:1536 + 256 * i] for i in range(4))
                N1 = WK[:, 3584:3840]
                v.wait_ge(ot_tr, at(ot_tr, 3 * NT))
                v.memset(AT, 0.0)
                v.drain()
                for t in range(NT):
                    kf, val, q = (HN[:, t, i * BW:(i + 1) * BW] for i in range(3))
                    a, b = t % 2, (t + 1) % 2
                    v.wait_ge(h_e, at(h_e, t + 1))
                    tt(K3, kf, E3, ALU.mult)
                    tt(QM, q, E1, ALU.mult)
                    tt(Q2, q, E2, ALU.mult)
                    tt(KM, kf, E1N, ALU.mult).then_inc(h_pr, 1)
                    v.wait_ge(h_kv, at(h_kv, t + 1))
                    kv = PA[:, :, 0:2 * HD].rearrange("p c (j d) -> p c j d", j=2)
                    tt(hstate[:, a, 1, :, :], hstate[:, a, 0, :, :], over(hdec[:, :, 0], HD), ALU.mult)
                    v.drain()
                    tt(hstate[:, a, 1, :, :], hstate[:, a, 1, :, :], kv[:, 0, :, :], ALU.add)
                    v.drain()
                    tt(hstate[:, b, 0, :, :], hstate[:, a, 1, :, :], over(hdec[:, :, 1], HD), ALU.mult)
                    v.drain()
                    tt(hstate[:, b, 0, :, :], hstate[:, b, 0, :, :], kv[:, 1, :, :], ALU.add).then_inc(h_st, 1)
                    v.wait_ge(h_a, at(h_a, t + 1))
                    v.sem_inc(passed, 1)
                    nc.vector.copy_predicated(paired(AT),
                                              hmask[:, :].unsqueeze(1).unsqueeze(1).to_broadcast([P, 2, 2, P]),
                                              by_bank(PB, P)).then_inc(h_am, 1)
                    v.wait_ge(h_sq, at(h_sq, t + 1))
                    nc.vector.tensor_reduce(st[:, 4:8], heads(WK[:, 3840:4096]), AX.X, ALU.add)
                    v.drain()
                    ts(st[:, 4:8], st[:, 4:8], 1.0 / HD, GN_EPS, ALU.mult, ALU.add).then_inc(h_var, 1)
                    v.wait_ge(h_rstd, at(h_rstd, t + 1))
                    tt(paired(N1), by_bank(PC, HD), over4(st[:, 8:12]), ALU.mult)
                    v.drain()
                    tt(heads(N1), heads(N1), ngain[:, :].unsqueeze(1).to_broadcast([P, H, HD]), ALU.mult)
                    v.drain()
                    tt(ON[:, t % 2, :], N1, HN[:, t, 3 * BW:4 * BW], ALU.mult).then_inc(h_on, 1)

                acc, tmp = WK[:, 2048:2560], WK[:, 2560:3072]
                with v.Fori(0, KD // 2) as dd:
                    for q in range(16):
                        b, half, n = q // 8, q // 4 % 2, q % 4
                        v.wait_ge(g_sig, at(g_sig, q + 5) + dd * 16)
                        sg = WK[:, (q % 4) * HALF:(q % 4 + 1) * HALF]
                        up = [PC, PD][(q % 4) // 2][:, q % 2, :]
                        tt(acc if n == 0 else tmp, sg, up, ALU.mult).then_inc(g_mul, 1)
                        v.drain()
                        if n in (1, 2):
                            tt(acc, acc, tmp, ALU.add)
                            v.drain()
                        if n == 3:
                            tt(MIXT[:, bass.ds(dd * 2 + b, 1), half * HALF:(half + 1) * HALF],
                               acc.unsqueeze(1), tmp.unsqueeze(1), ALU.add).then_inc(mix_ok, 1)
                            v.drain()

                def norm_stats(r, done):
                    for i in range(2):
                        nc.vector.bn_stats(st[:, 8 + 6 * i:14 + 6 * i], r[:, i * HALF:(i + 1) * HALF])
                    v.drain()
                    nc.vector.bn_aggr(st[:, 0:2], st[:, 8:20])
                    v.drain()
                    ts(st[:, 1:2], st[:, 1:2], LN_EPS, None, ALU.add).then_inc(done, 1)

                for t in range(NT):
                    v.wait_ge(o_mm, at(o_mm, t + 1))
                    v.wait_ge(xr_ld[t % 2], at(xr_ld[t % 2], 16 * (t // 2 + 1)))
                    if t >= 2:
                        v.wait_ge(o_x1, at(o_x1, t - 1))
                    r = WK[:, (t % 2) * D:(t % 2 + 1) * D]
                    stt(r, xres[t % 2], ALPHA, flat([PA, PB][t % 2]), ALU.mult, ALU.add).then_inc(o_rd, 1)
                    v.drain()
                    norm_stats(r, o_var)
                    v.wait_ge(o_rstd, at(o_rstd, t + 1))
                    ts(r, r, st[:, 0:1], st[:, 2:3], ALU.subtract, ALU.mult).then_inc(o_nrm, 1)

                v.wait_ge(lg_mm, at(lg_mm, NT))
                v.wait_ge(o_x1, at(o_x1, NT))

                def te(i):
                    return WK[:, i * NT * E:(i + 1) * NT * E]

                def t3(ap, n=NT):
                    return ap.rearrange("p (t e) -> p t e", t=n)

                pr, s1, s2, both, idx, big = (te(i) for i in range(6))
                small = WK[:, 3072:4096]
                m8, mi, gm = small[:, 0:NT], small[:, 16:16 + NT], small[:, 32:32 + NT * NG]
                gs, gi = small[:, 64:64 + NT * NG], small[:, 96:96 + NT * NG]
                tt(t3(pr), t3(PD[:, 0, 0:NT * E]), brt[:, :].unsqueeze(1).to_broadcast([P, NT, E]), ALU.add)
                v.drain()
                nc.vector.tensor_reduce(m8, t3(pr), AX.X, ALU.max)
                v.drain()
                tt(t3(pr), t3(pr), over(m8, E), ALU.subtract).then_inc(rt_v, 1)
                v.wait_ge(rt_a, at(rt_a, 1))
                nc.vector.tensor_reduce(m8, t3(pr), AX.X, ALU.add)
                v.drain()
                nc.vector.reciprocal(m8, m8)
                v.drain()
                tt(t3(pr), t3(pr), over(m8, E), ALU.mult)
                v.drain()
                nc.vector.tensor_reduce(gm, t3(pr, NT * NG), AX.X, ALU.max)
                v.drain()

                def first_of_max(val, n, iota, sel, scratch):
                    nc.vector.tensor_reduce(m8, t3(val), AX.X, ALU.max)
                    v.drain()
                    tt(t3(sel), t3(val), over(m8, n), ALU.is_equal)
                    v.drain()
                    stt(t3(scratch), t3(sel), -100.0, iota.unsqueeze(1).to_broadcast([P, NT, n]), ALU.mult, ALU.add)
                    v.drain()
                    nc.vector.tensor_reduce(mi, t3(scratch), AX.X, ALU.min)
                    v.drain()
                    tt(t3(sel), t3(scratch), over(mi, n), ALU.is_equal)
                    v.drain()

                first_of_max(gm, NG, co("iota4"), gs, gi)
                tt(t3(pr, NT * NG), t3(pr, NT * NG), over(gs, EPG), ALU.mult)
                ts(gi, gs, -1.0, None, ALU.add)
                v.drain()
                tt(t3(pr, NT * NG), t3(pr, NT * NG), over(gi, EPG), ALU.add)
                v.drain()
                first_of_max(pr, E, co("iota16"), s1, idx)
                nc.vector.tensor_copy(m12[:, 0, :], m8)
                v.drain()
                stt(pr, s1, -10.0, pr, ALU.mult, ALU.add)
                v.drain()
                first_of_max(pr, E, co("iota16"), s2, idx)
                nc.vector.tensor_copy(m12[:, 1, :], m8)
                tt(both, s1, s2, ALU.add).then_inc(sel_ok, 1)
                v.drain()
                tt(m8, m12[:, 0, :], m12[:, 1, :], ALU.add)
                v.drain()
                nc.vector.reciprocal(m8, m8)
                v.drain()
                for j in range(2):
                    tt(m12[:, 2 + j, :], m12[:, j, :], m8, ALU.mult)

                v.wait_ge(rank_mm, at(rank_mm, 1))
                tot = big
                off = te(6)
                nc.vector.tensor_copy(tot, PD[:, 1, NT * E:2 * NT * E])
                v.memset(off[:, 0:E], 0.0)
                v.drain()
                for t in range(1, NT):
                    tt(off[:, t * E:(t + 1) * E], off[:, (t - 1) * E:t * E], tot[:, (t - 1) * E:t * E], ALU.add)
                    v.drain()
                cnt, ntl, cum, base = (small[:, 128 + 16 * i:144 + 16 * i] for i in range(4))
                tt(cnt, off[:, (NT - 1) * E:NT * E], tot[:, (NT - 1) * E:NT * E], ALU.add)
                v.drain()
                tt(t3(idx, E), over(cnt, 8), co("thr").unsqueeze(1).to_broadcast([P, E, 8]), ALU.is_gt)
                v.drain()
                nc.vector.tensor_reduce(ntl, t3(idx, E), AX.X, ALU.add)
                v.drain()
                nc.vector.tensor_tensor_scan(cum, co("ones")[:, 0:E], ntl, 0.0, ALU.mult, ALU.add)
                v.drain()
                tt(base, cum, ntl, ALU.subtract)
                v.drain()
                ts(base, base, float(P), None, ALU.mult)
                v.drain()
                tt(t3(off), t3(off), base.unsqueeze(1).to_broadcast([P, NT, E]), ALU.add)
                v.drain()
                tt(off, off, PD[:, 1, 0:NT * E], ALU.add)
                v.drain()
                for j, s in enumerate((s1, s2)):
                    tt(s, s, off, ALU.mult)
                    v.drain()
                    nc.vector.tensor_reduce(gm[:, j * NT:(j + 1) * NT], t3(s), AX.X, ALU.add)
                    v.drain()
                    nc.vector.tensor_copy(slots[:, j, :], gm[:, j * NT:(j + 1) * NT])
                exq = small[:, 256:256 + TILES * E]
                tt(tabf[:, TILES + 1:TILES + 2], tabf[:, TILES + 1:TILES + 2], tabf[:, TILES:TILES + 1], ALU.add)
                tt(t3(exq, TILES), cum.unsqueeze(1).to_broadcast([P, TILES, E]), over(co("iota32"), E), ALU.is_le)
                v.drain()
                nc.vector.tensor_reduce(tabf[:, 0:TILES], t3(exq, TILES), AX.X, ALU.add)
                nc.vector.tensor_copy(tabf[:, TILES:TILES + 1], cum[:, E - 1:E])
                v.drain()
                ts(tabf[:, 0:TILES], tabf[:, 0:TILES], float(E - 1), None, ALU.min)
                v.drain()
                nc.vector.tensor_copy(tab[:, :], tabf[0:1, :])
                v.drain().then_inc(tab_ok, 1)

                n_tiles = v.value_load(tab[0:1, TILES:TILES + 1], min_val=E, max_val=TILES - 1)
                g0 = v.value_load(tab[0:1, TILES + 1:TILES + 2], min_val=0, max_val=TILES)
                with v.Fori(0, n_tiles) as i:
                    g = g0 + i
                    v.wait_ge(hid_sil, g + 1)
                    tt(WK[:, 512:1024], WK[:, 0:512], PA[:, 1, :], ALU.mult).then_inc(hid_ok, 1)
                    v.wait_ge(hid_tr, g + 1)
                    nc.vector.tensor_copy(WK[:, 1024:1536], PD[:, 0, :]).then_inc(hid_cp, 1)
                    v.wait_ge(weo_used, g * KF + 2 * KF)
                    v.wait_ge(y_st, (g + 1) * 16)
                    nc.vector.tensor_copy(WK[:, 2048:3072], flat(PB)).then_inc(y_ev, 1)

                for t in range(NT):
                    v.wait_ge(y_ld[t % 2], at(y_ld[t % 2], 32 * (t // 2 + 1)))
                    v.wait_ge(x2_st[t % 2], at(x2_st[t % 2], 32 * (t // 2 + 1)))
                    r = OT[:, (4 + t % 2) * D:(5 + t % 2) * D]
                    y1, y2 = (OT[:, (2 * (t % 2) + j) * D:(2 * (t % 2) + j + 1) * D] for j in range(2))
                    ts(r, X1[:, t, :], ALPHA, None, ALU.mult)
                    v.drain()
                    stt(r, y1, m12[:, 2, t:t + 1], r, ALU.mult, ALU.add)
                    v.drain()
                    stt(r, y2, m12[:, 3, t:t + 1], r, ALU.mult, ALU.add).then_inc(y_used, 1)
                    v.drain()
                    norm_stats(r, f_var)
                    v.wait_ge(f_rstd, at(f_rstd, t + 1))
                    ts(r, r, st[:, 0:1], st[:, 2:3], ALU.subtract, ALU.mult).then_inc(f_nrm, 1)

        @block.tensor
        def _(pe):
            mm = nc.tensor.matmul
            pe.wait_ge(c_ld, 64)
            with pe.Fori(0, LAYERS) as l:
                at = lambda s, n: l * per[s.name] + n

                def transposes(dst, src, n):
                    for k in range(n):
                        q = nc.tensor.transpose(flat(dst)[:, k * P:(k + 1) * P], src[:, k * P:(k + 1) * P], ident)
                    return q

                for t in range(NT + MT):
                    pe.wait_ge(nat_ld[t % 2], at(nat_ld[t % 2], 16 * (t // 2 + 1)))
                    if t >= 2:
                        pe.wait_ge(nat_a, at(nat_a, t - 1))
                        pe.wait_ge(nat_v, at(nat_v, t - 1))
                    transposes([PA, PB][t % 2], WK[:, (t % 2) * D:(t % 2 + 1) * D], 8).then_inc(nat_tr, 1)
                pe.wait_ge(nat_a, at(nat_a, NT + MT))
                pe.wait_ge(nat_v, at(nat_v, NT + MT))

                pe.wait_ge(par_ld, at(par_ld, 96))
                pe.sem_inc(passed, 1)
                nc.tensor.transpose(PD[:, 0, 0:6 + NBR * KD], b_rows, ident[0:6 + NBR * KD, 0:6 + NBR * KD]
                                    ).then_inc(bt_tr, 1)

                def unit_loaded(u):
                    pe.wait_ge(w_ld[u % 2], at(w_ld[u % 2], 64 * (u // 2 + 1)))

                def bank_free(j):
                    if 2 <= j < 18:
                        pe.wait_ge(pj_a, at(pj_a, j - 1))
                    elif j >= 18:
                        pe.wait_ge(pj_v, at(pj_v, j - 17))

                def project(j, n, lhs, rhs):
                    bank_free(j)
                    for k in range(KD):
                        q = mm(PA[:, j % 2, 0:n], lhs(k), rhs(k), start=k == 0, stop=k == KD - 1)
                    q.then_inc(pj, 1)
                    return q

                unit_loaded(0)
                for j in range(2):
                    project(j, BW, lambda k: W[0][:, k, j * P:(j + 1) * P], lambda k: memT[:, k, :])
                for j in range(2):
                    project(2 + j, BW, lambda k: memT[:, k, j * P:(j + 1) * P], lambda k: W[0][:, k, BW:2 * BW])
                pe.drain().then_inc(w_used, 1)
                for u, c0, n in ((1, 0, 4), (2, 4, 2)):
                    unit_loaded(u)
                    for c in range(n):
                        for half in range(2):
                            project(4 + (c0 + c) * 2 + half, HALF,
                                    lambda k: W[u % 2][:, k, c * P:(c + 1) * P],
                                    lambda k: XTk[:, k, half * HALF:(half + 1) * HALF])
                    pe.drain().then_inc(w_used, 1)
                unit_loaded(3)
                for t in range(NT):
                    project(16 + t, BW + H, lambda k: XTk[:, k, t * P:(t + 1) * P], lambda k: W[1][:, k, 0:BW + H])
                pe.drain().then_inc(w_used, 1)

                def project_pair(first, t, which, j):
                    u = first + which
                    if t == 0:
                        unit_loaded(u)
                    project(j, HALF, lambda k: XTk[:, k, t * P:(t + 1) * P], lambda k: W[u % 2][:, k, :])
                    if t == NT - 1:
                        pe.drain().then_inc(w_used, 1)

                pe.wait_ge(z_v, at(z_v, 1))
                for t in range(NT):
                    q = nc.tensor.transpose(flat(PC)[0:H, t * P:(t + 1) * P], ZF[:, 0, t * H:(t + 1) * H], ident)
                q.then_inc(lf_tr, 1)
                project_pair(4, 0, 0, 24)
                project_pair(4, 0, 1, 25)
                pe.wait_ge(c_row, at(c_row, 1))
                for h in range(H):
                    if h >= 1:
                        pe.wait_ge(cb_cp, at(cb_cp, h))
                    for half in range(2):
                        q = mm(PC[:, half, :], ident[0:H, h:h + 1].to_broadcast([H, P]),
                               WK[0:H, 3 * T + half * HALF:3 * T + (half + 1) * HALF], start=True, stop=True)
                    q.then_inc(cb_mm, 1)
                pe.wait_ge(cb_cp, at(cb_cp, H))

                units = att_units()
                N = len(units)

                def head(c, h):
                    return slice((h % 2) * HD, (h % 2 + 1) * HD), c + h // 2

                def scores(n):
                    t, i = units[n]
                    if n >= 1 and i == 0:
                        pe.wait_ge(p_ok, at(p_ok, n))
                    elif i >= 1:
                        pe.wait_ge(s_rd, at(s_rd, t * H + i))
                    if i < H:
                        rows, cq = head(0, i)
                        ck = cq + 2
                        w = (t + 1) * P
                        for c0 in range(0, w - P, HALF):
                            c1 = min(w - P, c0 + HALF)
                            mm(flat(PB)[:, c0:c1], qkT[rows, cq, t * P:(t + 1) * P], qkT[rows, ck, c0:c1],
                               start=True, stop=True)
                        mm(flat(PB)[:, w - P:w], qkT[rows, cq, t * P:(t + 1) * P], qkT[rows, ck, w - P:w],
                           start=True, stop=False)
                        q = mm(flat(PB)[:, w - P:w], ident, co("causal"), start=False, stop=True)
                    else:
                        for h in range(H):
                            rows, cq = head(4, h)
                            q = mm(flat(PB)[:, perm(h) * N_MEM:(perm(h) + 1) * N_MEM], qkT[rows, cq, t * P:(t + 1) * P],
                                   MKV[rows, h // 2, :], start=True, stop=True)
                    q.then_inc(s_mm, 1)

                def transpose_p(n):
                    t, i = units[n]
                    pe.wait_ge(p_ok, at(p_ok, n + 1))
                    pe.wait_ge(pt_cp, at(pt_cp, n + 1))
                    transposes(PC, WK[:, (n % 2) * T:(n % 2 + 1) * T], t + 1 if i < H else 8).then_inc(pt_tr, 1)

                def times_v(n):
                    t, i = units[n]
                    pt = WK[:, (2 + n % 2) * T:(3 + n % 2) * T]
                    pe.wait_ge(pt_cp, at(pt_cp, n + 2))
                    pe.wait_ge(o_ev, at(o_ev, n + 1))
                    if i < H:
                        for kt in range(t + 1):
                            q = mm(PD[:, 0, 0:HD], pt[:, kt * P:(kt + 1) * P], FV[:, kt, i * HD:(i + 1) * HD],
                                   start=kt == 0, stop=kt == t)
                    else:
                        for h in range(H):
                            for kt in range(MT):
                                q = mm(PD[:, 0, h * HD:(h + 1) * HD], pt[:, (2 * h + kt) * P:(2 * h + kt + 1) * P],
                                       MKV[:, 2 + kt, h * HD:(h + 1) * HD], start=kt == 0, stop=kt == MT - 1)
                    q.then_inc(pv_mm, 1)

                def transpose_o(c, src):
                    pe.wait_ge(ot_cp, at(ot_cp, c + 1))
                    for j in range(2):
                        q = nc.tensor.transpose(PD[:, 1, j * P:(j + 1) * P], src[:, j * P:(j + 1) * P], ident)
                    q.then_inc(ot_tr, 1)

                for n in range(N + 2):
                    if n < N:
                        t, i = units[n]
                        if i == 0 and t > 0:
                            project_pair(4, t, 0, 24 + 2 * t)
                            project_pair(4, t, 1, 25 + 2 * t)
                        scores(n)
                    if 1 <= n <= N:
                        transpose_p(n - 1)
                        times_v(n - 1)
                    if n >= 2 and units[n - 2][1] >= H - 1:
                        t, i = units[n - 2]
                        pe.wait_ge(o_ev, at(o_ev, n))
                        transpose_o(2 * t + (i == H), ON[:, i - H + 1, :])

                ROT, KDC, QKT = WK[:, 1024:1536], WK[:, 1536:1792], WK[:, 1792:2304]
                QDT, STM = WK[:, 2304:2560], WK[:, 2560:3072]
                for t in range(NT):
                    pe.wait_ge(r_rot, at(r_rot, t + 1))
                    for c in range(4):
                        q = nc.tensor.transpose(PB[:, 0, c * P:(c + 1) * P], ROT[:, c * P:(c + 1) * P], ident)
                    q.then_inc(r_tr, 1)
                    if t >= 1:
                        pe.wait_ge(r_on, at(r_on, t))
                        transpose_o(2 * NT + t - 1, ON[:, (t - 1) % 2, :])
                    project_pair(6, t, 0, 40 + 2 * t)
                    pe.wait_ge(r_qk, at(r_qk, t + 1))
                    for h in range(H):
                        rows, c = head(0, h)
                        q = mm(PC[:, h % 2, c * P:(c + 1) * P], QKT[rows, (2 + c) * P:(3 + c) * P],
                               QKT[rows, c * P:(c + 1) * P], start=True, stop=True)
                    q.then_inc(r_sc, 1)
                    project_pair(6, t, 1, 41 + 2 * t)
                    pe.wait_ge(r_mk, at(r_mk, t + 1))
                    for h in range(H):
                        rows, c = head(0, h)
                        val = RN[:, t, 2 * BW + h * HD:2 * BW + (h + 1) * HD]
                        mm(PB[:, h % 2, c * HD:(c + 1) * HD], STM[:, h * P:(h + 1) * P], val, start=True, stop=False)
                        mm(PB[:, h % 2, c * HD:(c + 1) * HD], QDT[rows, c * P:(c + 1) * P], rstate[rows, c, :],
                           start=False, stop=True)
                    for h in range(H):
                        rows, c = head(0, h)
                        val = RN[:, t, 2 * BW + h * HD:2 * BW + (h + 1) * HD]
                        q = mm(PD[rows, 0, c * HD:(c + 1) * HD], KDC[:, h * HD:(h + 1) * HD], val,
                               start=True, stop=True)
                    q.then_inc(r_o, 1)
                pe.wait_ge(r_on, at(r_on, NT))
                transpose_o(3 * NT - 1, ON[:, (NT - 1) % 2, :])

                AT = WK[:, 3072:3584]
                QM, Q2, KM, K3 = (WK[:, 1280 + 256 * i:1536 + 256 * i] for i in range(4))
                TQM, TQ2, TKM = (WK[:, 2304 + 256 * i:2560 + 256 * i] for i in range(3))
                for t in range(NT):
                    val = HN[:, t, BW:2 * BW]
                    pe.wait_ge(h_lf, at(h_lf, t + 1))
                    for i, name in enumerate(("c_mid", "c_cum", "c_rest")):
                        mm(flat(PB)[:, i * BW:(i + 1) * BW], co(name), WK[:, 0:BW], start=True, stop=True)
                    for j in range(2):
                        q = mm(PB[:, 1, BW + 2 * j:BW + 2 * j + 2], WK[:, j * P:(j + 1) * P], co("c_end"),
                               start=True, stop=True)
                    q.then_inc(h_b, 1)
                    if t >= 1:
                        pe.wait_ge(h_on, at(h_on, t))
                        transpose_o(3 * NT + t - 1, ON[:, (t - 1) % 2, :])
                    pe.wait_ge(h_pr, at(h_pr, t + 1))
                    for i, src in enumerate((QM, Q2, KM)):
                        for j in range(2):
                            q = nc.tensor.transpose(flat(PC)[:, (2 * i + j) * P:(2 * i + j + 1) * P],
                                                    src[:, j * P:(j + 1) * P], ident)
                    q.then_inc(h_tr, 1)
                    for c in range(2):
                        rc = slice(c * CH, (c + 1) * CH)
                        for h in range(H):
                            rows, p = head(0, h)
                            q = mm(PA[rows, c, p * HD:(p + 1) * HD], K3[rc, h * HD:(h + 1) * HD],
                                   val[rc, h * HD:(h + 1) * HD], start=True, stop=True)
                    q.then_inc(h_kv, 1)
                    pe.wait_ge(h_tc, at(h_tc, t + 1))
                    for h in range(H):
                        rows, p = head(0, h)
                        q = mm(PB[:, h % 2, p * P:(p + 1) * P], TKM[rows, p * P:(p + 1) * P],
                               TQM[rows, p * P:(p + 1) * P], start=True, stop=True)
                    q.then_inc(h_a, 1)
                    pe.wait_ge(h_st, at(h_st, t + 1))
                    pe.wait_ge(h_am, at(h_am, t + 1))
                    for h in range(H):
                        rows, p = head(0, h)
                        o = PC[:, h % 2, p * HD:(p + 1) * HD]
                        mm(o, AT[:, h * P:(h + 1) * P], val[:, h * HD:(h + 1) * HD], start=True, stop=False,
                           skip_group_check=True)
                        for c in range(2):
                            q = mm(PC[c * CH:(c + 1) * CH, h % 2, p * HD:(p + 1) * HD],
                                   TQ2[rows, p * P + c * CH:p * P + (c + 1) * CH], hstate[rows, t % 2, c, p, :],
                                   start=False, stop=c == 1, skip_group_check=True)
                    q.then_inc(h_o, 1)
                pe.wait_ge(h_on, at(h_on, NT))
                transpose_o(4 * NT - 1, ON[:, (NT - 1) % 2, :])

                pe.wait_ge(ot_cp, at(ot_cp, 4 * NT + 1))
                pe.sem_inc(passed, 1)
                with pe.Fori(0, KD // 2) as dd:
                    for b in range(2):
                        pe.wait_ge(w_ld[b], at(w_ld[b], 64 * (GATE_U // 2 + 1)) + dd * 64)
                        pe.wait_ge(wbr_ld[b], at(wbr_ld[b], 16) + dd * 16)
                        for q in range(8 * b, 8 * b + 8):
                            half, n = q // 4 % 2, q % 4
                            tok = slice(half * HALF, (half + 1) * HALF)
                            pe.wait_ge(g_sig, at(g_sig, q + 1) + dd * 16)
                            pe.wait_ge(g_mul, at(g_mul, q + 1) + dd * 16)
                            for k in range(KD):
                                z = mm([PA, PB][(q % 4) // 2][:, q % 2, :], W[b][:, k, n * P:(n + 1) * P],
                                       XTk[:, k, tok], start=k == 0, stop=k == KD - 1)
                            for j in range(2):
                                z = mm([PC, PD][(q % 4) // 2][:, q % 2, :], WBR[b][:, 2 * n + j, :],
                                       OTk[:, 2 * n + j, tok], start=j == 0, stop=j == 1)
                            z.then_inc(g_mm, 1)
                        pe.drain().then_inc(w_used, 1)
                        pe.sem_inc(wbr_used, 1)

                pe.wait_ge(mix_ok, at(mix_ok, 16))
                pe.wait_ge(g_sig, at(g_sig, 64 + 4))
                unit_loaded(OUT_U)
                unit_loaded(OUT_U + 1)
                X1T = WK[:, 2048:3072]
                for t in range(NT + 1):
                    if t < NT:
                        if t >= 2:
                            pe.wait_ge(o_rd, at(o_rd, t + 1))
                        for half in range(2):
                            for k in range(KD):
                                q = mm([PA, PB][t % 2][:, half, :], MIXT[:, k, t * P:(t + 1) * P], W[half][:, k, :],
                                       start=k == 0, stop=k == KD - 1)
                        q.then_inc(o_mm, 1)
                        if t == NT - 1:
                            pe.drain().then_inc(w_used, 2)
                    if t >= 1:
                        pe.wait_ge(o_x1, at(o_x1, t))
                        transposes(PC, X1[:, t - 1, :], 8).then_inc(x1_tr, 1)
                        pe.wait_ge(x1_cp, at(x1_cp, t))
                        for k in range(KD):
                            q = mm(PD[:, 0, (t - 1) * E:t * E], X1T[:, k * P:(k + 1) * P], wr[:, k, :],
                                   start=k == 0, stop=k == KD - 1)
                        q.then_inc(lg_mm, 1)
                pe.wait_ge(sel_ok, at(sel_ok, 1))
                both = WK[:, 3 * NT * E:4 * NT * E]
                mm(PD[:, 1, 0:NT * E], co("before"), both, start=True, stop=True)
                mm(PD[:, 1, NT * E:2 * NT * E], co("ones"), both, start=True, stop=True).then_inc(rank_mm, 1)

                pe.wait_ge(tab_ok, at(tab_ok, 1))
                pe.sem_inc(passed, 1)
                n_tiles = pe.value_load(tab[0:1, TILES:TILES + 1], min_val=E, max_val=TILES - 1)
                g0 = pe.value_load(tab[0:1, TILES + 1:TILES + 2], min_val=0, max_val=TILES)
                pe.wait_ge(row_ld, (g0 + l) * 16 + 16)
                transposes(PC, ROW, 8).then_inc(row_tr, 1)
                with pe.Fori(0, n_tiles) as i:
                    g = g0 + i
                    pe.wait_ge(row_cp, g + l + 1)
                    pe.wait_ge(hid_ok, g + 1)
                    for k in range(KD):
                        pe.wait_ge(wei_ld[k], (g + 1) * 16)
                        for half in range(2):
                            q = mm(PA[:, half, :], ROWT[:, k * P:(k + 1) * P], WEI[:, k, half * HALF:(half + 1) * HALF],
                                   start=k == 0, stop=k == KD - 1)
                        q.then_inc(wei_used, 1)
                    pe.wait_ge(row_ld, (g + l) * 16 + 32)
                    transposes(PC, ROW, 8).then_inc(row_tr, 1)
                    pe.wait_ge(hid_ok, g + 2)
                    for k in range(KF):
                        q = nc.tensor.transpose(PD[:, 0, k * P:(k + 1) * P], WK[:, 512 + k * P:512 + (k + 1) * P], ident)
                    q.then_inc(hid_tr, 1)
                    pe.wait_ge(hid_cp, g + 1)
                    pe.wait_ge(y_ev, g + 1)
                    for k in range(KF):
                        pe.wait_ge(weo_ld[k], (g + 1) * 16)
                        for half in range(2):
                            q = mm(PB[:, half, :], WK[:, 1024 + k * P:1024 + (k + 1) * P],
                                   WEO[:, k, half * HALF:(half + 1) * HALF], start=k == 0, stop=k == KF - 1)
                        q.then_inc(weo_used, 1)


def constants():
    import numpy as np
    c = np.zeros((P, N_CONST), np.float32)

    def put(name, value):
        a, b = CONST[name]
        c[:, a:b] = np.asarray(value, np.float64).reshape(P, b - a)

    i = np.arange(P)
    gamma = np.log1p(-np.exp2(-5.0 - np.arange(H)))
    put("ident", np.eye(P))
    put("causal", np.where(i[:, None] >= i[None, :], 0.0, NEG / QK_SCALE))
    j_, i_ = i[:, None], i[None, :]
    seen = (i_ // CH) >= (j_ // CH)
    put("rmask", np.stack([np.where(seen, np.exp(g * np.abs(i_ - j_)), 0.0) * QK_SCALE for g in gamma], 1))
    put("qdec", np.stack([np.stack([np.exp(gamma[2 * j + p // HD] * (i + 1)) for p in range(P)]) for j in range(2)], 1))
    put("kdec", np.exp(gamma[None, :] * (P - 1 - i[:, None])) * QK_SCALE)
    put("gtile", np.stack([[np.exp(gamma[2 * j + p // HD] * P) for j in range(2)] for p in range(P)]))
    inv = (10000.0 ** (-2.0 * np.arange(HD // 2, dtype=np.float32) / HD)).astype(np.float32)
    pos = np.arange(T, dtype=np.float32)
    ang = (pos[:, None] * inv[None, :]).astype(np.float32).astype(np.float64).reshape(NT, P, HD // 2).transpose(1, 0, 2)
    put("cos", np.cos(ang))
    put("sin", np.concatenate([-np.sin(ang), np.sin(ang)], 2))
    same = (i_ // CH) == (j_ // CH)
    cum = same & (j_ <= i_)
    put("c_cum", cum)
    put("c_mid", cum * 1.0 - (same & (j_ % CH < CH // 2)))
    put("c_rest", same & (j_ > i_))
    put("c_end", np.stack([i < CH, i >= CH], 1))
    put("before", j_ < i_)
    put("ones", np.ones((P, P)))
    put("iota4", np.tile(np.arange(4), (P, 1)))
    put("iota16", np.tile(np.arange(16), (P, 1)))
    put("iota32", np.tile(np.arange(32), (P, 1)))
    put("thr", np.tile(np.arange(8) * P, (P, 1)))
    return c, (same & (j_ <= i_)).astype(np.int32)


_INS = ['x', 'mem', 'w_in', 'b_in', 'w_mem_kv', 'hgrn_lb', 'hgrn_norm_g', 'w_branch', 'w_out', 'ln_g', 'ln_b',
        'w_router', 'b_router', 'w_e_in', 'w_e_out']


def kernel(**inputs):
    import numpy as _np
    import concourse.bacc as _bacc
    from concourse import mybir as _mybir
    from concourse.bass_utils import run_bass_kernel_spmd as _run

    nc = _bacc.Bacc("TRN2", target_bir_lowering=False, num_devices=1)
    arrays, args = {}, []
    tables, mask = constants()
    for name, a in [(n, _np.ascontiguousarray(inputs[n])) for n in _INS] + [("tables", tables), ("chunk_mask", mask)]:
        arrays[f"in_{name}_dram"] = a
        args.append(nc.dram_tensor(f"in_{name}_dram", a.shape, _mybir.dt.from_np(a.dtype), kind="ExternalInput").ap())
    args.append(nc.dram_tensor("out_0_dram", (1, T, D), F32, kind="ExternalOutput").ap())
    trunk(nc, *args)
    r = _run(nc, [arrays], core_ids=[0])
    return r.results[0]["out_0_dram"]
```

```python
from contextlib import ExitStack

import concourse.bass as bass
from concourse import mybir

F32 = mybir.dt.float32
I32 = mybir.dt.int32
U32 = mybir.dt.uint32
ALU = mybir.AluOpType
ACT = mybir.ActivationFunctionType
AX = mybir.AxisListType

P = 128
LAYERS = 2
T = 1024
D = 1024
NT = T // P
KD = D // P
H = 4
HD = 64
BW = H * HD
NBR = 4
N_MEM = 256
MT = N_MEM // P
CH = 64
E = 16
NG = 4
EPG = E // NG
FE = 512
KF = FE // P
HALF = 512
ALPHA = (2.0 * LAYERS) ** 0.25
LN_EPS = 1e-5
GN_EPS = 1e-6
QK_SCALE = HD ** -0.5
NEG = -1e30

C_FQ, C_FK, C_FV, C_FF = 0, BW, 2 * BW, 3 * BW
C_RQ = 3 * BW + H
C_HF = C_RQ + 4 * BW
C_MQ = C_HF + 4 * BW
C_GATE = C_MQ + BW
N_IN = C_GATE + NBR * D
N_NAT = C_MQ - C_FV

TILES = 2 * T // P + E
UNITS = 18
GATE_U, OUT_U = 8, 16
ATT = H + 1

CONST = {}
_at = 0
for _name, _width in (("ident", 128), ("causal", 128), ("rmask", 512), ("qdec", 256), ("kdec", 4), ("gtile", 2),
                      ("cos", 256), ("sin", 512), ("c_mid", 128), ("c_cum", 128), ("c_rest", 128), ("c_end", 2),
                      ("before", 128), ("ones", 128), ("iota4", 4), ("iota16", 16), ("iota32", 32), ("thr", 8)):
    CONST[_name] = (_at, _at + _width)
    _at += _width
N_CONST = _at


def trunk(nc, x, mem, w_in, b_in, w_mem_kv, hgrn_lb, hgrn_norm_g, w_branch, w_out, ln_g, ln_b,
          w_router, b_router, w_e_in, w_e_out, consts, chunk_mask, out):
    with ExitStack() as ctx:
        def sb(name, shape, dt=F32):
            return ctx.enter_context(nc.sbuf_tensor(name, shape, dt))

        def pb(name):
            return ctx.enter_context(nc.psum_tensor(name, [P, 2, HALF], F32))

        per = {}

        def sem(name, per_layer=0):
            s = ctx.enter_context(nc.semaphore(name))
            per[name] = per_layer
            return s

        def dram(name, shape):
            return nc.dram_tensor(name, shape, F32, kind="Internal").ap()

        mem_t = dram("mem_t", [P, KD * N_MEM])
        rows = dram("rows", [TILES * P, D])
        keep_rate = dram("keep_rate", [LAYERS, BW])

        XT = sb("XT", [P, KD * T])
        OT = sb("OT", [P, 8 * T])
        RA = sb("RA", [P, 8 * T])
        RC = sb("RC", [P, 8 * T])
        W = [sb(f"W{i}", [P, 8, HALF]) for i in range(2)]
        WK = sb("WK", [P, 4096])
        BR = sb("BR", [P, N_NAT])
        MKV = sb("MKV", [P, 4, BW])
        CO = sb("CO", [P, N_CONST])
        hmask = sb("hmask", [P, P], I32)
        bT = sb("bT", [P, 6 + NBR * KD])
        omlb = sb("omlb", [P, BW])
        ngain = sb("ngain", [P, HD])
        wr = sb("wr", [P, KD, E])
        brt = sb("brt", [P, E])
        ON = sb("ON", [P, 2, BW])
        ZF = sb("ZF", [P, 4, NT * H])
        nm = sb("nm", [P, 2, 8])
        rs = sb("rs", [P, 4, 4])
        rstate = sb("rstate", [P, 2, HD])
        hstate = sb("hstate", [P, 2, 2, 2, HD])
        hdec = sb("hdec", [P, 2, 2, 2])
        st = sb("st", [P, 32])
        m12 = sb("m12", [P, 4, NT])
        slots = sb("slots", [P, 2, NT], U32)
        tab = sb("tab", [1, TILES + 2], U32)
        tabf = sb("tabf", [P, TILES + 2])

        PA, PB, PC, PD = pb("PA"), pb("PB"), pb("PC"), pb("PD")

        def co(name):
            a, b = CONST[name]
            return CO[:, a:b]

        ident = co("ident")
        XTk = XT[:, :].rearrange("p (k t) -> p k t", k=KD)
        OTk = OT[:, :].rearrange("p (c t) -> p c t", c=8)
        memT = RA[:, 0:KD * N_MEM].rearrange("p (k m) -> p k m", k=KD)
        qkT = RC[:, 0:6 * T].rearrange("p (c t) -> p c t", c=6)
        FV = RC[:, 6 * T:8 * T].rearrange("p (t c) -> p t c", t=NT)
        RN = RA[:, :].rearrange("p (t c) -> p t c", t=NT)
        HN = RC[:, :].rearrange("p (t c) -> p t c", t=NT)
        MIXT = RA[:, :].rearrange("p (k t) -> p k t", k=KD)
        X1 = RC[:, :].rearrange("p (t c) -> p t c", t=NT)
        cb = OT[:, 2 * T:6 * T].rearrange("p (h t) -> p h t", h=H)
        WBR = [BR[:, i * T:(i + 1) * T].rearrange("p (c m) -> p c m", c=8) for i in range(2)]
        lnp = [XT[:, 0:D], XT[:, D:2 * D], RA[:, 5 * D:6 * D], RA[:, 7 * D:8 * D]]
        zeros = RA[:, 7 * D:8 * D]
        x2 = [OT[:, (4 + i) * D:(5 + i) * D] for i in range(4)]
        xres = [XT[:, (4 + i) * D:(5 + i) * D] for i in range(2)]
        WEI = OTk
        WEO = RA[:, 0:4 * T].rearrange("p (k n) -> p k n", k=KF)
        ROW = RA[:, 4 * T:5 * T]
        ROWT = RA[:, 6 * T:7 * T]

        b_rows = WK[0:6 + NBR * KD, 2 * T:2 * T + P]

        def flat(psum, n=2 * HALF):
            return psum[:, :, :].rearrange("p a b -> p (a b)")[:, 0:n]

        def heads(ap, n=H):
            return ap.rearrange("p (h d) -> p h d", h=n)

        def by_bank(psum, n, c0=0):
            return psum[:, :, c0:c0 + 2 * n].rearrange("p a (j d) -> p j a d", j=2)

        def over4(ap):
            return ap.rearrange("p (j a) -> p j a", j=2).unsqueeze(3).to_broadcast([P, 2, 2, HD])

        def paired(ap):
            return ap.rearrange("p (j a d) -> p j a d", j=2, a=2)

        def perm(h):
            return (h % 2) * 2 + h // 2

        def over(ap, n):
            return ap.unsqueeze(2).to_broadcast([ap.shape[0], ap.shape[1], n])

        c_ld = sem("c_ld")
        x0_ld = sem("x0_ld")
        zero_ok = sem("zero_ok")
        zero_st = sem("zero_st")
        lb_ld = sem("lb_ld")
        lb_v = sem("lb_v")
        lb_a = sem("lb_a")
        lb_st = sem("lb_st")
        par_ld = sem("par_ld", 6 * 16)
        nat_ld = [sem(f"nat_ld{i}") for i in range(NT + MT)]
        bt_tr = sem("bt_tr", 1)
        nat_tr = sem("nat_tr")
        nat_a = sem("nat_a")
        nat_v = sem("nat_v")
        mt_st = sem("mt_st")
        mt_ld = sem("mt_ld", 16)
        ln2_ld = sem("ln2_ld", 2 * 16)
        x1a_ok = sem("x1a_ok", 1)
        x2_tr = sem("x2_tr", NT)
        x2_cp = sem("x2_cp", NT)
        w_ld = [sem(f"w_ld{i}", UNITS // 2 * 64) for i in range(2)]
        w_used = sem("w_used", UNITS)
        pj = sem("pj", 56)
        pj_a = sem("pj_a", 16)
        pj_v = sem("pj_v", 40)
        z_v = sem("z_v", 1)
        z_a = sem("z_a", 1)
        lf_tr = sem("lf_tr", 1)
        c_row = sem("c_row", 1)
        cb_mm = sem("cb_mm", H)
        cb_cp = sem("cb_cp", H)
        s_mm = sem("s_mm", NT * ATT)
        s_rd = sem("s_rd", NT * H)
        mx_ok = sem("mx_ok", NT * ATT)
        p_ok = sem("p_ok", NT * ATT)
        pt_tr = sem("pt_tr", NT * ATT)
        pt_cp = sem("pt_cp", NT * ATT)
        pv_mm = sem("pv_mm", NT * ATT)
        o_ev = sem("o_ev", NT * ATT)
        ot_tr = sem("ot_tr", 4 * NT)
        ot_cp = sem("ot_cp", 4 * NT)
        r_sil = sem("r_sil", 1)
        r_rot = sem("r_rot", NT)
        r_tr = sem("r_tr", NT)
        r_qk = sem("r_qk", NT)
        r_sc = sem("r_sc", NT)
        r_mk = sem("r_mk", NT)
        r_o = sem("r_o", NT)
        r_var = sem("r_var", NT)
        r_rstd = sem("r_rstd", NT)
        r_on = sem("r_on", NT)
        h_sig = sem("h_sig", 1)
        h_kf = sem("h_kf", 1)
        h_sil = sem("h_sil", 1)
        h_lf = sem("h_lf", NT)
        h_b = sem("h_b", NT)
        h_e = sem("h_e", NT)
        h_pr = sem("h_pr", NT)
        h_kv = sem("h_kv", NT)
        h_tr = sem("h_tr", NT)
        h_tc = sem("h_tc", NT)
        h_a = sem("h_a", NT)
        h_st = sem("h_st", NT)
        h_am = sem("h_am", NT)
        h_o = sem("h_o", NT)
        h_sq = sem("h_sq", NT)
        h_var = sem("h_var", NT)
        h_rstd = sem("h_rstd", NT)
        h_on = sem("h_on", NT)
        wbr_ld = [sem(f"wbr_ld{i}", 4 * 16) for i in range(2)]
        wbr_used = sem("wbr_used", KD)
        g_mm = sem("g_mm", 64)
        g_sig = sem("g_sig", 64)
        g_mul = sem("g_mul", 64)
        mix_ok = sem("mix_ok", 16)
        lnp_ld = sem("lnp_ld", 2 * 16)
        xr_ld = [sem(f"xr_ld{i}", 4 * 16) for i in range(2)]
        o_mm = sem("o_mm", NT)
        o_rd = sem("o_rd", NT)
        o_var = sem("o_var", NT)
        o_rstd = sem("o_rstd", NT)
        o_nrm = sem("o_nrm", NT)
        o_x1 = sem("o_x1", NT)
        x1_tr = sem("x1_tr", NT)
        x1_cp = sem("x1_cp", NT)
        lg_mm = sem("lg_mm", NT)
        rt_v = sem("rt_v", 1)
        rt_a = sem("rt_a", 1)
        sel_ok = sem("sel_ok", 1)
        rank_mm = sem("rank_mm", 1)
        tab_ok = sem("tab_ok", 1)
        disp = sem("disp", 2 * NT * 16)
        row_ld = sem("row_ld")
        row_tr = sem("row_tr")
        row_cp = sem("row_cp")
        wei_ld = [sem(f"wei_ld{k}") for k in range(KD)]
        wei_used = sem("wei_used")
        weo_ld = [sem(f"weo_ld{k}") for k in range(KF)]
        weo_used = sem("weo_used")
        hid_sil = sem("hid_sil")
        hid_ok = sem("hid_ok")
        hid_tr = sem("hid_tr")
        hid_cp = sem("hid_cp")
        y_ev = sem("y_ev")
        y_st = sem("y_st")
        y_ld = [sem(f"y_ld{i}", 8 * 16) for i in range(2)]
        y_used = sem("y_used", NT)
        f_var = sem("f_var", NT)
        f_rstd = sem("f_rstd", NT)
        f_nrm = sem("f_nrm", NT)
        f_x2 = sem("f_x2", NT)
        x2_st = [sem(f"x2_st{i}", 2 * 16) for i in range(4)]
        passed = sem("passed")

        def att_units():
            return [(t, i) for t in range(NT) for i in range(ATT)]

        block = ctx.enter_context(nc.Block())

        @block.sync
        def _(sp):
            sp.dma_start(CO[:, :], consts).then_inc(c_ld, 16)
            for t in range(NT + MT):
                if t < NT:
                    sp.dma_start(RC[:, t * D:(t + 1) * D], x[0, t * P:(t + 1) * P, :]).then_inc(nat_ld[t], 16)
                else:
                    sp.dma_start(OT[:, (t - NT) * D:(t - NT + 1) * D], mem[0, (t - NT) * P:(t - NT + 1) * P, :]
                                 ).then_inc(nat_ld[t], 16)
            sp.dma_start(hmask[:, :], chunk_mask).then_inc(c_ld, 16)
            sp.dma_start(wr[:, :, :], w_router.rearrange("(k p) e -> p k e", p=P)).then_inc(c_ld, 16)
            sp.dma_start(brt[:, :], b_router.unsqueeze(0).to_broadcast([P, E])).then_inc(c_ld, 16)
            with sp.Fori(0, LAYERS) as l:
                at = lambda s, n: l * per[s.name] + n

                def load_unit(u):
                    slot = u % 2
                    sp.wait_ge(w_used, at(w_used, u + 1))
                    if u == 0:
                        c0, n, src = 0, 2 * BW, w_mem_kv
                    elif u in (1, 2, 3):
                        c0, n = {1: (C_FQ, 2 * BW), 2: (C_MQ, BW), 3: (C_FV, BW + H)}[u]
                        src = w_in
                    elif u < GATE_U:
                        c0, n, src = C_RQ + (u - 4) * HALF, HALF, w_in
                    else:
                        c0, n, src = (u - OUT_U) * HALF, HALF, w_out
                    for q in range(4):
                        sp.dma_start(W[slot][:, 2 * q:2 * q + 2, 0:n],
                                     src[l, 256 * q:256 * q + 256, c0:c0 + n].rearrange("(k p) n -> p k n", p=P)
                                     ).then_inc(w_ld[slot], 16)

                load_unit(0)
                load_unit(1)
                for u in range(2, GATE_U):
                    load_unit(u)
                sp.wait_ge(pj_v, at(pj_v, 40))
                sp.sem_inc(passed, 1)
                with sp.Fori(0, KD // 2) as dd:
                    for b in range(2):
                        d = dd * 2 + b
                        sp.wait_ge(w_used, at(w_used, GATE_U + 1) + d)
                        for n in range(NBR):
                            sp.dma_start(W[b][:, :, n * P:(n + 1) * P],
                                         w_in[l, :, bass.ds(C_GATE + n * D + d * P, P)].rearrange(
                                             "(k p) c -> p k c", p=P)).then_inc(w_ld[b], 16)
                        sp.wait_ge(wbr_used, at(wbr_used, 1) + d)
                        sp.dma_start(WBR[b], w_branch[l, :, :, bass.ds(d * P, P)].rearrange(
                            "n (j p) c -> p (n j) c", p=P)).then_inc(wbr_ld[b], 16)
                load_unit(OUT_U)
                load_unit(OUT_U + 1)
                sp.wait_ge(g_mm, at(g_mm, 64))
                for i, src in enumerate((ln_g, ln_b)):
                    sp.dma_start(lnp[i], src[l, 0:1, :].to_broadcast([P, D])).then_inc(lnp_ld, 16)
                sp.wait_ge(x0_ld, 16)
                for i in range(4):
                    sp.wait_ge(x2_st[i], at(x2_st[i], 16))
                    sp.sem_inc(passed, 1)
                for t in range(NT):
                    sp.wait_ge(o_rd, at(o_rd, t + 1))
                    sp.dma_start(xres[t % 2], out[0, t * P:(t + 1) * P, :]).then_inc(xr_ld[t % 2], 16)
                sp.wait_ge(o_mm, at(o_mm, NT))
                for i, src in enumerate((ln_g, ln_b)):
                    sp.dma_start(lnp[2 + i], src[l, 1:2, :].to_broadcast([P, D])).then_inc(ln2_ld, 16)

                sp.wait_ge(tab_ok, at(tab_ok, 1))
                sp.sem_inc(passed, 1)
                n_tiles = sp.value_load(tab[0:1, TILES:TILES + 1], min_val=E, max_val=TILES - 1)
                g0 = sp.value_load(tab[0:1, TILES + 1:TILES + 2], min_val=0, max_val=TILES)
                sp.wait_ge(zero_st, 16)
                sp.wait_ge(disp, at(disp, 2 * NT * 16))
                sp.dma_start(ROW, rows[0:P, :]).then_inc(row_ld, 16)
                with sp.Fori(0, n_tiles) as i:
                    g = g0 + i
                    e = sp.value_load(tab[0:1, bass.ds(i, 1)], min_val=0, max_val=E - 1)
                    for k in range(KD):
                        sp.wait_ge(wei_used, g * KD + (k + 1))
                        sp.dma_start(WEI[:, k, :], w_e_in[l, e, k * P:(k + 1) * P, :]).then_inc(wei_ld[k], 16)
                    sp.wait_ge(row_tr, g + l + 1)
                    sp.dma_start(ROW, rows[bass.ds(i * P + P, P), :]).then_inc(row_ld, 16)
                    for k in range(KF):
                        sp.wait_ge(weo_used, g * KF + (k + 1))
                        sp.dma_start(WEO[:, k, :], w_e_out[l, e, k * P:(k + 1) * P, :]).then_inc(weo_ld[k], 16)
                sp.wait_ge(mt_st, 16)
                sp.wait_ge(weo_used, (g0 + n_tiles) * KF + KF)
                sp.dma_start(RA[:, 0:KD * N_MEM], mem_t).then_inc(mt_ld, 16)
                sp.sem_inc(passed, 1)
            for i in range(4):
                sp.wait_ge(x2_st[i], LAYERS * per[x2_st[i].name] + 16)

        def gain(pool, l, t):
            pool.wait_ge(f_nrm, l * NT + t + 1)
            r = x2[t % 4]
            nc.gpsimd.tensor_tensor(r, r, lnp[2], ALU.mult)
            pool.drain()
            nc.gpsimd.tensor_tensor(r, r, lnp[3], ALU.add).then_inc(f_x2, 1)

        @block.gpsimd
        def _(pool):
            pool.dma_start(WK[0:1, 2048:2048 + 2 * BW], hgrn_lb.rearrange("l (a c) -> a (l c)", a=1)
                           ).then_inc(lb_ld, 16)
            pool.wait_ge(lb_v, 2)
            pool.dma_start(keep_rate.rearrange("l (a c) -> a (l c)", a=1), WK[0:1, 3072:3072 + 2 * BW]
                           ).then_inc(lb_st, 16)
            pool.wait_ge(lb_st, 16)
            for t in (NT, NT + 1):
                pool.wait_ge(nat_ld[t], 16)
            pool.dma_start(out[0], x[0]).then_inc(x0_ld, 16)
            pool.wait_ge(nat_a, NT + MT)
            pool.wait_ge(nat_v, NT + MT)
            pool.dma_start(mem_t, RA[:, 0:KD * N_MEM]).then_inc(mt_st, 16)
            with pool.Fori(0, LAYERS) as l:
                at = lambda s, n: l * per[s.name] + n
                pool.dma_start(BR[:, :], b_in[bass.ds(l, 1), C_FV:C_MQ].to_broadcast([P, N_NAT])).then_inc(par_ld, 16)
                for a, c0, n in ((0, C_FQ, 4), (4, C_MQ, 2), (6, C_GATE, NBR * KD)):
                    pool.dma_start(b_rows[a:a + n, :], b_in[l, c0:c0 + n * P].rearrange("(c p) -> c p", p=P)
                                   ).then_inc(par_ld, 16)
                pool.dma_start(ngain[:, :], hgrn_norm_g[bass.ds(l, 1), :].to_broadcast([P, HD])).then_inc(par_ld, 16)
                pool.dma_start(omlb[:, :], keep_rate[bass.ds(l, 1), :].to_broadcast([P, BW])).then_inc(par_ld, 16)
                for t in range(NT):
                    if t == 0:
                        pool.wait_ge(lnp_ld, at(lnp_ld, 32))
                    pool.wait_ge(o_nrm, at(o_nrm, t + 1))
                    r = WK[:, (t % 2) * D:(t % 2 + 1) * D]
                    nc.gpsimd.tensor_tensor(r, r, lnp[0], ALU.mult)
                    pool.drain()
                    nc.gpsimd.tensor_tensor(X1[:, t, :], r, lnp[1], ALU.add).then_inc(o_x1, 1)
                pool.wait_ge(tab_ok, at(tab_ok, 1))
                pool.wait_ge(zero_st, 16)
                pool.wait_ge(o_x1, at(o_x1, NT))
                pool.sem_inc(passed, 1)
                for t in range(NT):
                    for j in range(2):
                        nc.gpsimd.indirect_dma_start(
                            rows, bass.IndirectOffsetOnAxis(slots[:, j, t:t + 1], 0), X1[:, t, :], None
                        ).then_inc(disp, 16)
                pool.wait_ge(disp, at(disp, 2 * NT * 16))
                pool.sem_inc(passed, 1)
                for t in range(NT):
                    nc.gpsimd.tensor_scalar(X1[:, t, :], X1[:, t, :], ALPHA, None, ALU.mult)
                pool.drain().then_inc(x1a_ok, 1)
                n_tiles = pool.value_load(tab[0:1, TILES:TILES + 1], min_val=E, max_val=TILES - 1)
                g0 = pool.value_load(tab[0:1, TILES + 1:TILES + 2], min_val=0, max_val=TILES)
                pool.wait_ge(y_st, (g0 + n_tiles + 1) * 16)
                for t in range(NT):
                    pool.wait_ge(y_used, at(y_used, t + 1))
                    pool.sem_inc(passed, 1)
                    for j in range(2):
                        nc.gpsimd.indirect_dma_start(
                            OT[:, (2 * (t % 2) + j) * D:(2 * (t % 2) + j + 1) * D], None,
                            rows, bass.IndirectOffsetOnAxis(slots[:, j, t:t + 1], 0)
                        ).then_inc(y_ld[t % 2], 16)
                    if t == 2:
                        pool.wait_ge(ln2_ld, at(ln2_ld, 32))
                    if t >= 2:
                        gain(pool, l, t - 2)
                gain(pool, l, NT - 2)
                gain(pool, l, NT - 1)

        @block.scalar
        def _(act):
            act.preload_act_table_set("natural_log_exp_and_others")
            act.wait_ge(lb_v, 1)
            nc.scalar.activation(WK[0:1, 3072:3072 + 2 * BW], WK[0:1, 2048:2048 + 2 * BW], ACT.Exp).then_inc(lb_a, 1)
            for t in range(NT + MT):
                act.wait_ge(nat_tr, t + 1)
                dst = XTk[:, 0:4, t * P:(t + 1) * P] if t < NT else memT[:, 0:4, (t - NT) * P:(t - NT + 1) * P]
                nc.scalar.copy(dst, [PA, PB][t % 2][:, 0, :].rearrange("p (k q) -> p k q", k=4)).then_inc(nat_a, 1)
            act.wait_ge(zero_ok, 1)
            act.dma_start(rows.rearrange("(n p) d -> p n d", p=P),
                          zeros.unsqueeze(1).to_broadcast([P, TILES, D])).then_inc(zero_st, 16)
            with act.Fori(0, LAYERS) as l:
                at = lambda s, n: l * per[s.name] + n
                for j in range(16):
                    if j == 4:
                        act.wait_ge(bt_tr, at(bt_tr, 1))
                        nc.scalar.copy(bT[:, :], PD[:, 0, 0:6 + NBR * KD])
                        act.drain()
                    act.wait_ge(pj, at(pj, j + 1))
                    src = PA[:, j % 2, :]
                    if j < 4:
                        nc.scalar.copy(MKV[:, j, :], src[:, 0:BW]).then_inc(pj_a, 1)
                    else:
                        c, half = (j - 4) // 2, j % 2
                        nc.scalar.activation(qkT[:, c, half * HALF:(half + 1) * HALF], src, ACT.Identity,
                                             bias=bT[:, c:c + 1]).then_inc(pj_a, 1)
                act.wait_ge(pj_v, at(pj_v, NT))
                nc.scalar.activation(ZF[:, 1, :], ZF[:, 0, :], ACT.Abs)
                act.drain()
                nc.scalar.activation(ZF[:, 2, :], ZF[:, 1, :], ACT.Exp, scale=-1.0)
                act.drain()
                nc.scalar.activation(ZF[:, 3, :], ZF[:, 2, :], ACT.Ln, bias=1.0).then_inc(z_a, 1)

                units = att_units()
                N = len(units)

                def softmax_exp(n):
                    t, i = units[n]
                    act.wait_ge(mx_ok, at(mx_ok, n + 1))
                    s = WK[:, (n % 2) * T:(n % 2 + 1) * T]
                    if i < H:
                        w = (t + 1) * P
                        nc.scalar.activation(s[:, 0:w], s[:, 0:w], ACT.Exp, bias=nm[:, n % 2, 4:5],
                                             accum_out=rs[:, n % 4, 0:1]).then_inc(p_ok, 1)
                    else:
                        act.wait_ge(pt_tr, at(pt_tr, n))
                        for h in range(H):
                            q = nc.scalar.activation(s[:, h * N_MEM:(h + 1) * N_MEM],
                                                     flat(PB)[:, perm(h) * N_MEM:(perm(h) + 1) * N_MEM], ACT.Exp,
                                                     bias=nm[:, n % 2, 4 + perm(h):5 + perm(h)], scale=QK_SCALE,
                                                     accum_out=rs[:, n % 4, h:h + 1])
                        q.then_inc(p_ok, 1)

                def copy_pt(n):
                    t, i = units[n]
                    w = (t + 1) * P if i < H else T
                    act.wait_ge(pt_tr, at(pt_tr, n + 2))
                    if n >= 2:
                        act.wait_ge(pv_mm, at(pv_mm, n))
                    nc.scalar.copy(WK[:, (2 + n % 2) * T:(2 + n % 2) * T + w], flat(PC, w)).then_inc(pt_cp, 1)

                def copy_ot(c, branch, t):
                    act.wait_ge(ot_tr, at(ot_tr, c + 1))
                    nc.scalar.copy(OTk[:, 2 * branch:2 * branch + 2, t * P:(t + 1) * P],
                                   PD[:, 1, 0:BW].rearrange("p (j q) -> p j q", j=2)).then_inc(ot_cp, 1)

                for n in range(N + 3):
                    if n < N:
                        softmax_exp(n)
                    if 1 <= n <= N:
                        copy_pt(n - 1)
                    if n >= 3 and units[n - 3][1] >= H - 1:
                        t, i = units[n - 3]
                        copy_ot(2 * t + (i == H), 0 if i < H else 3, t)

                act.wait_ge(pj_v, at(pj_v, 24))
                nc.scalar.activation(RN[:, :, 3 * BW:4 * BW], RN[:, :, 3 * BW:4 * BW], ACT.Silu).then_inc(r_sil, 1)
                act.preload_act_table_set("natural_log_exp_and_others")
                for t in range(NT):
                    act.wait_ge(r_tr, at(r_tr, t + 1))
                    nc.scalar.copy(WK[:, 1792:2304], PC[:, 0, :]).then_inc(r_qk, 1)
                    if t >= 1:
                        copy_ot(2 * NT + t - 1, 1, t - 1)
                    act.wait_ge(r_var, at(r_var, t + 1))
                    nc.scalar.activation(st[:, 8:12], st[:, 4:8], ACT.Ln)
                    act.drain()
                    nc.scalar.activation(st[:, 8:12], st[:, 8:12], ACT.Exp, scale=-0.5).then_inc(r_rstd, 1)
                copy_ot(3 * NT - 1, 1, NT - 1)

                act.wait_ge(pj_v, at(pj_v, 40))
                nc.scalar.activation(HN[:, :, 0:BW], HN[:, :, 0:BW], ACT.Sigmoid, scale=-1.0).then_inc(h_sig, 1)
                nc.scalar.activation(HN[:, :, 3 * BW:4 * BW], HN[:, :, 3 * BW:4 * BW], ACT.Silu).then_inc(h_sil, 1)
                act.preload_act_table_set("natural_log_exp_and_others")
                act.wait_ge(h_kf, at(h_kf, 1))

                def log_forget(t):
                    nc.scalar.activation(WK[:, 0:BW], HN[:, t, 0:BW], ACT.Ln, bias=1.0, scale=-1.0).then_inc(h_lf, 1)

                def decays(t):
                    act.wait_ge(h_b, at(h_b, t + 1))
                    nc.scalar.activation(WK[:, 256:1024], flat(PB, 768), ACT.Exp)
                    nc.scalar.activation(WK[:, 1024:1280], PB[:, 0, 0:BW], ACT.Exp, scale=-1.0)
                    nc.scalar.activation(hdec[:, t % 2, :, :], PB[:, 1, BW:BW + 4].rearrange("p (a b) -> p a b", a=2),
                                         ACT.Exp).then_inc(h_e, 1)

                log_forget(0)
                decays(0)
                for t in range(NT):
                    if t + 1 < NT:
                        log_forget(t + 1)
                    act.wait_ge(h_tr, at(h_tr, t + 1))
                    nc.scalar.copy(WK[:, 2304:3072], flat(PC, 768)).then_inc(h_tc, 1)
                    if t + 1 < NT:
                        decays(t + 1)
                    if t >= 1:
                        copy_ot(3 * NT + t - 1, 2, t - 1)
                    act.wait_ge(h_o, at(h_o, t + 1))
                    nc.scalar.activation(paired(WK[:, 3840:4096]), by_bank(PD, HD, 2 * P), ACT.Square).then_inc(h_sq, 1)
                    act.wait_ge(h_var, at(h_var, t + 1))
                    nc.scalar.activation(st[:, 8:12], st[:, 4:8], ACT.Ln)
                    act.drain()
                    nc.scalar.activation(st[:, 8:12], st[:, 8:12], ACT.Exp, scale=-0.5).then_inc(h_rstd, 1)
                copy_ot(4 * NT - 1, 2, NT - 1)

                with act.Fori(0, KD // 2) as dd:
                    for q in range(16):
                        b, n = q // 8, q % 4
                        act.wait_ge(g_mm, at(g_mm, q + 1) + dd * 16)
                        act.wait_ge(g_mul, at(g_mul, q + 1) + dd * 16)
                        act.sem_inc(passed, 1)
                        bank = [PA, PB][(q % 4) // 2][:, q % 2, :]
                        nc.scalar.activation(WK[:, (q % 4) * HALF:(q % 4 + 1) * HALF], bank, ACT.Sigmoid,
                                             bias=bT[:, bass.ds(dd * 2 + (6 + n * KD + b), 1)]).then_inc(g_sig, 1)

                act.preload_act_table_set("natural_log_exp_and_others")
                for t in range(NT + 1):
                    if t < NT:
                        act.wait_ge(o_var, at(o_var, t + 1))
                        nc.scalar.activation(st[:, 2:3], st[:, 1:2], ACT.Ln)
                        act.drain()
                        nc.scalar.activation(st[:, 2:3], st[:, 2:3], ACT.Exp, scale=-0.5).then_inc(o_rstd, 1)
                    if t >= 1:
                        act.wait_ge(x1_tr, at(x1_tr, t))
                        nc.scalar.copy(WK[:, 2048:3072], flat(PC)).then_inc(x1_cp, 1)
                act.wait_ge(rt_v, at(rt_v, 1))
                nc.scalar.activation(WK[:, 0:NT * E], WK[:, 0:NT * E], ACT.Exp).then_inc(rt_a, 1)

                act.wait_ge(tab_ok, at(tab_ok, 1))
                act.sem_inc(passed, 1)
                n_tiles = act.value_load(tab[0:1, TILES:TILES + 1], min_val=E, max_val=TILES - 1)
                g0 = act.value_load(tab[0:1, TILES + 1:TILES + 2], min_val=0, max_val=TILES)
                act.wait_ge(row_tr, g0 + l + 1)
                nc.scalar.copy(ROWT, flat(PC)).then_inc(row_cp, 1)
                with act.Fori(0, n_tiles) as i:
                    g = g0 + i
                    act.wait_ge(wei_used, g * KD + 2 * KD)
                    nc.scalar.activation(WK[:, 0:FE], PA[:, 0, :], ACT.Silu).then_inc(hid_sil, 1)
                    act.wait_ge(row_tr, g + l + 2)
                    nc.scalar.copy(ROWT, flat(PC)).then_inc(row_cp, 1)
                    act.wait_ge(y_ev, g + 2)
                    act.dma_start(rows[bass.ds(i * P, P), :], WK[:, 2048:3072]).then_inc(y_st, 16)
                    act.sem_inc(passed, 1)

                act.preload_act_table_set("natural_log_exp_and_others")
                for t in range(NT + 2):
                    if t < NT:
                        act.wait_ge(f_var, at(f_var, t + 1))
                        b = 4 * (t % 2)
                        nc.scalar.activation(st[:, b + 2:b + 3], st[:, b + 1:b + 2], ACT.Ln)
                        act.drain()
                        nc.scalar.activation(st[:, b + 2:b + 3], st[:, b + 2:b + 3], ACT.Exp, scale=-0.5
                                             ).then_inc(f_rstd, 1)
                    if t >= 2:
                        act.wait_ge(f_x2, at(f_x2, t - 1))
                        act.dma_start(out[0, (t - 2) * P:(t - 1) * P, :], x2[(t - 2) % 4]
                                      ).then_inc(x2_st[(t - 2) % 4], 16)
                        act.wait_ge(x2_tr, at(x2_tr, t - 1))
                        nc.scalar.copy(XTk[:, :, (t - 2) * P:(t - 1) * P],
                                       flat([PA, PB][t % 2]).rearrange("p (k q) -> p k q", k=8)).then_inc(x2_cp, 1)

        @block.vector
        def _(v):
            tt, ts, stt = nc.vector.tensor_tensor, nc.vector.tensor_scalar, nc.vector.scalar_tensor_tensor
            v.memset(zeros, 0.0).then_inc(zero_ok, 1)
            for s, n in ((w_used, 2), (pv_mm, 1), (pt_tr, 1), (pt_cp, 1), (o_ev, 1), (ot_cp, 1),
                         (wbr_used, 2), (g_mul, 4), (g_sig, 4), (o_rd, 2), (wei_used, KD), (weo_used, KF),
                         (y_ev, 1), (y_st, 16), (y_used, 2), (x2_st[0], 16), (x2_st[1], 16), (x2_st[2], 16), (x2_st[3], 16), (hid_ok, 1)):
                v.sem_inc(s, n)
            v.memset(tabf[:, :], 0.0)
            lb = WK[0:1, 2048:2048 + 2 * BW]
            ex = WK[0:1, 3072:3072 + 2 * BW]
            v.wait_ge(lb_ld, 16)
            tt(WK[0:1, 2560:2560 + BW], lb[:, 0:BW], lb[:, BW:2 * BW], ALU.max)
            v.drain()
            tt(lb[:, 0:BW], lb[:, 0:BW], WK[0:1, 2560:2560 + BW], ALU.subtract)
            tt(lb[:, BW:2 * BW], lb[:, BW:2 * BW], WK[0:1, 2560:2560 + BW], ALU.subtract).then_inc(lb_v, 1)
            v.wait_ge(lb_a, 1)
            tt(WK[0:1, 2560:2560 + BW], ex[:, 0:BW], ex[:, BW:2 * BW], ALU.add)
            v.drain()
            nc.vector.reciprocal(WK[0:1, 2560:2560 + BW], WK[0:1, 2560:2560 + BW])
            v.drain()
            tt(ex[:, BW:2 * BW], ex[:, BW:2 * BW], WK[0:1, 2560:2560 + BW], ALU.mult)
            v.drain()
            ts(ex[:, BW:2 * BW], ex[:, BW:2 * BW], -1.0, 1.0, ALU.mult, ALU.add)
            v.memset(ex[:, 0:BW], 1.0)
            v.drain().then_inc(lb_v, 1)
            v.wait_ge(c_ld, 64)
            for t in range(NT + MT):
                v.wait_ge(nat_tr, t + 1)
                dst = XTk[:, 4:8, t * P:(t + 1) * P] if t < NT else memT[:, 4:8, (t - NT) * P:(t - NT + 1) * P]
                nc.vector.tensor_copy(dst, [PA, PB][t % 2][:, 1, :].rearrange("p (k q) -> p k q", k=4)
                                      ).then_inc(nat_v, 1)

            with v.Fori(0, LAYERS) as l:
                at = lambda s, n: l * per[s.name] + n
                v.memset(rstate[:, :, :], 0.0)
                v.memset(hstate[:, 0, 0, :, :], 0.0)
                v.wait_ge(par_ld, at(par_ld, 96))
                for t in range(NT):
                    v.wait_ge(pj, at(pj, 17 + t))
                    src = PA[:, t % 2, :]
                    tt(FV[:, t, :], src[:, 0:BW], BR[:, 0:BW], ALU.add)
                    tt(ZF[:, 0, t * H:(t + 1) * H], src[:, BW:BW + H], BR[:, BW:BW + H], ALU.add).then_inc(pj_v, 1)
                v.wait_ge(z_a, at(z_a, 1))
                stt(ZF[:, 0, :], ZF[:, 0, :], 0.0, ZF[:, 3, :], ALU.min, ALU.subtract).then_inc(z_v, 1)

                def evict_proj(j, dst, c0):
                    v.wait_ge(pj, at(pj, j + 1))
                    tt(dst, PA[:, j % 2, :], BR[:, c0 - C_FV:c0 - C_FV + HALF], ALU.add).then_inc(pj_v, 1)

                lf_row, c_sum = WK[0:H, 2 * T:3 * T], WK[0:H, 3 * T:4 * T]
                v.wait_ge(lf_tr, at(lf_tr, 1))
                nc.vector.tensor_copy(lf_row, flat(PC)[0:H, :])
                v.drain()
                nc.vector.tensor_tensor_scan(c_sum, co("ones")[0:H, 0:1].to_broadcast([H, T]), lf_row, 0.0,
                                             ALU.mult, ALU.add).then_inc(c_row, 1)
                evict_proj(24, RN[:, 0, 0:HALF], C_RQ)
                evict_proj(25, RN[:, 0, HALF:2 * HALF], C_RQ + HALF)
                for h in range(H):
                    v.wait_ge(cb_mm, at(cb_mm, h + 1))
                    ts(cb[:, h, :], flat(PC), -1.0 / QK_SCALE, None, ALU.mult).then_inc(cb_cp, 1)

                units = att_units()
                N = len(units)

                def softmax_max(n):
                    t, i = units[n]
                    b = n % 2
                    s = WK[:, b * T:(b + 1) * T]
                    v.wait_ge(s_mm, at(s_mm, n + 1))
                    if i < H:
                        w = (t + 1) * P
                        v.wait_ge(pt_tr, at(pt_tr, n))
                        v.sem_inc(passed, 1)
                        nc.vector.tensor_tensor_reduce(s[:, 0:w], flat(PB, w), cb[:, i, 0:w], QK_SCALE, 2 * NEG,
                                                       ALU.add, ALU.max, nm[:, b, 0:1]).then_inc(s_rd, 1)
                        v.drain()
                        ts(nm[:, b, 4:5], nm[:, b, 0:1], -1.0, None, ALU.mult).then_inc(mx_ok, 1)
                    else:
                        nc.vector.tensor_reduce(nm[:, b, 0:H], flat(PB).rearrange("p (h m) -> p h m", h=H), AX.X, ALU.max)
                        v.drain()
                        ts(nm[:, b, 4:8], nm[:, b, 0:4], -QK_SCALE, None, ALU.mult).then_inc(mx_ok, 1)

                def normalize(n):
                    t, i = units[n]
                    v.wait_ge(pv_mm, at(pv_mm, n + 2))
                    if i < H:
                        nc.vector.reciprocal(rs[:, n % 4, 0:1], rs[:, n % 4, 0:1])
                        v.drain()
                        ts(ON[:, 0, i * HD:(i + 1) * HD], PD[:, 0, 0:HD], rs[:, n % 4, 0:1], None,
                           ALU.mult).then_inc(o_ev, 1)
                    else:
                        nc.vector.reciprocal(rs[:, n % 4, :], rs[:, n % 4, :])
                        v.drain()
                        tt(heads(ON[:, 1, :]), heads(PD[:, 0, 0:BW]), over(rs[:, n % 4, :], HD), ALU.mult
                           ).then_inc(o_ev, 1)

                for n in range(N + 2):
                    if n < N:
                        if units[n][1] == 0 and units[n][0] > 0:
                            t = units[n][0]
                            if t == NT - 1:
                                v.wait_ge(zero_st, 16)
                            evict_proj(24 + 2 * t, RN[:, t, 0:HALF], C_RQ)
                            evict_proj(25 + 2 * t, RN[:, t, HALF:2 * HALF], C_RQ + HALF)
                        softmax_max(n)
                    if n >= 2:
                        normalize(n - 2)

                v.wait_ge(r_sil, at(r_sil, 1))
                A4, B4, ROT = WK[:, 0:512], WK[:, 512:1024], WK[:, 1024:1536]
                KDC = [WK[:, 1536:1792], WK[:, 3584:3840]]
                QKT, QDT, STM = WK[:, 1792:2304], WK[:, 2304:2560], WK[:, 2560:3072]
                CEN, SQ = WK[:, 3072:3328], WK[:, 3328:3584]

                def group_norm_stats(o, done):
                    nc.vector.tensor_reduce(st[:, 0:4].rearrange("p (j a) -> p j a", j=2), o, AX.X, ALU.add)
                    v.drain()
                    ts(st[:, 0:4], st[:, 0:4], 1.0 / HD, None, ALU.mult)
                    v.drain()
                    tt(paired(CEN), o, over4(st[:, 0:4]), ALU.subtract)
                    v.drain()
                    tt(SQ, CEN, CEN, ALU.mult)
                    v.drain()
                    nc.vector.tensor_reduce(st[:, 4:8], heads(SQ), AX.X, ALU.add)
                    v.drain()
                    ts(st[:, 4:8], st[:, 4:8], 1.0 / HD, GN_EPS, ALU.mult, ALU.add).then_inc(done, 1)

                def rotate(t):
                    X8 = RN[:, t, 0:HALF].rearrange("p (h d) -> p h d", h=8)
                    cs = co("cos")[:, t * 32:(t + 1) * 32].unsqueeze(1).to_broadcast([P, 16, 32])
                    tt(A4.rearrange("p (h d) -> p h d", h=16),
                       RN[:, t, 0:HALF].rearrange("p (h d) -> p h d", h=16), cs, ALU.mult)
                    for a in range(2):
                        sn = co("sin")[:, t * HD + 32 * a:t * HD + 32 * a + 32].unsqueeze(1).to_broadcast([P, 8, 32])
                        tt(B4.rearrange("p (h d) -> p h d", h=8)[:, :, 32 * a:32 * a + 32],
                           X8[:, :, 32 - 32 * a:64 - 32 * a], sn, ALU.mult)
                    v.drain()
                    tt(ROT, A4, B4, ALU.add)
                    v.drain()
                    tt(heads(KDC[t % 2]), heads(ROT[:, BW:2 * BW]), over(co("kdec"), HD), ALU.mult).then_inc(r_rot, 1)

                rotate(0)
                for t in range(NT):
                    evict_proj(40 + 2 * t, HN[:, t, 0:HALF], C_HF)
                    v.wait_ge(r_qk, at(r_qk, t + 1))
                    tt(QDT, QKT[:, 0:BW], co("qdec"), ALU.mult)
                    v.wait_ge(r_sc, at(r_sc, t + 1))
                    tt(paired(STM), by_bank(PC, P), paired(co("rmask")), ALU.mult).then_inc(r_mk, 1)
                    if t + 1 < NT:
                        rotate(t + 1)
                    evict_proj(41 + 2 * t, HN[:, t, HALF:2 * HALF], C_HF + HALF)
                    v.wait_ge(r_o, at(r_o, t + 1))
                    tt(rstate[:, :, :], rstate[:, :, :], over(co("gtile"), HD), ALU.mult)
                    v.drain()
                    tt(rstate[:, :, :], rstate[:, :, :], PD[:, 0, 0:2 * HD].rearrange("p (j d) -> p j d", j=2), ALU.add)
                    group_norm_stats(by_bank(PB, HD), r_var)
                    v.wait_ge(r_rstd, at(r_rstd, t + 1))
                    tt(heads(CEN), heads(CEN), over(st[:, 8:12], HD), ALU.mult)
                    v.drain()
                    tt(ON[:, t % 2, :], CEN, RN[:, t, 3 * BW:4 * BW], ALU.mult).then_inc(r_on, 1)

                v.wait_ge(h_sig, at(h_sig, 1))
                tt(HN[:, :, 0:BW], HN[:, :, 0:BW], omlb[:, :].unsqueeze(1).to_broadcast([P, NT, BW]), ALU.mult
                   ).then_inc(h_kf, 1)
                v.wait_ge(h_sil, at(h_sil, 1))
                AT = WK[:, 3072:3584]
                E1, E2, E3, E1N = (WK[:, 256 + 256 * i:512 + 256 * i] for i in range(4))
                QM, Q2, KM, K3 = (WK[:, 1280 + 256 * i:1536 + 256 * i] for i in range(4))
                N1 = WK[:, 3584:3840]
                v.wait_ge(ot_tr, at(ot_tr, 3 * NT))
                v.memset(AT, 0.0)
                v.drain()
                def decayed(t):
                    kf, val, q = (HN[:, t, i * BW:(i + 1) * BW] for i in range(3))
                    v.wait_ge(h_e, at(h_e, t + 1))
                    tt(K3, kf, E3, ALU.mult)
                    tt(QM, q, E1, ALU.mult)
                    tt(Q2, q, E2, ALU.mult)
                    tt(KM, kf, E1N, ALU.mult).then_inc(h_pr, 1)

                decayed(0)
                for t in range(NT):
                    a, b = t % 2, (t + 1) % 2
                    v.wait_ge(h_kv, at(h_kv, t + 1))
                    kv = PA[:, :, 0:2 * HD].rearrange("p c (j d) -> p c j d", j=2)
                    tt(hstate[:, a, 1, :, :], hstate[:, a, 0, :, :], over(hdec[:, t % 2, :, 0], HD), ALU.mult)
                    v.drain()
                    tt(hstate[:, a, 1, :, :], hstate[:, a, 1, :, :], kv[:, 0, :, :], ALU.add)
                    v.drain()
                    tt(hstate[:, b, 0, :, :], hstate[:, a, 1, :, :], over(hdec[:, t % 2, :, 1], HD), ALU.mult)
                    v.drain()
                    tt(hstate[:, b, 0, :, :], hstate[:, b, 0, :, :], kv[:, 1, :, :], ALU.add).then_inc(h_st, 1)
                    v.wait_ge(h_a, at(h_a, t + 1))
                    v.sem_inc(passed, 1)
                    nc.vector.copy_predicated(paired(AT),
                                              hmask[:, :].unsqueeze(1).unsqueeze(1).to_broadcast([P, 2, 2, P]),
                                              by_bank(PA, P, P)).then_inc(h_am, 1)
                    if t + 1 < NT:
                        decayed(t + 1)
                    v.wait_ge(h_sq, at(h_sq, t + 1))
                    nc.vector.tensor_reduce(st[:, 4:8], heads(WK[:, 3840:4096]), AX.X, ALU.add)
                    v.drain()
                    ts(st[:, 4:8], st[:, 4:8], 1.0 / HD, GN_EPS, ALU.mult, ALU.add).then_inc(h_var, 1)
                    v.wait_ge(h_rstd, at(h_rstd, t + 1))
                    tt(paired(N1), by_bank(PD, HD, 2 * P), over4(st[:, 8:12]), ALU.mult)
                    v.drain()
                    tt(heads(N1), heads(N1), ngain[:, :].unsqueeze(1).to_broadcast([P, H, HD]), ALU.mult)
                    v.drain()
                    tt(ON[:, t % 2, :], N1, HN[:, t, 3 * BW:4 * BW], ALU.mult).then_inc(h_on, 1)

                acc, tmp = WK[:, 2048:2560], WK[:, 2560:3072]
                with v.Fori(0, KD // 2) as dd:
                    for q in range(16):
                        b, half, n = q // 8, q // 4 % 2, q % 4
                        v.wait_ge(g_sig, at(g_sig, q + 5) + dd * 16)
                        sg = WK[:, (q % 4) * HALF:(q % 4 + 1) * HALF]
                        up = [PC, PD][(q % 4) // 2][:, q % 2, :]
                        tt(acc if n == 0 else tmp, sg, up, ALU.mult).then_inc(g_mul, 1)
                        v.drain()
                        if n in (1, 2):
                            tt(acc, acc, tmp, ALU.add)
                            v.drain()
                        if n == 3:
                            tt(MIXT[:, bass.ds(dd * 2 + b, 1), half * HALF:(half + 1) * HALF],
                               acc.unsqueeze(1), tmp.unsqueeze(1), ALU.add).then_inc(mix_ok, 1)
                            v.drain()

                def norm_stats(r, done, b=0):
                    for i in range(2):
                        nc.vector.bn_stats(st[:, 8 + 6 * i:14 + 6 * i], r[:, i * HALF:(i + 1) * HALF])
                    v.drain()
                    nc.vector.bn_aggr(st[:, b:b + 2], st[:, 8:20])
                    v.drain()
                    ts(st[:, b + 1:b + 2], st[:, b + 1:b + 2], LN_EPS, None, ALU.add).then_inc(done, 1)

                for t in range(NT):
                    v.wait_ge(o_mm, at(o_mm, t + 1))
                    v.wait_ge(xr_ld[t % 2], at(xr_ld[t % 2], 16 * (t // 2 + 1)))
                    if t >= 2:
                        v.wait_ge(o_x1, at(o_x1, t - 1))
                    r = WK[:, (t % 2) * D:(t % 2 + 1) * D]
                    stt(r, xres[t % 2], ALPHA, flat([PA, PB][t % 2]), ALU.mult, ALU.add).then_inc(o_rd, 1)
                    v.drain()
                    norm_stats(r, o_var)
                    v.wait_ge(o_rstd, at(o_rstd, t + 1))
                    ts(r, r, st[:, 0:1], st[:, 2:3], ALU.subtract, ALU.mult).then_inc(o_nrm, 1)

                v.wait_ge(lg_mm, at(lg_mm, NT))
                v.wait_ge(o_x1, at(o_x1, NT))

                def te(i):
                    return WK[:, i * NT * E:(i + 1) * NT * E]

                def t3(ap, n=NT):
                    return ap.rearrange("p (t e) -> p t e", t=n)

                pr, s1, s2, both, idx, big = (te(i) for i in range(6))
                small = WK[:, 3072:4096]
                m8, mi, gm = small[:, 0:NT], small[:, 16:16 + NT], small[:, 32:32 + NT * NG]
                gs, gi = small[:, 64:64 + NT * NG], small[:, 96:96 + NT * NG]
                tt(t3(pr), t3(PD[:, 0, 0:NT * E]), brt[:, :].unsqueeze(1).to_broadcast([P, NT, E]), ALU.add)
                v.drain()
                nc.vector.tensor_reduce(m8, t3(pr), AX.X, ALU.max)
                v.drain()
                tt(t3(pr), t3(pr), over(m8, E), ALU.subtract).then_inc(rt_v, 1)
                v.wait_ge(rt_a, at(rt_a, 1))
                nc.vector.tensor_reduce(m8, t3(pr), AX.X, ALU.add)
                v.drain()
                nc.vector.reciprocal(m8, m8)
                v.drain()
                tt(t3(pr), t3(pr), over(m8, E), ALU.mult)
                v.drain()
                nc.vector.tensor_reduce(gm, t3(pr, NT * NG), AX.X, ALU.max)
                v.drain()

                def first_of_max(val, n, iota, sel, scratch):
                    nc.vector.tensor_reduce(m8, t3(val), AX.X, ALU.max)
                    v.drain()
                    tt(t3(sel), t3(val), over(m8, n), ALU.is_equal)
                    v.drain()
                    stt(t3(scratch), t3(sel), -100.0, iota.unsqueeze(1).to_broadcast([P, NT, n]), ALU.mult, ALU.add)
                    v.drain()
                    nc.vector.tensor_reduce(mi, t3(scratch), AX.X, ALU.min)
                    v.drain()
                    tt(t3(sel), t3(scratch), over(mi, n), ALU.is_equal)
                    v.drain()

                first_of_max(gm, NG, co("iota4"), gs, gi)
                tt(t3(pr, NT * NG), t3(pr, NT * NG), over(gs, EPG), ALU.mult)
                ts(gi, gs, -1.0, None, ALU.add)
                v.drain()
                tt(t3(pr, NT * NG), t3(pr, NT * NG), over(gi, EPG), ALU.add)
                v.drain()
                first_of_max(pr, E, co("iota16"), s1, idx)
                nc.vector.tensor_copy(m12[:, 0, :], m8)
                v.drain()
                stt(pr, s1, -10.0, pr, ALU.mult, ALU.add)
                v.drain()
                first_of_max(pr, E, co("iota16"), s2, idx)
                nc.vector.tensor_copy(m12[:, 1, :], m8)
                tt(both, s1, s2, ALU.add).then_inc(sel_ok, 1)
                v.drain()
                tt(m8, m12[:, 0, :], m12[:, 1, :], ALU.add)
                v.drain()
                nc.vector.reciprocal(m8, m8)
                v.drain()
                for j in range(2):
                    tt(m12[:, 2 + j, :], m12[:, j, :], m8, ALU.mult)

                v.wait_ge(rank_mm, at(rank_mm, 1))
                tot = big
                off = te(6)
                nc.vector.tensor_copy(tot, PD[:, 1, NT * E:2 * NT * E])
                v.memset(off[:, 0:E], 0.0)
                v.drain()
                for t in range(1, NT):
                    tt(off[:, t * E:(t + 1) * E], off[:, (t - 1) * E:t * E], tot[:, (t - 1) * E:t * E], ALU.add)
                    v.drain()
                cnt, ntl, cum, base = (small[:, 128 + 16 * i:144 + 16 * i] for i in range(4))
                tt(cnt, off[:, (NT - 1) * E:NT * E], tot[:, (NT - 1) * E:NT * E], ALU.add)
                v.drain()
                tt(t3(idx, E), over(cnt, 8), co("thr").unsqueeze(1).to_broadcast([P, E, 8]), ALU.is_gt)
                v.drain()
                nc.vector.tensor_reduce(ntl, t3(idx, E), AX.X, ALU.add)
                v.drain()
                nc.vector.tensor_tensor_scan(cum, co("ones")[:, 0:E], ntl, 0.0, ALU.mult, ALU.add)
                v.drain()
                tt(base, cum, ntl, ALU.subtract)
                v.drain()
                ts(base, base, float(P), None, ALU.mult)
                v.drain()
                tt(t3(off), t3(off), base.unsqueeze(1).to_broadcast([P, NT, E]), ALU.add)
                v.drain()
                tt(off, off, PD[:, 1, 0:NT * E], ALU.add)
                v.drain()
                for j, s in enumerate((s1, s2)):
                    tt(s, s, off, ALU.mult)
                    v.drain()
                    nc.vector.tensor_reduce(gm[:, j * NT:(j + 1) * NT], t3(s), AX.X, ALU.add)
                    v.drain()
                    nc.vector.tensor_copy(slots[:, j, :], gm[:, j * NT:(j + 1) * NT])
                exq = small[:, 256:256 + TILES * E]
                tt(tabf[:, TILES + 1:TILES + 2], tabf[:, TILES + 1:TILES + 2], tabf[:, TILES:TILES + 1], ALU.add)
                tt(t3(exq, TILES), cum.unsqueeze(1).to_broadcast([P, TILES, E]), over(co("iota32"), E), ALU.is_le)
                v.drain()
                nc.vector.tensor_reduce(tabf[:, 0:TILES], t3(exq, TILES), AX.X, ALU.add)
                nc.vector.tensor_copy(tabf[:, TILES:TILES + 1], cum[:, E - 1:E])
                v.drain()
                ts(tabf[:, 0:TILES], tabf[:, 0:TILES], float(E - 1), None, ALU.min)
                v.drain()
                nc.vector.tensor_copy(tab[:, :], tabf[0:1, :])
                v.drain().then_inc(tab_ok, 1)

                n_tiles = v.value_load(tab[0:1, TILES:TILES + 1], min_val=E, max_val=TILES - 1)
                g0 = v.value_load(tab[0:1, TILES + 1:TILES + 2], min_val=0, max_val=TILES)
                with v.Fori(0, n_tiles) as i:
                    g = g0 + i
                    v.wait_ge(hid_sil, g + 1)
                    tt(WK[:, 512:1024], WK[:, 0:512], PA[:, 1, :], ALU.mult).then_inc(hid_ok, 1)
                    v.wait_ge(hid_tr, g + 1)
                    nc.vector.tensor_copy(WK[:, 1024:1536], PD[:, 0, :]).then_inc(hid_cp, 1)
                    v.wait_ge(weo_used, g * KF + 2 * KF)
                    v.wait_ge(y_st, (g + 1) * 16)
                    nc.vector.tensor_copy(WK[:, 2048:3072], flat(PB)).then_inc(y_ev, 1)

                v.wait_ge(x1a_ok, at(x1a_ok, 1))
                for t in range(NT + 1):
                    if t < NT:
                        v.wait_ge(y_ld[t % 2], at(y_ld[t % 2], 32 * (t // 2 + 1)))
                        if t >= 4:
                            v.wait_ge(x2_st[t % 4], at(x2_st[t % 4], 32))
                            v.wait_ge(x2_tr, at(x2_tr, t - 3))
                        y1, y2 = (OT[:, (2 * (t % 2) + j) * D:(2 * (t % 2) + j + 1) * D] for j in range(2))
                        r = x2[t % 4]
                        stt(r, y1, m12[:, 2, t:t + 1], X1[:, t, :], ALU.mult, ALU.add)
                        v.drain()
                        stt(r, y2, m12[:, 3, t:t + 1], r, ALU.mult, ALU.add).then_inc(y_used, 1)
                        v.drain()
                        norm_stats(r, f_var, 4 * (t % 2))
                    if t >= 1:
                        v.wait_ge(f_rstd, at(f_rstd, t))
                        r, b = x2[(t - 1) % 4], 4 * ((t - 1) % 2)
                        ts(r, r, st[:, b:b + 1], st[:, b + 2:b + 3], ALU.subtract, ALU.mult).then_inc(f_nrm, 1)
                for i in range(4):
                    v.wait_ge(x2_st[i], at(x2_st[i], 48))
                    v.sem_inc(passed, 1)

        @block.tensor
        def _(pe):
            mm = nc.tensor.matmul

            def transposes(dst, src, n):
                for k in range(n):
                    q = nc.tensor.transpose(flat(dst)[:, k * P:(k + 1) * P], src[:, k * P:(k + 1) * P], ident)
                return q

            pe.wait_ge(c_ld, 64)
            for t in range(NT + MT):
                pe.wait_ge(nat_ld[t], 16)
                if t >= 2:
                    pe.wait_ge(nat_a, t - 1)
                    pe.wait_ge(nat_v, t - 1)
                src = RC[:, t * D:(t + 1) * D] if t < NT else OT[:, (t - NT) * D:(t - NT + 1) * D]
                transposes([PA, PB][t % 2], src, 8).then_inc(nat_tr, 1)
            pe.wait_ge(nat_a, NT + MT)
            pe.wait_ge(nat_v, NT + MT)
            with pe.Fori(0, LAYERS) as l:
                at = lambda s, n: l * per[s.name] + n

                def unit_loaded(u):
                    pe.wait_ge(w_ld[u % 2], at(w_ld[u % 2], 64 * (u // 2 + 1)))

                def bank_free(j):
                    if 2 <= j < 18:
                        pe.wait_ge(pj_a, at(pj_a, j - 1))
                    elif j >= 18:
                        pe.wait_ge(pj_v, at(pj_v, j - 17))

                def project(j, n, lhs, rhs):
                    bank_free(j)
                    for k in range(KD):
                        q = mm(PA[:, j % 2, 0:n], lhs(k), rhs(k), start=k == 0, stop=k == KD - 1)
                    q.then_inc(pj, 1)
                    return q

                unit_loaded(0)
                for j in range(2):
                    project(j, BW, lambda k: W[0][:, k, j * P:(j + 1) * P], lambda k: memT[:, k, :])
                for j in range(2):
                    project(2 + j, BW, lambda k: memT[:, k, j * P:(j + 1) * P], lambda k: W[0][:, k, BW:2 * BW])
                pe.drain().then_inc(w_used, 1)
                pe.wait_ge(par_ld, at(par_ld, 96))
                pe.sem_inc(passed, 1)
                nc.tensor.transpose(PD[:, 0, 0:6 + NBR * KD], b_rows, ident[0:6 + NBR * KD, 0:6 + NBR * KD]
                                    ).then_inc(bt_tr, 1)
                for u, c0, n in ((1, 0, 4), (2, 4, 2)):
                    unit_loaded(u)
                    for c in range(n):
                        for half in range(2):
                            project(4 + (c0 + c) * 2 + half, HALF,
                                    lambda k: W[u % 2][:, k, c * P:(c + 1) * P],
                                    lambda k: XTk[:, k, half * HALF:(half + 1) * HALF])
                    pe.drain().then_inc(w_used, 1)
                unit_loaded(3)
                for t in range(NT):
                    project(16 + t, BW + H, lambda k: XTk[:, k, t * P:(t + 1) * P], lambda k: W[1][:, k, 0:BW + H])
                pe.drain().then_inc(w_used, 1)

                def project_pair(first, t, which, j):
                    u = first + which
                    if t == 0:
                        unit_loaded(u)
                    project(j, HALF, lambda k: XTk[:, k, t * P:(t + 1) * P], lambda k: W[u % 2][:, k, :])
                    if t == NT - 1:
                        pe.drain().then_inc(w_used, 1)

                pe.wait_ge(z_v, at(z_v, 1))
                for t in range(NT):
                    q = nc.tensor.transpose(flat(PC)[0:H, t * P:(t + 1) * P], ZF[:, 0, t * H:(t + 1) * H], ident)
                q.then_inc(lf_tr, 1)
                project_pair(4, 0, 0, 24)
                project_pair(4, 0, 1, 25)
                pe.wait_ge(c_row, at(c_row, 1))
                for h in range(H):
                    if h >= 1:
                        pe.wait_ge(cb_cp, at(cb_cp, h))
                    for half in range(2):
                        q = mm(PC[:, half, :], ident[0:H, h:h + 1].to_broadcast([H, P]),
                               WK[0:H, 3 * T + half * HALF:3 * T + (half + 1) * HALF], start=True, stop=True)
                    q.then_inc(cb_mm, 1)
                pe.wait_ge(cb_cp, at(cb_cp, H))

                units = att_units()
                N = len(units)

                def head(c, h):
                    return slice((h % 2) * HD, (h % 2 + 1) * HD), c + h // 2

                def scores(n):
                    t, i = units[n]
                    if n >= 1 and i == 0:
                        pe.wait_ge(p_ok, at(p_ok, n))
                    elif i >= 1:
                        pe.wait_ge(s_rd, at(s_rd, t * H + i))
                    if i < H:
                        rows, cq = head(0, i)
                        ck = cq + 2
                        w = (t + 1) * P
                        for c0 in range(0, w - P, HALF):
                            c1 = min(w - P, c0 + HALF)
                            mm(flat(PB)[:, c0:c1], qkT[rows, cq, t * P:(t + 1) * P], qkT[rows, ck, c0:c1],
                               start=True, stop=True)
                        mm(flat(PB)[:, w - P:w], qkT[rows, cq, t * P:(t + 1) * P], qkT[rows, ck, w - P:w],
                           start=True, stop=False)
                        q = mm(flat(PB)[:, w - P:w], ident, co("causal"), start=False, stop=True)
                    else:
                        for h in range(H):
                            rows, cq = head(4, h)
                            q = mm(flat(PB)[:, perm(h) * N_MEM:(perm(h) + 1) * N_MEM], qkT[rows, cq, t * P:(t + 1) * P],
                                   MKV[rows, h // 2, :], start=True, stop=True)
                    q.then_inc(s_mm, 1)

                def transpose_p(n):
                    t, i = units[n]
                    pe.wait_ge(p_ok, at(p_ok, n + 1))
                    pe.wait_ge(pt_cp, at(pt_cp, n + 1))
                    transposes(PC, WK[:, (n % 2) * T:(n % 2 + 1) * T], t + 1 if i < H else 8).then_inc(pt_tr, 1)

                def times_v(n):
                    t, i = units[n]
                    pt = WK[:, (2 + n % 2) * T:(3 + n % 2) * T]
                    pe.wait_ge(pt_cp, at(pt_cp, n + 2))
                    pe.wait_ge(o_ev, at(o_ev, n + 1))
                    if i < H:
                        for kt in range(t + 1):
                            q = mm(PD[:, 0, 0:HD], pt[:, kt * P:(kt + 1) * P], FV[:, kt, i * HD:(i + 1) * HD],
                                   start=kt == 0, stop=kt == t)
                    else:
                        for h in range(H):
                            for kt in range(MT):
                                q = mm(PD[:, 0, h * HD:(h + 1) * HD], pt[:, (2 * h + kt) * P:(2 * h + kt + 1) * P],
                                       MKV[:, 2 + kt, h * HD:(h + 1) * HD], start=kt == 0, stop=kt == MT - 1)
                    q.then_inc(pv_mm, 1)

                def transpose_o(c, src):
                    pe.wait_ge(ot_cp, at(ot_cp, c + 1))
                    for j in range(2):
                        q = nc.tensor.transpose(PD[:, 1, j * P:(j + 1) * P], src[:, j * P:(j + 1) * P], ident)
                    q.then_inc(ot_tr, 1)

                for n in range(N + 3):
                    if n < N:
                        t, i = units[n]
                        if i == 0 and t > 0:
                            project_pair(4, t, 0, 24 + 2 * t)
                            project_pair(4, t, 1, 25 + 2 * t)
                        scores(n)
                    if 1 <= n <= N:
                        transpose_p(n - 1)
                    if 2 <= n <= N + 1:
                        times_v(n - 2)
                    if n >= 3 and units[n - 3][1] >= H - 1:
                        t, i = units[n - 3]
                        pe.wait_ge(o_ev, at(o_ev, n - 1))
                        transpose_o(2 * t + (i == H), ON[:, i - H + 1, :])

                ROT, QKT = WK[:, 1024:1536], WK[:, 1792:2304]
                KDC = [WK[:, 1536:1792], WK[:, 3584:3840]]
                QDT, STM = WK[:, 2304:2560], WK[:, 2560:3072]
                for t in range(NT):
                    pe.wait_ge(r_rot, at(r_rot, t + 1))
                    for c in range(4):
                        q = nc.tensor.transpose(PC[:, 0, c * P:(c + 1) * P], ROT[:, c * P:(c + 1) * P], ident)
                    q.then_inc(r_tr, 1)
                    project_pair(6, t, 0, 40 + 2 * t)
                    if t >= 1:
                        pe.wait_ge(r_on, at(r_on, t))
                        transpose_o(2 * NT + t - 1, ON[:, (t - 1) % 2, :])
                    pe.wait_ge(r_qk, at(r_qk, t + 1))
                    for h in range(H):
                        rows, c = head(0, h)
                        q = mm(PC[:, h % 2, c * P:(c + 1) * P], QKT[rows, (2 + c) * P:(3 + c) * P],
                               QKT[rows, c * P:(c + 1) * P], start=True, stop=True)
                    q.then_inc(r_sc, 1)
                    project_pair(6, t, 1, 41 + 2 * t)
                    pe.wait_ge(r_mk, at(r_mk, t + 1))
                    for h in range(H):
                        rows, c = head(0, h)
                        val = RN[:, t, 2 * BW + h * HD:2 * BW + (h + 1) * HD]
                        mm(PB[:, h % 2, c * HD:(c + 1) * HD], STM[:, h * P:(h + 1) * P], val, start=True, stop=False)
                        mm(PB[:, h % 2, c * HD:(c + 1) * HD], QDT[rows, c * P:(c + 1) * P], rstate[rows, c, :],
                           start=False, stop=True)
                    for h in range(H):
                        rows, c = head(0, h)
                        val = RN[:, t, 2 * BW + h * HD:2 * BW + (h + 1) * HD]
                        q = mm(PD[rows, 0, c * HD:(c + 1) * HD], KDC[t % 2][:, h * HD:(h + 1) * HD], val,
                               start=True, stop=True)
                    q.then_inc(r_o, 1)
                pe.wait_ge(r_on, at(r_on, NT))
                transpose_o(3 * NT - 1, ON[:, (NT - 1) % 2, :])

                AT = WK[:, 3072:3584]
                QM, Q2, KM, K3 = (WK[:, 1280 + 256 * i:1536 + 256 * i] for i in range(4))
                TQM, TQ2, TKM = (WK[:, 2304 + 256 * i:2560 + 256 * i] for i in range(3))

                def running_sums(t):
                    pe.wait_ge(h_lf, at(h_lf, t + 1))
                    if t >= 1:
                        pe.wait_ge(h_e, at(h_e, t))
                    for i, name in enumerate(("c_mid", "c_cum", "c_rest")):
                        mm(flat(PB)[:, i * BW:(i + 1) * BW], co(name), WK[:, 0:BW], start=True, stop=True)
                    for j in range(2):
                        q = mm(PB[:, 1, BW + 2 * j:BW + 2 * j + 2], WK[:, j * P:(j + 1) * P], co("c_end"),
                               start=True, stop=True)
                    q.then_inc(h_b, 1)

                running_sums(0)
                for t in range(NT):
                    val = HN[:, t, BW:2 * BW]
                    pe.wait_ge(h_pr, at(h_pr, t + 1))
                    for i, src in enumerate((QM, Q2, KM)):
                        for j in range(2):
                            q = nc.tensor.transpose(flat(PC)[:, (2 * i + j) * P:(2 * i + j + 1) * P],
                                                    src[:, j * P:(j + 1) * P], ident)
                    q.then_inc(h_tr, 1)
                    for c in range(2):
                        rc = slice(c * CH, (c + 1) * CH)
                        for h in range(H):
                            rows, p = head(0, h)
                            q = mm(PA[rows, c, p * HD:(p + 1) * HD], K3[rc, h * HD:(h + 1) * HD],
                                   val[rc, h * HD:(h + 1) * HD], start=True, stop=True)
                    q.then_inc(h_kv, 1)
                    pe.wait_ge(h_tc, at(h_tc, t + 1))
                    pe.wait_ge(h_st, at(h_st, t + 1))
                    for h in range(H):
                        rows, p = head(0, h)
                        q = mm(PA[:, h % 2, (p + 1) * P:(p + 2) * P], TKM[rows, p * P:(p + 1) * P],
                               TQM[rows, p * P:(p + 1) * P], start=True, stop=True)
                    q.then_inc(h_a, 1)
                    if t + 1 < NT:
                        running_sums(t + 1)
                    if t >= 1:
                        pe.wait_ge(h_on, at(h_on, t))
                        transpose_o(3 * NT + t - 1, ON[:, (t - 1) % 2, :])
                        pe.wait_ge(ot_cp, at(ot_cp, 3 * NT + t + 1))
                    pe.wait_ge(h_am, at(h_am, t + 1))
                    for h in range(H):
                        rows, p = head(0, h)
                        o = PD[:, h % 2, 2 * P + p * HD:2 * P + (p + 1) * HD]
                        mm(o, AT[:, h * P:(h + 1) * P], val[:, h * HD:(h + 1) * HD], start=True, stop=False,
                           skip_group_check=True)
                        for c in range(2):
                            q = mm(PD[c * CH:(c + 1) * CH, h % 2, 2 * P + p * HD:2 * P + (p + 1) * HD],
                                   TQ2[rows, p * P + c * CH:p * P + (c + 1) * CH], hstate[rows, t % 2, c, p, :],
                                   start=False, stop=c == 1, skip_group_check=True)
                    q.then_inc(h_o, 1)
                pe.wait_ge(h_on, at(h_on, NT))
                transpose_o(4 * NT - 1, ON[:, (NT - 1) % 2, :])

                pe.wait_ge(ot_cp, at(ot_cp, 4 * NT + 1))
                pe.sem_inc(passed, 1)
                with pe.Fori(0, KD // 2) as dd:
                    for b in range(2):
                        pe.wait_ge(w_ld[b], at(w_ld[b], 64 * (GATE_U // 2 + 1)) + dd * 64)
                        pe.wait_ge(wbr_ld[b], at(wbr_ld[b], 16) + dd * 16)
                        for q in range(8 * b, 8 * b + 8):
                            half, n = q // 4 % 2, q % 4
                            tok = slice(half * HALF, (half + 1) * HALF)
                            pe.wait_ge(g_sig, at(g_sig, q + 1) + dd * 16)
                            pe.wait_ge(g_mul, at(g_mul, q + 1) + dd * 16)
                            for k in range(KD):
                                z = mm([PA, PB][(q % 4) // 2][:, q % 2, :], W[b][:, k, n * P:(n + 1) * P],
                                       XTk[:, k, tok], start=k == 0, stop=k == KD - 1)
                            for j in range(2):
                                z = mm([PC, PD][(q % 4) // 2][:, q % 2, :], WBR[b][:, 2 * n + j, :],
                                       OTk[:, 2 * n + j, tok], start=j == 0, stop=j == 1)
                            z.then_inc(g_mm, 1)
                        pe.drain().then_inc(w_used, 1)
                        pe.sem_inc(wbr_used, 1)

                pe.wait_ge(mix_ok, at(mix_ok, 16))
                pe.wait_ge(g_sig, at(g_sig, 64 + 4))
                unit_loaded(OUT_U)
                unit_loaded(OUT_U + 1)
                X1T = WK[:, 2048:3072]
                for t in range(NT + 2):
                    if t < NT:
                        if t >= 2:
                            pe.wait_ge(o_rd, at(o_rd, t + 1))
                        for half in range(2):
                            for k in range(KD):
                                q = mm([PA, PB][t % 2][:, half, :], MIXT[:, k, t * P:(t + 1) * P], W[half][:, k, :],
                                       start=k == 0, stop=k == KD - 1)
                        q.then_inc(o_mm, 1)
                        if t == NT - 1:
                            pe.drain().then_inc(w_used, 2)
                    if t >= 2:
                        pe.wait_ge(x1_cp, at(x1_cp, t - 1))
                        for k in range(KD):
                            q = mm(PD[:, 0, (t - 2) * E:(t - 1) * E], X1T[:, k * P:(k + 1) * P], wr[:, k, :],
                                   start=k == 0, stop=k == KD - 1)
                        q.then_inc(lg_mm, 1)
                    if 1 <= t <= NT:
                        pe.wait_ge(o_x1, at(o_x1, t))
                        transposes(PC, X1[:, t - 1, :], 8).then_inc(x1_tr, 1)
                pe.wait_ge(sel_ok, at(sel_ok, 1))
                both = WK[:, 3 * NT * E:4 * NT * E]
                mm(PD[:, 1, 0:NT * E], co("before"), both, start=True, stop=True)
                mm(PD[:, 1, NT * E:2 * NT * E], co("ones"), both, start=True, stop=True).then_inc(rank_mm, 1)

                pe.wait_ge(tab_ok, at(tab_ok, 1))
                pe.sem_inc(passed, 1)
                n_tiles = pe.value_load(tab[0:1, TILES:TILES + 1], min_val=E, max_val=TILES - 1)
                g0 = pe.value_load(tab[0:1, TILES + 1:TILES + 2], min_val=0, max_val=TILES)
                pe.wait_ge(row_ld, (g0 + l) * 16 + 16)
                transposes(PC, ROW, 8).then_inc(row_tr, 1)
                with pe.Fori(0, n_tiles) as i:
                    g = g0 + i
                    pe.wait_ge(row_cp, g + l + 1)
                    pe.wait_ge(hid_ok, g + 1)
                    for k in range(KD):
                        pe.wait_ge(wei_ld[k], (g + 1) * 16)
                        for half in range(2):
                            q = mm(PA[:, half, :], ROWT[:, k * P:(k + 1) * P], WEI[:, k, half * HALF:(half + 1) * HALF],
                                   start=k == 0, stop=k == KD - 1)
                        q.then_inc(wei_used, 1)
                    pe.wait_ge(row_ld, (g + l) * 16 + 32)
                    transposes(PC, ROW, 8).then_inc(row_tr, 1)
                    pe.wait_ge(hid_ok, g + 2)
                    for k in range(KF):
                        q = nc.tensor.transpose(PD[:, 0, k * P:(k + 1) * P], WK[:, 512 + k * P:512 + (k + 1) * P], ident)
                    q.then_inc(hid_tr, 1)
                    pe.wait_ge(hid_cp, g + 1)
                    pe.wait_ge(y_ev, g + 1)
                    for k in range(KF):
                        pe.wait_ge(weo_ld[k], (g + 1) * 16)
                        for half in range(2):
                            q = mm(PB[:, half, :], WK[:, 1024 + k * P:1024 + (k + 1) * P],
                                   WEO[:, k, half * HALF:(half + 1) * HALF], start=k == 0, stop=k == KF - 1)
                        q.then_inc(weo_used, 1)

                for t in range(NT):
                    pe.wait_ge(f_x2, at(f_x2, t + 1))
                    if t >= 2:
                        pe.wait_ge(x2_cp, at(x2_cp, t - 1))
                    transposes([PA, PB][t % 2], x2[t % 4], 8).then_inc(x2_tr, 1)
                pe.wait_ge(x2_cp, at(x2_cp, NT))
                pe.wait_ge(mt_ld, at(mt_ld, 16))
                pe.sem_inc(passed, 1)


def constants():
    import numpy as np
    c = np.zeros((P, N_CONST), np.float32)

    def put(name, value):
        a, b = CONST[name]
        c[:, a:b] = np.asarray(value, np.float64).reshape(P, b - a)

    i = np.arange(P)
    gamma = np.log1p(-np.exp2(-5.0 - np.arange(H)))
    put("ident", np.eye(P))
    put("causal", np.where(i[:, None] >= i[None, :], 0.0, NEG / QK_SCALE))
    j_, i_ = i[:, None], i[None, :]
    seen = (i_ // CH) >= (j_ // CH)
    put("rmask", np.stack([np.where(seen, np.exp(g * np.abs(i_ - j_)), 0.0) * QK_SCALE for g in gamma], 1))
    put("qdec", np.stack([np.stack([np.exp(gamma[2 * j + p // HD] * (i + 1)) for p in range(P)]) for j in range(2)], 1))
    put("kdec", np.exp(gamma[None, :] * (P - 1 - i[:, None])) * QK_SCALE)
    put("gtile", np.stack([[np.exp(gamma[2 * j + p // HD] * P) for j in range(2)] for p in range(P)]))
    inv = (10000.0 ** (-2.0 * np.arange(HD // 2, dtype=np.float32) / HD)).astype(np.float32)
    pos = np.arange(T, dtype=np.float32)
    ang = (pos[:, None] * inv[None, :]).astype(np.float32).astype(np.float64).reshape(NT, P, HD // 2).transpose(1, 0, 2)
    put("cos", np.cos(ang))
    put("sin", np.concatenate([-np.sin(ang), np.sin(ang)], 2))
    same = (i_ // CH) == (j_ // CH)
    cum = same & (j_ <= i_)
    put("c_cum", cum)
    put("c_mid", cum * 1.0 - (same & (j_ % CH < CH // 2)))
    put("c_rest", same & (j_ > i_))
    put("c_end", np.stack([i < CH, i >= CH], 1))
    put("before", j_ < i_)
    put("ones", np.ones((P, P)))
    put("iota4", np.tile(np.arange(4), (P, 1)))
    put("iota16", np.tile(np.arange(16), (P, 1)))
    put("iota32", np.tile(np.arange(32), (P, 1)))
    put("thr", np.tile(np.arange(8) * P, (P, 1)))
    return c, (same & (j_ <= i_)).astype(np.int32)


_INS = ['x', 'mem', 'w_in', 'b_in', 'w_mem_kv', 'hgrn_lb', 'hgrn_norm_g', 'w_branch', 'w_out', 'ln_g', 'ln_b',
        'w_router', 'b_router', 'w_e_in', 'w_e_out']


def kernel(**inputs):
    import numpy as _np
    import concourse.bacc as _bacc
    from concourse import mybir as _mybir
    from concourse.bass_utils import run_bass_kernel_spmd as _run

    nc = _bacc.Bacc("TRN2", target_bir_lowering=False, num_devices=1)
    arrays, args = {}, []
    tables, mask = constants()
    for name, a in [(n, _np.ascontiguousarray(inputs[n])) for n in _INS] + [("tables", tables), ("chunk_mask", mask)]:
        arrays[f"in_{name}_dram"] = a
        args.append(nc.dram_tensor(f"in_{name}_dram", a.shape, _mybir.dt.from_np(a.dtype), kind="ExternalInput").ap())
    args.append(nc.dram_tensor("out_0_dram", (1, T, D), F32, kind="ExternalOutput").ap())
    trunk(nc, *args)
    r = _run(nc, [arrays], core_ids=[0])
    return r.results[0]["out_0_dram"]
```

```python
from contextlib import ExitStack

import concourse.bass as bass
from concourse import mybir

F32 = mybir.dt.float32
I32 = mybir.dt.int32
U32 = mybir.dt.uint32
F16 = mybir.dt.float16
ALU = mybir.AluOpType
ACT = mybir.ActivationFunctionType
AX = mybir.AxisListType

P = 128
LAYERS = 2
T = 1024
D = 1024
NT = T // P
KD = D // P
H = 4
HD = 64
BW = H * HD
NBR = 4
N_MEM = 256
MT = N_MEM // P
CH = 64
E = 16
NG = 4
EPG = E // NG
FE = 512
KF = FE // P
HALF = 512
ALPHA = (2.0 * LAYERS) ** 0.25
LN_EPS = 1e-5
GN_EPS = 1e-6
QK_SCALE = HD ** -0.5
NEG = -1e30
SX = 2.0 ** 4
SW = 2.0 ** 10
UN = 1.0 / (SX * SW)
SPARE = 2

C_FQ, C_FK, C_FV, C_FF = 0, BW, 2 * BW, 3 * BW
C_RQ = 3 * BW + H
C_HF = C_RQ + 4 * BW
C_MQ = C_HF + 4 * BW
C_GATE = C_MQ + BW
N_IN = C_GATE + NBR * D
N_NAT = C_MQ - C_FV

TILES = 2 * T // P + E
TAB_N, TAB_G, TAB_B, TAB_C = TILES, TILES + 1, TILES + 2, TILES + 3
TAB_W = TAB_C + 1 + TILES
UNITS = 18
GATE_U, OUT_U = 8, 16
ATT = H + 1

CONST = {}
_at = 0
for _name, _width in (("ident", 128), ("causal", 128), ("rmask", 512), ("qdec", 256), ("kdec", 4), ("gtile", 2),
                      ("cos", 256), ("sin", 512), ("c_mid", 128), ("c_cum", 128), ("c_rest", 128), ("c_end", 2),
                      ("before", 128), ("ones", 128), ("iota4", 4), ("iota16", 16), ("iota32", 32), ("thr", 8)):
    CONST[_name] = (_at, _at + _width)
    _at += _width
N_CONST = _at


def trunk(nc, x, mem, w_in, b_in, w_mem_kv, hgrn_lb, hgrn_norm_g, w_branch, w_out, ln_g, ln_b,
          w_router, b_router, w_e_in, w_e_out, consts, chunk_mask, out):
    with ExitStack() as ctx:
        def sb(name, shape, dt=F32):
            return ctx.enter_context(nc.sbuf_tensor(name, shape, dt))

        def pb(name):
            return ctx.enter_context(nc.psum_tensor(name, [P, 2, HALF], F32))

        per = {}

        def sem(name, per_layer=0):
            s = ctx.enter_context(nc.semaphore(name))
            per[name] = per_layer
            return s

        def dram(name, shape, dt=F32):
            return nc.dram_tensor(name, shape, dt, kind="Internal").ap()

        mem_t = dram("mem_t", [P, 2 * KD * N_MEM], F16)
        rows = dram("rows", [TILES * P, D])
        keep_rate = dram("keep_rate", [LAYERS, BW])

        XT = sb("XT", [P, KD * T])
        OT = sb("OT", [P, 8 * T])
        RA = sb("RA", [P, 8 * T])
        RC = sb("RC", [P, 8 * T])
        W = [sb(f"W{i}", [P, 8 + SPARE, HALF]) for i in range(2)]
        WK = sb("WK", [P, 4096])
        BR = sb("BR", [P, N_NAT])
        MKV = sb("MKV", [P, 4, BW])
        CO = sb("CO", [P, N_CONST])
        hmask = sb("hmask", [P, P], I32)
        bT = sb("bT", [P, 6 + NBR * KD])
        omlb = sb("omlb", [P, BW])
        ngain = sb("ngain", [P, HD])
        wr = sb("wr", [P, KD, E])
        brt = sb("brt", [P, E])
        ON = sb("ON", [P, 2, BW])
        ZF = sb("ZF", [P, 4, NT * H])
        nm = sb("nm", [P, 2, 8])
        rs = sb("rs", [P, 4, 4])
        rstate = sb("rstate", [P, 2, HD])
        hstate = sb("hstate", [P, 2, 2, 2, HD])
        hdec = sb("hdec", [P, 2, 2, 2])
        st = sb("st", [P, 32])
        m12 = sb("m12", [P, 4, NT])
        slots = sb("slots", [P, 2, NT], U32)
        tab = sb("tab", [1, TAB_W], U32)
        tabf = sb("tabf", [P, TAB_W])

        PA, PB, PC, PD = pb("PA"), pb("PB"), pb("PC"), pb("PD")

        def co(name):
            a, b = CONST[name]
            return CO[:, a:b]

        ident = co("ident")
        XS = XT[:, :].bitcast(F16).rearrange("p (s k t) -> p s k t", s=2, k=KD)
        WS = [w[:, :, :].rearrange("p k n -> p (k n)").bitcast(F16).rearrange("p (k s n) -> p k s n", s=2, n=HALF)
              for w in W]
        OTS = OT[:, :].bitcast(F16).rearrange("p (s c t) -> p s c t", s=2, c=8)
        memS = RA[:, 0:KD * N_MEM].bitcast(F16).rearrange("p (s k m) -> p s k m", s=2, k=KD)
        qkT = RC[:, 0:6 * T].rearrange("p (c t) -> p c t", c=6)
        FV = RC[:, 6 * T:8 * T].rearrange("p (t c) -> p t c", t=NT)
        RN = RA[:, :].rearrange("p (t c) -> p t c", t=NT)
        HN = RC[:, :].rearrange("p (t c) -> p t c", t=NT)
        MIXS = RA[:, :].bitcast(F16).rearrange("p (s k t) -> p s k t", s=2, k=KD)
        X1 = RC[:, :].rearrange("p (t c) -> p t c", t=NT)
        cb = [OT[:, i * T:(i + 1) * T] for i in (1, 2, 5, 6)]
        WBR = [BR[:, i * T:(i + 1) * T].rearrange("p (c m) -> p c m", c=8) for i in range(2)]
        lnp = [XT[:, 0:D], XT[:, D:2 * D], RA[:, 5 * D:6 * D], RA[:, 7 * D:8 * D]]
        zeros = RA[:, 7 * D:8 * D]
        x2 = [OT[:, (4 + i) * D:(5 + i) * D] for i in range(4)]
        xres = [XT[:, (4 + i) * D:(5 + i) * D] for i in range(2)]
        WEI = OT[:, :].rearrange("p (c t) -> p c t", c=8)
        WBS = [RC[:, i * T:(i + 1) * T].bitcast(F16).rearrange("p (s c m) -> p s c m", s=2, c=8) for i in range(2)]
        WEO = RA[:, 0:4 * T].rearrange("p (k n) -> p k n", k=KF)
        ROW = RA[:, 4 * T:5 * T]
        ROWS = RA[:, 6 * T:7 * T].bitcast(F16).rearrange("p (s n) -> p s n", s=2)
        EIS = XT[:, :].bitcast(F16).rearrange("p (s k n) -> p s k n", s=2, k=KD)
        EOS = W[0][:, 0:8, :].rearrange("p k n -> p (k n)").bitcast(F16).rearrange("p (s k n) -> p s k n", s=2, k=KF)
        HIDS = WK[:, 1024:1536].bitcast(F16).rearrange("p (s n) -> p s n", s=2)

        b_rows = WK[0:6 + NBR * KD, 2 * T:2 * T + P]

        def flat(psum, n=2 * HALF):
            return psum[:, :, :].rearrange("p a b -> p (a b)")[:, 0:n]

        def heads(ap, n=H):
            return ap.rearrange("p (h d) -> p h d", h=n)

        def by_bank(psum, n, c0=0):
            return psum[:, :, c0:c0 + 2 * n].rearrange("p a (j d) -> p j a d", j=2)

        def over4(ap):
            return ap.rearrange("p (j a) -> p j a", j=2).unsqueeze(3).to_broadcast([P, 2, 2, HD])

        def paired(ap):
            return ap.rearrange("p (j a d) -> p j a d", j=2, a=2)

        def perm(h):
            return (h % 2) * 2 + h // 2

        def over(ap, n):
            return ap.unsqueeze(2).to_broadcast([ap.shape[0], ap.shape[1], n])

        c_ld = sem("c_ld")
        x0_ld = sem("x0_ld")
        zero_ok = sem("zero_ok")
        zero_st = sem("zero_st")
        lb_ld = sem("lb_ld")
        lb_v = sem("lb_v")
        lb_a = sem("lb_a")
        lb_st = sem("lb_st")
        par_ld = sem("par_ld", 6 * 16)
        nat_ld = [sem(f"nat_ld{i}") for i in range(NT + MT)]
        bt_tr = sem("bt_tr", 1)
        nat_tr = sem("nat_tr")
        nat_a = sem("nat_a")
        nat_v = sem("nat_v")
        mt_st = sem("mt_st")
        mt_ld = sem("mt_ld", 16)
        ln2_ld = sem("ln2_ld", 2 * 16)
        x1a_ok = sem("x1a_ok", 1)
        x2_tr = sem("x2_tr", NT)
        x2_hi = sem("x2_hi", NT)
        x2_cp = sem("x2_cp", NT)
        misc_ld = sem("misc_ld")
        w_ld = [sem(f"w_ld{i}", UNITS // 2 * 64) for i in range(2)]
        w_hi = sem("w_hi", UNITS * 8)
        w_lo = sem("w_lo", UNITS * 8)
        w_used = sem("w_used", UNITS)
        pj = sem("pj", 56)
        pj_a = sem("pj_a", 16)
        pj_v = sem("pj_v", 40)
        z_v = sem("z_v", 1)
        z_a = sem("z_a", 1)
        lf_tr = sem("lf_tr", 1)
        c_row = sem("c_row", 1)
        cb_mm = sem("cb_mm", H)
        cb_cp = sem("cb_cp", H)
        s_mm = sem("s_mm", NT * ATT)
        s_rd = sem("s_rd", NT * H)
        mx_ok = sem("mx_ok", NT * ATT)
        p_ok = sem("p_ok", NT * ATT)
        pt_tr = sem("pt_tr", NT * ATT)
        pt_cp = sem("pt_cp", NT * ATT)
        pv_mm = sem("pv_mm", NT * ATT)
        o_ev = sem("o_ev", NT * ATT)
        ot_tr = sem("ot_tr", 4 * NT)
        ot_hi = sem("ot_hi", 4 * NT)
        ot_cp = sem("ot_cp", 4 * NT)
        r_sil = sem("r_sil", 1)
        r_rot = sem("r_rot", NT)
        r_tr = sem("r_tr", NT)
        r_qk = sem("r_qk", NT)
        r_sc = sem("r_sc", NT)
        r_mk = sem("r_mk", NT)
        r_o = sem("r_o", NT)
        r_var = sem("r_var", NT)
        r_rstd = sem("r_rstd", NT)
        r_on = sem("r_on", NT)
        h_sig = sem("h_sig", 1)
        h_kf = sem("h_kf", 1)
        h_sil = sem("h_sil", 1)
        h_lf = sem("h_lf", NT)
        h_b = sem("h_b", NT)
        h_e = sem("h_e", NT)
        h_pr = sem("h_pr", NT)
        h_kv = sem("h_kv", NT)
        h_tr = sem("h_tr", NT)
        h_tc = sem("h_tc", NT)
        h_a = sem("h_a", NT)
        h_st = sem("h_st", NT)
        h_am = sem("h_am", NT)
        h_o = sem("h_o", NT)
        h_sq = sem("h_sq", NT)
        h_var = sem("h_var", NT)
        h_rstd = sem("h_rstd", NT)
        h_on = sem("h_on", NT)
        wbr_ld = [sem(f"wbr_ld{i}", 4 * 16) for i in range(2)]
        wbr_hi = sem("wbr_hi", KD)
        wbr_lo = sem("wbr_lo", KD)
        g_mm = sem("g_mm", 64)
        g_sig = sem("g_sig", 64)
        g_mul = sem("g_mul", 64)
        mix_f = sem("mix_f", 16)
        mix_hi = sem("mix_hi", 16)
        mix_ok = sem("mix_ok", 16)
        lnp_ld = sem("lnp_ld", 2 * 16)
        xr_ld = [sem(f"xr_ld{i}", 4 * 16) for i in range(2)]
        o_mm = sem("o_mm", NT)
        o_rd = sem("o_rd", NT)
        o_var = sem("o_var", NT)
        o_rstd = sem("o_rstd", NT)
        o_nrm = sem("o_nrm", NT)
        o_x1 = sem("o_x1", NT)
        x1_tr = sem("x1_tr", NT)
        x1_cp = sem("x1_cp", NT)
        lg_mm = sem("lg_mm", NT)
        rt_v = sem("rt_v", 1)
        rt_a = sem("rt_a", 1)
        sel_ok = sem("sel_ok", 1)
        rank_mm = sem("rank_mm", 1)
        tab_ok = sem("tab_ok", 1)
        disp = sem("disp", 2 * NT * 16)
        row_ld = sem("row_ld")
        row_tr = sem("row_tr")
        row_hi = sem("row_hi")
        row_lo = sem("row_lo")
        wei_ld = [sem(f"wei_ld{k}") for k in range(KD)]
        wei_used = sem("wei_used")
        weo_ld = [sem(f"weo_ld{k}") for k in range(KF)]
        weo_used = sem("weo_used")
        hid_sil = sem("hid_sil")
        hid_ok = sem("hid_ok")
        hid_tr = sem("hid_tr")
        hid_hi = sem("hid_hi")
        hid_lo = sem("hid_lo")
        ei_hi = sem("ei_hi")
        ei_lo = sem("ei_lo")
        eo_hi = sem("eo_hi")
        eo_lo = sem("eo_lo")
        y_ev = sem("y_ev")
        y_st = sem("y_st")
        y_ld = [sem(f"y_ld{i}", 8 * 16) for i in range(2)]
        y_used = sem("y_used", NT)
        f_var = sem("f_var", NT)
        f_ms = sem("f_ms", NT)
        f_nrm = sem("f_nrm", NT)
        f_x2 = sem("f_x2", NT)
        x2_st = [sem(f"x2_st{i}", 2 * 16) for i in range(4)]
        passed = sem("passed")

        def turned(branch):
            return PC[:, 1, BW:2 * BW] if branch == 2 else PD[:, 1, 0:BW]

        def in_part(part, t):
            if t < NT:
                return XS[:, part, :, t * P:(t + 1) * P]
            return memS[:, part, :, (t - NT) * P:(t - NT + 1) * P]

        def w_width(u):
            return {2: BW, 3: BW + H}.get(u, HALF)

        def loads(eng, i):
            at_ = TAB_C + 1 + i if isinstance(i, int) else i + (TAB_C + 1)
            return eng.value_load(tab[0:1, bass.ds(at_, 1)], min_val=0, max_val=LAYERS * E)

        def att_units():
            return [(t, i) for t in range(NT) for i in range(ATT)]

        block = ctx.enter_context(nc.Block())

        @block.sync
        def _(sp):
            sp.dma_start(CO[:, :], consts).then_inc(c_ld, 16)
            for t in range(NT + MT):
                if t < NT:
                    sp.dma_start(RC[:, t * D:(t + 1) * D], x[0, t * P:(t + 1) * P, :]).then_inc(nat_ld[t], 16)
                else:
                    sp.dma_start(OT[:, (t - NT) * D:(t - NT + 1) * D], mem[0, (t - NT) * P:(t - NT + 1) * P, :]
                                 ).then_inc(nat_ld[t], 16)
            sp.dma_start(hmask[:, :], chunk_mask).then_inc(misc_ld, 16)
            sp.dma_start(wr[:, :, :], w_router.rearrange("(k p) e -> p k e", p=P)).then_inc(misc_ld, 16)
            sp.dma_start(brt[:, :], b_router.unsqueeze(0).to_broadcast([P, E])).then_inc(misc_ld, 16)
            with sp.Fori(0, LAYERS) as l:
                at = lambda s, n: l * per[s.name] + n

                def load_unit(u):
                    slot = u % 2
                    sp.wait_ge(w_used, at(w_used, u + 1))
                    if u == 0:
                        c0, n, src = 0, 2 * BW, w_mem_kv
                    elif u in (1, 2, 3):
                        c0, n = {1: (C_FQ, 2 * BW), 2: (C_MQ, BW), 3: (C_FV, BW + H)}[u]
                        src = w_in
                    elif u < GATE_U:
                        c0, n, src = C_RQ + (u - 4) * HALF, HALF, w_in
                    else:
                        c0, n, src = (u - OUT_U) * HALF, HALF, w_out
                    for q in range(4):
                        sp.dma_start(W[slot][:, SPARE + 2 * q:SPARE + 2 * q + 2, 0:n],
                                     src[l, 256 * q:256 * q + 256, c0:c0 + n].rearrange("(k p) n -> p k n", p=P)
                                     ).then_inc(w_ld[slot], 16)

                load_unit(0)
                load_unit(1)
                for u in range(2, GATE_U):
                    load_unit(u)
                sp.wait_ge(pj_v, at(pj_v, 40))
                sp.sem_inc(passed, 1)
                with sp.Fori(0, KD // 2) as dd:
                    for b in range(2):
                        d = dd * 2 + b
                        sp.wait_ge(w_used, at(w_used, GATE_U + 1) + d)
                        for n in range(NBR):
                            sp.dma_start(W[b][:, SPARE:8 + SPARE, n * P:(n + 1) * P],
                                         w_in[l, :, bass.ds(C_GATE + n * D + d * P, P)].rearrange(
                                             "(k p) c -> p k c", p=P)).then_inc(w_ld[b], 16)
                        sp.wait_ge(wbr_lo, at(wbr_lo, 1) + d)
                        sp.dma_start(WBR[b], w_branch[l, :, :, bass.ds(d * P, P)].rearrange(
                            "n (j p) c -> p (n j) c", p=P)).then_inc(wbr_ld[b], 16)
                load_unit(OUT_U)
                load_unit(OUT_U + 1)
                sp.wait_ge(g_mm, at(g_mm, 64))
                for i, src in enumerate((ln_g, ln_b)):
                    sp.dma_start(lnp[i], src[l, 0:1, :].to_broadcast([P, D])).then_inc(lnp_ld, 16)
                sp.wait_ge(x0_ld, 16)
                for i in range(4):
                    sp.wait_ge(x2_st[i], at(x2_st[i], 16))
                    sp.sem_inc(passed, 1)
                for t in range(NT):
                    sp.wait_ge(o_rd, at(o_rd, t + 1))
                    sp.dma_start(xres[t % 2], out[0, t * P:(t + 1) * P, :]).then_inc(xr_ld[t % 2], 16)
                sp.wait_ge(o_mm, at(o_mm, NT))
                for i, src in enumerate((ln_g, ln_b)):
                    sp.dma_start(lnp[2 + i], src[l, 1:2, :].to_broadcast([P, D])).then_inc(ln2_ld, 16)

                sp.wait_ge(tab_ok, at(tab_ok, 1))
                sp.sem_inc(passed, 1)
                before_last = sp.value_load(tab[0:1, TILES + 2:TILES + 3], min_val=E - 2, max_val=TILES - 3)
                last = before_last + 1
                g0 = sp.value_load(tab[0:1, TILES + 1:TILES + 2], min_val=0, max_val=TILES)

                def load_ei(i, before):
                    e = sp.value_load(tab[0:1, bass.ds(i, 1)], min_val=0, max_val=E - 1)
                    for k in range(KD):
                        sp.wait_ge(ei_lo, before * KD + (k + 1))
                        sp.dma_start(WEI[:, k, :], w_e_in[l, e, k * P:(k + 1) * P, :]).then_inc(wei_ld[k], 16)

                def load_eo(i, before):
                    e = sp.value_load(tab[0:1, bass.ds(i, 1)], min_val=0, max_val=E - 1)
                    for k in range(KF):
                        sp.wait_ge(eo_lo, before * KF + (k + 1))
                        sp.dma_start(WEO[:, k, :], w_e_out[l, e, k * P:(k + 1) * P, :]).then_inc(weo_ld[k], 16)

                sp.wait_ge(zero_st, 16)
                sp.wait_ge(disp, at(disp, 2 * NT * 16))
                sp.dma_start(ROW, rows[0:P, :]).then_inc(row_ld, 16)
                load_ei(0, loads(sp, -1))
                sp.wait_ge(row_tr, g0 + l + 1)
                sp.dma_start(ROW, rows[P:2 * P, :]).then_inc(row_ld, 16)
                with sp.Fori(0, last) as i:
                    c0, c1, c2 = loads(sp, i - 1), loads(sp, i), loads(sp, i + 1)
                    with sp.If(c1 < c2):
                        load_ei(i + 1, c1)
                    sp.wait_ge(row_tr, g0 + i + (l + 2))
                    sp.dma_start(ROW, rows[bass.ds(i * P + 2 * P, P), :]).then_inc(row_ld, 16)
                    with sp.If(c0 < c1):
                        load_eo(i, c0)
                c0, c1 = loads(sp, before_last), loads(sp, last)
                with sp.If(c0 < c1):
                    load_eo(last, c0)
                sp.wait_ge(mt_st, 16)
                sp.wait_ge(weo_used, (g0 + last + 2) * KF)
                sp.dma_start(RA[:, 0:KD * N_MEM].bitcast(F16), mem_t).then_inc(mt_ld, 16)
                sp.sem_inc(passed, 1)
            for i in range(4):
                sp.wait_ge(x2_st[i], LAYERS * per[x2_st[i].name] + 16)

        def gain(pool, l, t):
            pool.wait_ge(f_nrm, l * NT + t + 1)
            r = x2[t % 4]
            nc.gpsimd.tensor_tensor(r, r, lnp[3], ALU.add).then_inc(f_x2, 1)

        @block.gpsimd
        def _(pool):
            pool.dma_start(WK[0:1, 2048:2048 + 2 * BW], hgrn_lb.rearrange("l (a c) -> a (l c)", a=1)
                           ).then_inc(lb_ld, 16)
            pool.wait_ge(lb_v, 2)
            pool.dma_start(keep_rate.rearrange("l (a c) -> a (l c)", a=1), WK[0:1, 3072:3072 + 2 * BW]
                           ).then_inc(lb_st, 16)
            pool.wait_ge(lb_st, 16)
            with pool.Fori(0, LAYERS) as l:
                at = lambda s, n: l * per[s.name] + n
                pool.dma_start(BR[:, :], b_in[bass.ds(l, 1), C_FV:C_MQ].to_broadcast([P, N_NAT])).then_inc(par_ld, 16)
                for a, c0, n in ((0, C_FQ, 4), (4, C_MQ, 2), (6, C_GATE, NBR * KD)):
                    pool.dma_start(b_rows[a:a + n, :], b_in[l, c0:c0 + n * P].rearrange("(c p) -> c p", p=P)
                                   ).then_inc(par_ld, 16)
                pool.dma_start(ngain[:, :], hgrn_norm_g[bass.ds(l, 1), :].to_broadcast([P, HD])).then_inc(par_ld, 16)
                pool.dma_start(omlb[:, :], keep_rate[bass.ds(l, 1), :].to_broadcast([P, BW])).then_inc(par_ld, 16)
                for t in range(NT):
                    if t == 0:
                        pool.wait_ge(lnp_ld, at(lnp_ld, 32))
                    pool.wait_ge(o_nrm, at(o_nrm, t + 1))
                    r = WK[:, (t % 2) * D:(t % 2 + 1) * D]
                    nc.gpsimd.tensor_tensor(r, r, lnp[0], ALU.mult)
                    pool.drain()
                    nc.gpsimd.tensor_tensor(X1[:, t, :], r, lnp[1], ALU.add).then_inc(o_x1, 1)
                pool.wait_ge(tab_ok, at(tab_ok, 1))
                pool.wait_ge(zero_st, 16)
                pool.wait_ge(o_x1, at(o_x1, NT))
                pool.sem_inc(passed, 1)
                for t in range(NT):
                    for j in range(2):
                        nc.gpsimd.indirect_dma_start(
                            rows, bass.IndirectOffsetOnAxis(slots[:, j, t:t + 1], 0), X1[:, t, :], None
                        ).then_inc(disp, 16)
                pool.wait_ge(disp, at(disp, 2 * NT * 16))
                pool.sem_inc(passed, 1)
                for t in range(NT):
                    nc.gpsimd.tensor_scalar(X1[:, t, :], X1[:, t, :], ALPHA, None, ALU.mult)
                pool.drain().then_inc(x1a_ok, 1)
                n_tiles = pool.value_load(tab[0:1, TILES:TILES + 1], min_val=E, max_val=TILES - 1)
                g0 = pool.value_load(tab[0:1, TILES + 1:TILES + 2], min_val=0, max_val=TILES)
                pool.wait_ge(y_st, (g0 + n_tiles + 1) * 16)
                for t in range(NT):
                    pool.wait_ge(y_used, at(y_used, t + 1))
                    pool.sem_inc(passed, 1)
                    for j in range(2):
                        nc.gpsimd.indirect_dma_start(
                            OT[:, (2 * (t % 2) + j) * D:(2 * (t % 2) + j + 1) * D], None,
                            rows, bass.IndirectOffsetOnAxis(slots[:, j, t:t + 1], 0)
                        ).then_inc(y_ld[t % 2], 16)
                    if t == 2:
                        pool.wait_ge(ln2_ld, at(ln2_ld, 32))
                    if t >= 2:
                        gain(pool, l, t - 2)
                gain(pool, l, NT - 2)
                gain(pool, l, NT - 1)

        @block.scalar
        def _(act):
            act.preload_act_table_set("natural_log_exp_and_others")
            act.wait_ge(lb_v, 1)
            nc.scalar.activation(WK[0:1, 3072:3072 + 2 * BW], WK[0:1, 2048:2048 + 2 * BW], ACT.Exp).then_inc(lb_a, 1)
            for t in range(NT + MT):
                act.wait_ge(nat_tr, t + 1)
                nc.scalar.activation(in_part(0, t), flat([PA, PB][t % 2]).rearrange("p (k q) -> p k q", k=8),
                                     ACT.Copy, scale=SX).then_inc(nat_a, 1)
            act.wait_ge(nat_v, NT + MT)
            act.dma_start(mem_t, RA[:, 0:KD * N_MEM].bitcast(F16)).then_inc(mt_st, 16)
            act.wait_ge(par_ld, 96)
            act.wait_ge(w_ld[0], 64)
            act.wait_ge(w_ld[1], 64)
            act.dma_start(out[0], x[0]).then_inc(x0_ld, 16)
            act.wait_ge(zero_ok, 1)
            act.dma_start(rows.rearrange("(n p) d -> p n d", p=P),
                          zeros.unsqueeze(1).to_broadcast([P, TILES, D])).then_inc(zero_st, 16)
            with act.Fori(0, LAYERS) as l:
                at = lambda s, n: l * per[s.name] + n

                def high_parts(u, chunks=range(8), d=None, b=None):
                    slot = u % 2 if b is None else b
                    c0, w0 = (8 * u, 64 * (u // 2 + 1)) if d is None else (8 * u + d * 8, 64 * (u // 2 + 1) + d * 32)
                    n = w_width(u)
                    for k in chunks:
                        if k == 0:
                            act.wait_ge(w_ld[slot], at(w_ld[slot], w0))
                        if k >= SPARE:
                            act.wait_ge(w_lo, at(w_lo, c0 + k - SPARE + 1))
                        nc.scalar.activation(WS[slot][:, k, 0, 0:n], W[slot][:, k + SPARE, 0:n], ACT.Copy, scale=SW
                                             ).then_inc(w_hi, 1)

                high_parts(0)
                high_parts(1)
                for j in range(16):
                    if 8 <= j < 12:
                        high_parts(2, range(2 * (j - 8), 2 * (j - 8) + 2))
                    if j >= 14:
                        high_parts(3, range(4 * (j - 14), 4 * (j - 14) + 4))
                    if j == 4:
                        act.wait_ge(bt_tr, at(bt_tr, 1))
                        nc.scalar.copy(bT[:, :], PD[:, 0, 0:6 + NBR * KD])
                        act.drain()
                    act.wait_ge(pj, at(pj, j + 1))
                    src = PA[:, j % 2, :]
                    if j < 4:
                        nc.scalar.activation(MKV[:, j, :], src[:, 0:BW], ACT.Copy, scale=UN).then_inc(pj_a, 1)
                    else:
                        c, half = (j - 4) // 2, j % 2
                        nc.scalar.activation(qkT[:, c, half * HALF:(half + 1) * HALF], src, ACT.Identity,
                                             bias=bT[:, c:c + 1], scale=UN).then_inc(pj_a, 1)
                high_parts(4)
                act.wait_ge(pj_v, at(pj_v, NT))
                nc.scalar.activation(ZF[:, 1, :], ZF[:, 0, :], ACT.Abs)
                act.drain()
                nc.scalar.activation(ZF[:, 2, :], ZF[:, 1, :], ACT.Exp, scale=-1.0)
                act.drain()
                nc.scalar.activation(ZF[:, 3, :], ZF[:, 2, :], ACT.Ln, bias=1.0).then_inc(z_a, 1)
                high_parts(5)

                units = att_units()
                N = len(units)

                def softmax_exp(n):
                    t, i = units[n]
                    act.wait_ge(mx_ok, at(mx_ok, n + 1))
                    s = WK[:, (n % 2) * T:(n % 2 + 1) * T]
                    if i < H:
                        w = (t + 1) * P
                        nc.scalar.activation(s[:, 0:w], s[:, 0:w], ACT.Exp, bias=nm[:, n % 2, 4:5],
                                             accum_out=rs[:, n % 4, 0:1]).then_inc(p_ok, 1)
                    else:
                        act.wait_ge(pt_tr, at(pt_tr, n))
                        for h in range(H):
                            q = nc.scalar.activation(s[:, h * N_MEM:(h + 1) * N_MEM],
                                                     flat(PB)[:, perm(h) * N_MEM:(perm(h) + 1) * N_MEM], ACT.Exp,
                                                     bias=nm[:, n % 2, 4 + perm(h):5 + perm(h)], scale=QK_SCALE,
                                                     accum_out=rs[:, n % 4, h:h + 1])
                        q.then_inc(p_ok, 1)

                def copy_pt(n):
                    t, i = units[n]
                    w = (t + 1) * P if i < H else T
                    act.wait_ge(pt_tr, at(pt_tr, n + 2))
                    if n >= 2:
                        act.wait_ge(pv_mm, at(pv_mm, n))
                    nc.scalar.copy(WK[:, (2 + n % 2) * T:(2 + n % 2) * T + w], flat(PC, w)).then_inc(pt_cp, 1)

                def copy_ot(c, branch, t):
                    act.wait_ge(ot_tr, at(ot_tr, c + 1))
                    nc.scalar.activation(OTS[:, 0, 2 * branch:2 * branch + 2, t * P:(t + 1) * P],
                                         turned(branch).rearrange("p (j q) -> p j q", j=2), ACT.Copy, scale=SX
                                         ).then_inc(ot_hi, 1)

                for n in range(N + 3):
                    if N - 4 <= n < N:
                        i = n - (N - 4)
                        high_parts(6 + i // 2, range(4 * (i % 2), 4 * (i % 2) + 4))
                    if n < N:
                        softmax_exp(n)
                    if 1 <= n <= N:
                        copy_pt(n - 1)
                    if n >= 3 and units[n - 3][1] >= H - 1:
                        t, i = units[n - 3]
                        copy_ot(2 * t + (i == H), 0 if i < H else 3, t)

                act.wait_ge(pj_v, at(pj_v, 24))
                nc.scalar.activation(RN[:, :, 3 * BW:4 * BW], RN[:, :, 3 * BW:4 * BW], ACT.Silu).then_inc(r_sil, 1)
                act.preload_act_table_set("natural_log_exp_and_others")
                for t in range(NT):
                    act.wait_ge(r_tr, at(r_tr, t + 1))
                    nc.scalar.copy(WK[:, 1792:2304], PC[:, 0, :]).then_inc(r_qk, 1)
                    if t >= 1:
                        copy_ot(2 * NT + t - 1, 1, t - 1)
                    act.wait_ge(r_var, at(r_var, t + 1))
                    nc.scalar.activation(st[:, 8:12], st[:, 4:8], ACT.Ln)
                    act.drain()
                    nc.scalar.activation(st[:, 8:12], st[:, 8:12], ACT.Exp, scale=-0.5).then_inc(r_rstd, 1)
                copy_ot(3 * NT - 1, 1, NT - 1)

                act.wait_ge(pj_v, at(pj_v, 40))
                nc.scalar.activation(HN[:, :, 0:BW], HN[:, :, 0:BW], ACT.Sigmoid, scale=-1.0).then_inc(h_sig, 1)
                nc.scalar.activation(HN[:, :, 3 * BW:4 * BW], HN[:, :, 3 * BW:4 * BW], ACT.Silu).then_inc(h_sil, 1)
                act.preload_act_table_set("natural_log_exp_and_others")
                act.wait_ge(h_kf, at(h_kf, 1))

                def log_forget(t):
                    nc.scalar.activation(WK[:, 0:BW], HN[:, t, 0:BW], ACT.Ln, bias=1.0, scale=-1.0).then_inc(h_lf, 1)

                def decays(t):
                    act.wait_ge(h_b, at(h_b, t + 1))
                    nc.scalar.activation(WK[:, 256:1024], flat(PB, 768), ACT.Exp)
                    nc.scalar.activation(WK[:, 1024:1280], PB[:, 0, 0:BW], ACT.Exp, scale=-1.0)
                    nc.scalar.activation(hdec[:, t % 2, :, :], PB[:, 1, BW:BW + 4].rearrange("p (a b) -> p a b", a=2),
                                         ACT.Exp).then_inc(h_e, 1)

                log_forget(0)
                decays(0)
                for t in range(NT):
                    if t + 1 < NT:
                        log_forget(t + 1)
                    act.wait_ge(h_tr, at(h_tr, t + 1))
                    nc.scalar.copy(WK[:, 2304:3072], flat(PC, 768)).then_inc(h_tc, 1)
                    if t + 1 < NT:
                        decays(t + 1)
                    if t >= 1:
                        copy_ot(3 * NT + t - 1, 2, t - 1)
                    if t >= 4:
                        high_parts(GATE_U, range(2 * (t - 4), 2 * (t - 4) + 2))
                    act.wait_ge(h_o, at(h_o, t + 1))
                    nc.scalar.activation(paired(WK[:, 3840:4096]), by_bank(PD, HD, 2 * P), ACT.Square).then_inc(h_sq, 1)
                    act.wait_ge(h_var, at(h_var, t + 1))
                    nc.scalar.activation(st[:, 8:12], st[:, 4:8], ACT.Ln)
                    act.drain()
                    nc.scalar.activation(st[:, 8:12], st[:, 8:12], ACT.Exp, scale=-0.5).then_inc(h_rstd, 1)
                copy_ot(4 * NT - 1, 2, NT - 1)

                with act.Fori(0, KD // 2) as dd:
                    for q in range(16):
                        b, n = q // 8, q % 4
                        if q % 8 == 0:
                            act.wait_ge(wbr_ld[b], at(wbr_ld[b], 16) + dd * 16)
                            act.sem_inc(passed, 1)
                            nc.scalar.activation(WBS[b][:, 0, :, :], WBR[b], ACT.Copy, scale=SW).then_inc(wbr_hi, 1)
                        if q % 8 == 2:
                            high_parts(GATE_U + 1 + b, d=2 * dd, b=1 - b)
                        act.wait_ge(g_mm, at(g_mm, q + 1) + dd * 16)
                        act.wait_ge(g_mul, at(g_mul, q + 1) + dd * 16)
                        act.sem_inc(passed, 1)
                        bank = [PA, PB][(q % 4) // 2][:, q % 2, :]
                        nc.scalar.activation(WK[:, (q % 4) * HALF:(q % 4 + 1) * HALF], bank, ACT.Sigmoid,
                                             bias=bT[:, bass.ds(dd * 2 + (6 + n * KD + b), 1)], scale=UN
                                             ).then_inc(g_sig, 1)
                        if n == 3:
                            act.wait_ge(mix_f, at(mix_f, q // 4 + 1) + dd * 4)
                            act.sem_inc(passed, 1)
                            nc.scalar.activation(MIXS[:, 0, bass.ds(dd * 2 + b, 1), q // 4 % 2 * HALF:(q // 4 % 2 + 1) * HALF],
                                                 WK[:, 3072:3584].unsqueeze(1), ACT.Copy, scale=SX).then_inc(mix_hi, 1)
                high_parts(OUT_U + 1)

                act.preload_act_table_set("natural_log_exp_and_others")
                for t in range(NT + 1):
                    if t < NT:
                        act.wait_ge(o_var, at(o_var, t + 1))
                        nc.scalar.activation(st[:, 2:3], st[:, 1:2], ACT.Ln)
                        act.drain()
                        nc.scalar.activation(st[:, 2:3], st[:, 2:3], ACT.Exp, scale=-0.5).then_inc(o_rstd, 1)
                    if t >= 1:
                        act.wait_ge(x1_tr, at(x1_tr, t))
                        nc.scalar.copy(WK[:, 2048:3072], flat(PC)).then_inc(x1_cp, 1)
                act.wait_ge(rt_v, at(rt_v, 1))
                nc.scalar.activation(WK[:, 0:NT * E], WK[:, 0:NT * E], ACT.Exp).then_inc(rt_a, 1)

                act.wait_ge(tab_ok, at(tab_ok, 1))
                act.sem_inc(passed, 1)
                before_last = act.value_load(tab[0:1, TILES + 2:TILES + 3], min_val=E - 2, max_val=TILES - 3)
                last = before_last + 1
                g0 = act.value_load(tab[0:1, TILES + 1:TILES + 2], min_val=0, max_val=TILES)

                def ei_high(i, before):
                    for k in range(KD):
                        act.wait_ge(wei_ld[k], (before + 1) * 16)
                        act.wait_ge(wei_used, (g0 + i) * KD + (k + 1))
                        nc.scalar.activation(EIS[:, 0, k, :], WEI[:, k, :], ACT.Copy, scale=SW).then_inc(ei_hi, 1)

                def eo_high(i, before):
                    for k in range(KF):
                        act.wait_ge(weo_ld[k], (before + 1) * 16)
                        act.wait_ge(weo_used, (g0 + i) * KF + (k + 1))
                        nc.scalar.activation(EOS[:, 0, k, :], WEO[:, k, :], ACT.Copy, scale=SW).then_inc(eo_hi, 1)

                def row_high(i):
                    act.wait_ge(row_tr, g0 + i + (l + 1))
                    nc.scalar.activation(ROWS[:, 0, :], flat(PC), ACT.Copy, scale=SX).then_inc(row_hi, 1)

                def hidden_high(i):
                    act.wait_ge(hid_tr, g0 + i + 1)
                    nc.scalar.activation(HIDS[:, 0, :], PD[:, 0, :], ACT.Copy, scale=SX).then_inc(hid_hi, 1)

                def silu(i):
                    act.wait_ge(wei_used, (g0 + i + 2) * KD)
                    nc.scalar.activation(WK[:, 0:FE], PA[:, 0, :], ACT.Silu, scale=UN).then_inc(hid_sil, 1)

                def store_rows(i):
                    act.wait_ge(weo_used, (g0 + i + 2) * KF)
                    act.wait_ge(y_st, (g0 + i + 1) * 16)
                    nc.scalar.activation(WK[:, 2048:3072], flat(PB), ACT.Copy, scale=UN).then_inc(y_ev, 1)
                    act.drain()
                    act.dma_start(rows[bass.ds(i * P, P), :], WK[:, 2048:3072]).then_inc(y_st, 16)

                def act_step(i, stores):
                    c0, c1, c2 = loads(act, i - 1), loads(act, i), loads(act, i + 1)
                    with act.If(c1 < c2):
                        ei_high(i + 1, c1)
                    if stores:
                        store_rows(i - 1)
                    hidden_high(i)
                    with act.If(c0 < c1):
                        eo_high(i, c0)
                    silu(i + 1)
                    row_high(i + 2)

                ei_high(0, loads(act, -1))
                row_high(0)
                silu(0)
                row_high(1)
                act_step(0, False)
                with act.Fori(1, last) as i:
                    act_step(i, True)
                store_rows(before_last)
                hidden_high(last)
                c0, c1 = loads(act, before_last), loads(act, last)
                with act.If(c0 < c1):
                    eo_high(last, c0)
                store_rows(last)

                act.preload_act_table_set("natural_log_exp_and_others")
                for t in range(NT + 2):
                    if t < NT:
                        act.wait_ge(f_var, at(f_var, t + 1))
                        b = 4 * (t % 2)
                        nc.scalar.activation(st[:, b + 2:b + 3], st[:, b + 1:b + 2], ACT.Ln)
                        act.drain()
                        nc.scalar.activation(st[:, b + 2:b + 3], st[:, b + 2:b + 3], ACT.Exp, scale=-0.5)
                        act.drain()
                        nc.scalar.activation(x2[t % 4], x2[t % 4], ACT.Copy, scale=st[:, b + 2:b + 3]
                                             ).then_inc(f_nrm, 1)
                    if t >= 2:
                        act.wait_ge(f_x2, at(f_x2, t - 1))
                        act.dma_start(out[0, (t - 2) * P:(t - 1) * P, :], x2[(t - 2) % 4]
                                      ).then_inc(x2_st[(t - 2) % 4], 16)
                        act.wait_ge(x2_tr, at(x2_tr, t - 1))
                        nc.scalar.activation(in_part(0, t - 2), flat([PA, PB][t % 2]).rearrange("p (k q) -> p k q", k=8),
                                             ACT.Copy, scale=SX).then_inc(x2_hi, 1)

        @block.vector
        def _(v):
            tt, ts, stt = nc.vector.tensor_tensor, nc.vector.tensor_scalar, nc.vector.scalar_tensor_tensor
            v.memset(zeros, 0.0).then_inc(zero_ok, 1)
            for s, n in ((w_used, 2), (pv_mm, 1), (pt_tr, 1), (pt_cp, 1), (o_ev, 1), (ot_cp, 1),
                         (wbr_lo, 2), (g_mul, 4), (g_sig, 4), (o_rd, 2), (wei_used, KD), (weo_used, KF), (ei_lo, KD), (eo_lo, KF),
                         (y_ev, 1), (y_st, 16), (y_used, 2), (x2_st[0], 16), (x2_st[1], 16), (x2_st[2], 16), (x2_st[3], 16),):
                v.sem_inc(s, n)
            v.memset(tabf[:, :], 0.0)
            lb = WK[0:1, 2048:2048 + 2 * BW]
            ex = WK[0:1, 3072:3072 + 2 * BW]
            v.wait_ge(lb_ld, 16)
            tt(WK[0:1, 2560:2560 + BW], lb[:, 0:BW], lb[:, BW:2 * BW], ALU.max)
            v.drain()
            tt(lb[:, 0:BW], lb[:, 0:BW], WK[0:1, 2560:2560 + BW], ALU.subtract)
            tt(lb[:, BW:2 * BW], lb[:, BW:2 * BW], WK[0:1, 2560:2560 + BW], ALU.subtract).then_inc(lb_v, 1)
            v.wait_ge(lb_a, 1)
            tt(WK[0:1, 2560:2560 + BW], ex[:, 0:BW], ex[:, BW:2 * BW], ALU.add)
            v.drain()
            nc.vector.reciprocal(WK[0:1, 2560:2560 + BW], WK[0:1, 2560:2560 + BW])
            v.drain()
            tt(ex[:, BW:2 * BW], ex[:, BW:2 * BW], WK[0:1, 2560:2560 + BW], ALU.mult)
            v.drain()
            ts(ex[:, BW:2 * BW], ex[:, BW:2 * BW], -1.0, 1.0, ALU.mult, ALU.add)
            v.memset(ex[:, 0:BW], 1.0)
            v.drain().then_inc(lb_v, 1)
            v.wait_ge(c_ld, 16)
            def low_part(dst, src, scale, high):
                return stt(dst, src, scale, high, ALU.mult, ALU.subtract)

            for t in range(NT + MT):
                v.wait_ge(nat_a, t + 1)
                low_part(in_part(1, t), flat([PA, PB][t % 2]).rearrange("p (k q) -> p k q", k=8), SX, in_part(0, t)
                         ).then_inc(nat_v, 1)
            v.wait_ge(misc_ld, 48)

            with v.Fori(0, LAYERS) as l:
                at = lambda s, n: l * per[s.name] + n

                def low_parts(u, chunks=range(8), d=None, b=None):
                    slot = u % 2 if b is None else b
                    c0 = 8 * u if d is None else 8 * u + d * 8
                    n = w_width(u)
                    for k in chunks:
                        v.wait_ge(w_hi, at(w_hi, c0 + k + 1))
                        low_part(WS[slot][:, k, 1, 0:n], W[slot][:, k + SPARE, 0:n], SW, WS[slot][:, k, 0, 0:n]
                                 ).then_inc(w_lo, 1)

                v.memset(rstate[:, :, :], 0.0)
                v.memset(hstate[:, 0, 0, :, :], 0.0)
                for u in range(4):
                    low_parts(u)
                v.wait_ge(par_ld, at(par_ld, 96))
                for t in range(NT):
                    v.wait_ge(pj, at(pj, 17 + t))
                    src = PA[:, t % 2, :]
                    stt(FV[:, t, :], src[:, 0:BW], UN, BR[:, 0:BW], ALU.mult, ALU.add)
                    stt(ZF[:, 0, t * H:(t + 1) * H], src[:, BW:BW + H], UN, BR[:, BW:BW + H], ALU.mult, ALU.add
                        ).then_inc(pj_v, 1)
                    if t % 2 == 1:
                        low_parts(4, range(t - 1, t + 1))
                v.wait_ge(z_a, at(z_a, 1))
                stt(ZF[:, 0, :], ZF[:, 0, :], 0.0, ZF[:, 3, :], ALU.min, ALU.subtract).then_inc(z_v, 1)

                def evict_proj(j, dst, c0):
                    v.wait_ge(pj, at(pj, j + 1))
                    stt(dst, PA[:, j % 2, :], UN, BR[:, c0 - C_FV:c0 - C_FV + HALF], ALU.mult, ALU.add
                        ).then_inc(pj_v, 1)

                lf_row, c_sum = WK[0:H, 2 * T:3 * T], WK[0:H, 3 * T:4 * T]
                v.wait_ge(lf_tr, at(lf_tr, 1))
                nc.vector.tensor_copy(lf_row, flat(PC)[0:H, :])
                v.drain()
                nc.vector.tensor_tensor_scan(c_sum, co("ones")[0:H, 0:1].to_broadcast([H, T]), lf_row, 0.0,
                                             ALU.mult, ALU.add).then_inc(c_row, 1)
                low_parts(5)
                v.wait_ge(mt_st, 16)
                evict_proj(24, RN[:, 0, 0:HALF], C_RQ)
                evict_proj(25, RN[:, 0, HALF:2 * HALF], C_RQ + HALF)
                for h in range(H):
                    v.wait_ge(cb_mm, at(cb_mm, h + 1))
                    ts(cb[h], flat(PC), -1.0 / QK_SCALE, None, ALU.mult).then_inc(cb_cp, 1)

                def low_ot(c, branch, t):
                    v.wait_ge(ot_hi, at(ot_hi, c + 1))
                    hi, lo = (OTS[:, i, 2 * branch:2 * branch + 2, t * P:(t + 1) * P] for i in range(2))
                    low_part(lo, turned(branch).rearrange("p (j q) -> p j q", j=2), SX, hi).then_inc(ot_cp, 1)

                units = att_units()
                N = len(units)

                def softmax_max(n):
                    t, i = units[n]
                    b = n % 2
                    s = WK[:, b * T:(b + 1) * T]
                    v.wait_ge(s_mm, at(s_mm, n + 1))
                    if i < H:
                        w = (t + 1) * P
                        v.wait_ge(pt_tr, at(pt_tr, n))
                        v.sem_inc(passed, 1)
                        nc.vector.tensor_tensor_reduce(s[:, 0:w], flat(PB, w), cb[i][:, 0:w], QK_SCALE, 2 * NEG,
                                                       ALU.add, ALU.max, nm[:, b, 0:1]).then_inc(s_rd, 1)
                        v.drain()
                        ts(nm[:, b, 4:5], nm[:, b, 0:1], -1.0, None, ALU.mult).then_inc(mx_ok, 1)
                    else:
                        nc.vector.tensor_reduce(nm[:, b, 0:H], flat(PB).rearrange("p (h m) -> p h m", h=H), AX.X, ALU.max)
                        v.drain()
                        ts(nm[:, b, 4:8], nm[:, b, 0:4], -QK_SCALE, None, ALU.mult).then_inc(mx_ok, 1)

                def normalize(n):
                    t, i = units[n]
                    v.wait_ge(pv_mm, at(pv_mm, n + 2))
                    if i < H:
                        nc.vector.reciprocal(rs[:, n % 4, 0:1], rs[:, n % 4, 0:1])
                        v.drain()
                        ts(ON[:, 0, i * HD:(i + 1) * HD], PD[:, 0, 0:HD], rs[:, n % 4, 0:1], None,
                           ALU.mult).then_inc(o_ev, 1)
                    else:
                        nc.vector.reciprocal(rs[:, n % 4, :], rs[:, n % 4, :])
                        v.drain()
                        tt(heads(ON[:, 1, :]), heads(PD[:, 0, 0:BW]), over(rs[:, n % 4, :], HD), ALU.mult
                           ).then_inc(o_ev, 1)

                for n in range(N + 4):
                    if n >= 4 and units[n - 4][1] >= H - 1:
                        t, i = units[n - 4]
                        low_ot(2 * t + (i == H), 0 if i < H else 3, t)
                    if N - 4 <= n < N:
                        i = n - (N - 4)
                        low_parts(6 + i // 2, range(4 * (i % 2), 4 * (i % 2) + 4))
                    if n < N:
                        if units[n][1] == 0 and units[n][0] > 0:
                            t = units[n][0]
                            if t == NT - 1:
                                v.wait_ge(zero_st, 16)
                            evict_proj(24 + 2 * t, RN[:, t, 0:HALF], C_RQ)
                            evict_proj(25 + 2 * t, RN[:, t, HALF:2 * HALF], C_RQ + HALF)
                        softmax_max(n)
                    if 2 <= n < N + 2:
                        normalize(n - 2)

                v.wait_ge(r_sil, at(r_sil, 1))
                A4, B4, ROT = WK[:, 0:512], WK[:, 512:1024], WK[:, 1024:1536]
                KDC = [WK[:, 1536:1792], WK[:, 3584:3840]]
                QKT, QDT, STM = WK[:, 1792:2304], WK[:, 2304:2560], WK[:, 2560:3072]
                CEN, SQ = WK[:, 3072:3328], WK[:, 3328:3584]

                def group_norm_stats(o, done):
                    nc.vector.tensor_reduce(st[:, 0:4].rearrange("p (j a) -> p j a", j=2), o, AX.X, ALU.add)
                    v.drain()
                    ts(st[:, 0:4], st[:, 0:4], 1.0 / HD, None, ALU.mult)
                    v.drain()
                    tt(paired(CEN), o, over4(st[:, 0:4]), ALU.subtract)
                    v.drain()
                    tt(SQ, CEN, CEN, ALU.mult)
                    v.drain()
                    nc.vector.tensor_reduce(st[:, 4:8], heads(SQ), AX.X, ALU.add)
                    v.drain()
                    ts(st[:, 4:8], st[:, 4:8], 1.0 / HD, GN_EPS, ALU.mult, ALU.add).then_inc(done, 1)

                def rotate(t):
                    X8 = RN[:, t, 0:HALF].rearrange("p (h d) -> p h d", h=8)
                    cs = co("cos")[:, t * 32:(t + 1) * 32].unsqueeze(1).to_broadcast([P, 16, 32])
                    tt(A4.rearrange("p (h d) -> p h d", h=16),
                       RN[:, t, 0:HALF].rearrange("p (h d) -> p h d", h=16), cs, ALU.mult)
                    for a in range(2):
                        sn = co("sin")[:, t * HD + 32 * a:t * HD + 32 * a + 32].unsqueeze(1).to_broadcast([P, 8, 32])
                        tt(B4.rearrange("p (h d) -> p h d", h=8)[:, :, 32 * a:32 * a + 32],
                           X8[:, :, 32 - 32 * a:64 - 32 * a], sn, ALU.mult)
                    v.drain()
                    tt(ROT, A4, B4, ALU.add)
                    v.drain()
                    tt(heads(KDC[t % 2]), heads(ROT[:, BW:2 * BW]), over(co("kdec"), HD), ALU.mult).then_inc(r_rot, 1)

                rotate(0)
                for t in range(NT):
                    evict_proj(40 + 2 * t, HN[:, t, 0:HALF], C_HF)
                    v.wait_ge(r_qk, at(r_qk, t + 1))
                    tt(QDT, QKT[:, 0:BW], co("qdec"), ALU.mult)
                    if t >= 1:
                        low_ot(2 * NT + t - 1, 1, t - 1)
                    v.wait_ge(r_sc, at(r_sc, t + 1))
                    tt(paired(STM), by_bank(PC, P), paired(co("rmask")), ALU.mult).then_inc(r_mk, 1)
                    if t + 1 < NT:
                        rotate(t + 1)
                    evict_proj(41 + 2 * t, HN[:, t, HALF:2 * HALF], C_HF + HALF)
                    v.wait_ge(r_o, at(r_o, t + 1))
                    tt(rstate[:, :, :], rstate[:, :, :], over(co("gtile"), HD), ALU.mult)
                    v.drain()
                    tt(rstate[:, :, :], rstate[:, :, :], PD[:, 0, 0:2 * HD].rearrange("p (j d) -> p j d", j=2), ALU.add)
                    group_norm_stats(by_bank(PB, HD), r_var)
                    v.wait_ge(r_rstd, at(r_rstd, t + 1))
                    tt(heads(CEN), heads(CEN), over(st[:, 8:12], HD), ALU.mult)
                    v.drain()
                    tt(ON[:, t % 2, :], CEN, RN[:, t, 3 * BW:4 * BW], ALU.mult).then_inc(r_on, 1)

                low_ot(3 * NT - 1, 1, NT - 1)

                v.wait_ge(h_sig, at(h_sig, 1))
                tt(HN[:, :, 0:BW], HN[:, :, 0:BW], omlb[:, :].unsqueeze(1).to_broadcast([P, NT, BW]), ALU.mult
                   ).then_inc(h_kf, 1)
                v.wait_ge(h_sil, at(h_sil, 1))
                AT = WK[:, 3072:3584]
                E1, E2, E3, E1N = (WK[:, 256 + 256 * i:512 + 256 * i] for i in range(4))
                QM, Q2, KM, K3 = (WK[:, 1280 + 256 * i:1536 + 256 * i] for i in range(4))
                N1 = WK[:, 3584:3840]
                v.wait_ge(ot_tr, at(ot_tr, 3 * NT))
                v.memset(AT, 0.0)
                v.drain()
                def decayed(t):
                    kf, val, q = (HN[:, t, i * BW:(i + 1) * BW] for i in range(3))
                    v.wait_ge(h_e, at(h_e, t + 1))
                    tt(K3, kf, E3, ALU.mult)
                    tt(QM, q, E1, ALU.mult)
                    tt(Q2, q, E2, ALU.mult)
                    tt(KM, kf, E1N, ALU.mult).then_inc(h_pr, 1)

                decayed(0)
                for t in range(NT):
                    a, b = t % 2, (t + 1) % 2
                    v.wait_ge(h_kv, at(h_kv, t + 1))
                    kv = PA[:, :, 0:2 * HD].rearrange("p c (j d) -> p c j d", j=2)
                    tt(hstate[:, a, 1, :, :], hstate[:, a, 0, :, :], over(hdec[:, t % 2, :, 0], HD), ALU.mult)
                    v.drain()
                    tt(hstate[:, a, 1, :, :], hstate[:, a, 1, :, :], kv[:, 0, :, :], ALU.add)
                    v.drain()
                    tt(hstate[:, b, 0, :, :], hstate[:, a, 1, :, :], over(hdec[:, t % 2, :, 1], HD), ALU.mult)
                    v.drain()
                    tt(hstate[:, b, 0, :, :], hstate[:, b, 0, :, :], kv[:, 1, :, :], ALU.add).then_inc(h_st, 1)
                    v.wait_ge(h_a, at(h_a, t + 1))
                    v.sem_inc(passed, 1)
                    nc.vector.copy_predicated(paired(AT),
                                              hmask[:, :].unsqueeze(1).unsqueeze(1).to_broadcast([P, 2, 2, P]),
                                              by_bank(PA, P, P)).then_inc(h_am, 1)
                    if t + 1 < NT:
                        decayed(t + 1)
                    if t >= 1:
                        low_ot(3 * NT + t - 1, 2, t - 1)
                    if t >= 4:
                        low_parts(GATE_U, range(2 * (t - 4), 2 * (t - 4) + 2))
                    v.wait_ge(h_sq, at(h_sq, t + 1))
                    nc.vector.tensor_reduce(st[:, 4:8], heads(WK[:, 3840:4096]), AX.X, ALU.add)
                    v.drain()
                    ts(st[:, 4:8], st[:, 4:8], 1.0 / HD, GN_EPS, ALU.mult, ALU.add).then_inc(h_var, 1)
                    v.wait_ge(h_rstd, at(h_rstd, t + 1))
                    tt(paired(N1), by_bank(PD, HD, 2 * P), over4(st[:, 8:12]), ALU.mult)
                    v.drain()
                    tt(heads(N1), heads(N1), ngain[:, :].unsqueeze(1).to_broadcast([P, H, HD]), ALU.mult)
                    v.drain()
                    tt(ON[:, t % 2, :], N1, HN[:, t, 3 * BW:4 * BW], ALU.mult).then_inc(h_on, 1)

                low_ot(4 * NT - 1, 2, NT - 1)

                acc, tmp = WK[:, 2048:2560], WK[:, 2560:3072]
                with v.Fori(0, KD // 2) as dd:
                    for q in range(16):
                        b, half, n = q // 8, q // 4 % 2, q % 4
                        if q % 8 == 0:
                            v.wait_ge(wbr_hi, at(wbr_hi, b + 1) + dd * 2)
                            low_part(WBS[b][:, 1, :, :], WBR[b], SW, WBS[b][:, 0, :, :]).then_inc(wbr_lo, 1)
                        if q % 8 == 2:
                            low_parts(GATE_U + 1 + b, d=2 * dd, b=1 - b)
                        v.wait_ge(g_sig, at(g_sig, q + 5) + dd * 16)
                        sg = WK[:, (q % 4) * HALF:(q % 4 + 1) * HALF]
                        up = [PC, PD][(q % 4) // 2][:, q % 2, :]
                        stt(acc if n == 0 else tmp, up, UN, sg, ALU.mult, ALU.mult).then_inc(g_mul, 1)
                        v.drain()
                        if n in (1, 2):
                            tt(acc, acc, tmp, ALU.add)
                            v.drain()
                        if n == 3:
                            mix = WK[:, 3072:3584]
                            tt(mix, acc, tmp, ALU.add).then_inc(mix_f, 1)
                            v.wait_ge(mix_hi, at(mix_hi, q // 4 + 1) + dd * 4)
                            v.sem_inc(passed, 1)
                            hi, lo = (MIXS[:, i, bass.ds(dd * 2 + b, 1), half * HALF:(half + 1) * HALF] for i in range(2))
                            low_part(lo, mix.unsqueeze(1), SX, hi).then_inc(mix_ok, 1)
                            v.drain()
                low_parts(OUT_U + 1)

                def norm_stats(r, done, b=0, scale=1.0):
                    for i in range(2):
                        nc.vector.bn_stats(st[:, 8 + 6 * i:14 + 6 * i], r[:, i * HALF:(i + 1) * HALF])
                    v.drain()
                    nc.vector.bn_aggr(st[:, b:b + 2], st[:, 8:20])
                    v.drain()
                    ts(st[:, b + 1:b + 2], st[:, b + 1:b + 2], scale * scale, LN_EPS, ALU.mult, ALU.add).then_inc(done, 1)

                for t in range(NT):
                    v.wait_ge(o_mm, at(o_mm, t + 1))
                    v.wait_ge(xr_ld[t % 2], at(xr_ld[t % 2], 16 * (t // 2 + 1)))
                    if t >= 2:
                        v.wait_ge(o_x1, at(o_x1, t - 1))
                    r = WK[:, (t % 2) * D:(t % 2 + 1) * D]
                    stt(r, xres[t % 2], ALPHA / UN, flat([PA, PB][t % 2]), ALU.mult, ALU.add).then_inc(o_rd, 1)
                    v.drain()
                    norm_stats(r, o_var, 0, UN)
                    v.wait_ge(o_rstd, at(o_rstd, t + 1))
                    ts(st[:, 2:3], st[:, 2:3], UN, None, ALU.mult)
                    v.drain()
                    ts(r, r, st[:, 0:1], st[:, 2:3], ALU.subtract, ALU.mult).then_inc(o_nrm, 1)

                v.wait_ge(lg_mm, at(lg_mm, NT))
                v.wait_ge(o_x1, at(o_x1, NT))

                def te(i):
                    return WK[:, i * NT * E:(i + 1) * NT * E]

                def t3(ap, n=NT):
                    return ap.rearrange("p (t e) -> p t e", t=n)

                pr, s1, s2, both, idx, big = (te(i) for i in range(6))
                small = WK[:, 3072:4096]
                m8, mi, gm = small[:, 0:NT], small[:, 16:16 + NT], small[:, 32:32 + NT * NG]
                gs, gi = small[:, 64:64 + NT * NG], small[:, 96:96 + NT * NG]
                tt(t3(pr), t3(PD[:, 0, 0:NT * E]), brt[:, :].unsqueeze(1).to_broadcast([P, NT, E]), ALU.add)
                v.drain()
                nc.vector.tensor_reduce(m8, t3(pr), AX.X, ALU.max)
                v.drain()
                tt(t3(pr), t3(pr), over(m8, E), ALU.subtract).then_inc(rt_v, 1)
                v.wait_ge(rt_a, at(rt_a, 1))
                nc.vector.tensor_reduce(m8, t3(pr), AX.X, ALU.add)
                v.drain()
                nc.vector.reciprocal(m8, m8)
                v.drain()
                tt(t3(pr), t3(pr), over(m8, E), ALU.mult)
                v.drain()
                nc.vector.tensor_reduce(gm, t3(pr, NT * NG), AX.X, ALU.max)
                v.drain()

                def first_of_max(val, n, iota, sel, scratch):
                    nc.vector.tensor_reduce(m8, t3(val), AX.X, ALU.max)
                    v.drain()
                    tt(t3(sel), t3(val), over(m8, n), ALU.is_equal)
                    v.drain()
                    stt(t3(scratch), t3(sel), -100.0, iota.unsqueeze(1).to_broadcast([P, NT, n]), ALU.mult, ALU.add)
                    v.drain()
                    nc.vector.tensor_reduce(mi, t3(scratch), AX.X, ALU.min)
                    v.drain()
                    tt(t3(sel), t3(scratch), over(mi, n), ALU.is_equal)
                    v.drain()

                first_of_max(gm, NG, co("iota4"), gs, gi)
                tt(t3(pr, NT * NG), t3(pr, NT * NG), over(gs, EPG), ALU.mult)
                ts(gi, gs, -1.0, None, ALU.add)
                v.drain()
                tt(t3(pr, NT * NG), t3(pr, NT * NG), over(gi, EPG), ALU.add)
                v.drain()
                first_of_max(pr, E, co("iota16"), s1, idx)
                nc.vector.tensor_copy(m12[:, 0, :], m8)
                v.drain()
                stt(pr, s1, -10.0, pr, ALU.mult, ALU.add)
                v.drain()
                first_of_max(pr, E, co("iota16"), s2, idx)
                nc.vector.tensor_copy(m12[:, 1, :], m8)
                tt(both, s1, s2, ALU.add).then_inc(sel_ok, 1)
                v.drain()
                tt(m8, m12[:, 0, :], m12[:, 1, :], ALU.add)
                v.drain()
                nc.vector.reciprocal(m8, m8)
                v.drain()
                for j in range(2):
                    tt(m12[:, 2 + j, :], m12[:, j, :], m8, ALU.mult)

                v.wait_ge(rank_mm, at(rank_mm, 1))
                tot = big
                off = te(6)
                nc.vector.tensor_copy(tot, PD[:, 1, NT * E:2 * NT * E])
                v.memset(off[:, 0:E], 0.0)
                v.drain()
                for t in range(1, NT):
                    tt(off[:, t * E:(t + 1) * E], off[:, (t - 1) * E:t * E], tot[:, (t - 1) * E:t * E], ALU.add)
                    v.drain()
                cnt, ntl, cum, base = (small[:, 128 + 16 * i:144 + 16 * i] for i in range(4))
                tt(cnt, off[:, (NT - 1) * E:NT * E], tot[:, (NT - 1) * E:NT * E], ALU.add)
                v.drain()
                tt(t3(idx, E), over(cnt, 8), co("thr").unsqueeze(1).to_broadcast([P, E, 8]), ALU.is_gt)
                v.drain()
                nc.vector.tensor_reduce(ntl, t3(idx, E), AX.X, ALU.add)
                v.drain()
                nc.vector.tensor_tensor_scan(cum, co("ones")[:, 0:E], ntl, 0.0, ALU.mult, ALU.add)
                v.drain()
                tt(base, cum, ntl, ALU.subtract)
                v.drain()
                ts(base, base, float(P), None, ALU.mult)
                v.drain()
                tt(t3(off), t3(off), base.unsqueeze(1).to_broadcast([P, NT, E]), ALU.add)
                v.drain()
                tt(off, off, PD[:, 1, 0:NT * E], ALU.add)
                v.drain()
                for j, s in enumerate((s1, s2)):
                    tt(s, s, off, ALU.mult)
                    v.drain()
                    nc.vector.tensor_reduce(gm[:, j * NT:(j + 1) * NT], t3(s), AX.X, ALU.add)
                    v.drain()
                    nc.vector.tensor_copy(slots[:, j, :], gm[:, j * NT:(j + 1) * NT])
                exq = small[:, 256:256 + TILES * E]
                tt(tabf[:, TILES + 1:TILES + 2], tabf[:, TILES + 1:TILES + 2], tabf[:, TILES:TILES + 1], ALU.add)
                has, begin = (small[:, 192 + 16 * i:208 + 16 * i] for i in range(2))
                tt(begin, cum, ntl, ALU.subtract)
                ts(has, ntl, 0.0, None, ALU.is_gt)
                nc.vector.tensor_copy(tabf[:, TAB_C:TAB_C + 1], tabf[:, TAB_W - 1:TAB_W])
                tt(t3(exq, TILES), cum.unsqueeze(1).to_broadcast([P, TILES, E]), over(co("iota32"), E), ALU.is_le)
                v.drain()
                nc.vector.tensor_reduce(tabf[:, 0:TILES], t3(exq, TILES), AX.X, ALU.add)
                nc.vector.tensor_copy(tabf[:, TILES:TILES + 1], cum[:, E - 1:E])
                ts(tabf[:, TILES + 2:TILES + 3], cum[:, E - 1:E], -2.0, None, ALU.add)
                v.drain()
                ts(tabf[:, 0:TILES], tabf[:, 0:TILES], float(E - 1), None, ALU.min)
                tt(t3(exq, TILES), begin.unsqueeze(1).to_broadcast([P, TILES, E]), over(co("iota32"), E), ALU.is_le)
                v.drain()
                tt(t3(exq, TILES), t3(exq, TILES), has.unsqueeze(1).to_broadcast([P, TILES, E]), ALU.mult)
                v.drain()
                nc.vector.tensor_reduce(tabf[:, TAB_C + 1:TAB_W], t3(exq, TILES), AX.X, ALU.add)
                v.drain()
                ts(tabf[:, TAB_C + 1:TAB_W], tabf[:, TAB_C + 1:TAB_W], tabf[:, TAB_C:TAB_C + 1], None, ALU.add)
                v.drain()
                nc.vector.tensor_copy(tab[:, :], tabf[0:1, :])
                v.drain().then_inc(tab_ok, 1)

                before_last = v.value_load(tab[0:1, TILES + 2:TILES + 3], min_val=E - 2, max_val=TILES - 3)
                last = before_last + 1
                g0 = v.value_load(tab[0:1, TILES + 1:TILES + 2], min_val=0, max_val=TILES)

                def ei_low(before):
                    for k in range(KD):
                        v.wait_ge(ei_hi, before * KD + (k + 1))
                        low_part(EIS[:, 1, k, :], WEI[:, k, :], SW, EIS[:, 0, k, :]).then_inc(ei_lo, 1)

                def eo_low(before):
                    for k in range(KF):
                        v.wait_ge(eo_hi, before * KF + (k + 1))
                        low_part(EOS[:, 1, k, :], WEO[:, k, :], SW, EOS[:, 0, k, :]).then_inc(eo_lo, 1)

                def row_low(i):
                    v.wait_ge(row_hi, g0 + i + (l + 1))
                    low_part(ROWS[:, 1, :], flat(PC), SX, ROWS[:, 0, :]).then_inc(row_lo, 1)

                def hidden_low(i):
                    v.wait_ge(hid_hi, g0 + i + 1)
                    low_part(HIDS[:, 1, :], PD[:, 0, :], SX, HIDS[:, 0, :]).then_inc(hid_lo, 1)

                def hidden(i):
                    v.wait_ge(hid_sil, g0 + i + 1)
                    stt(WK[:, 512:1024], PA[:, 1, :], UN, WK[:, 0:512], ALU.mult, ALU.mult).then_inc(hid_ok, 1)

                ei_low(loads(v, -1))
                row_low(0)
                hidden(0)
                row_low(1)
                with v.Fori(0, last) as i:
                    c0, c1, c2 = loads(v, i - 1), loads(v, i), loads(v, i + 1)
                    with v.If(c1 < c2):
                        ei_low(c1)
                    hidden_low(i)
                    with v.If(c0 < c1):
                        eo_low(c0)
                    hidden(i + 1)
                    row_low(i + 2)
                hidden_low(last)
                c0, c1 = loads(v, before_last), loads(v, last)
                with v.If(c0 < c1):
                    eo_low(c0)

                v.wait_ge(x1a_ok, at(x1a_ok, 1))
                for t in range(NT + 3):
                    if t < NT:
                        v.wait_ge(y_ld[t % 2], at(y_ld[t % 2], 32 * (t // 2 + 1)))
                        if t >= 4:
                            v.wait_ge(x2_st[t % 4], at(x2_st[t % 4], 32))
                            v.wait_ge(x2_tr, at(x2_tr, t - 3))
                        y1, y2 = (OT[:, (2 * (t % 2) + j) * D:(2 * (t % 2) + j + 1) * D] for j in range(2))
                        r, b = x2[t % 4], 4 * (t % 2)
                        stt(r, y1, m12[:, 2, t:t + 1], X1[:, t, :], ALU.mult, ALU.add)
                        v.drain()
                        stt(r, y2, m12[:, 3, t:t + 1], r, ALU.mult, ALU.add).then_inc(y_used, 1)
                        v.drain()
                        if t >= 2:
                            v.wait_ge(f_nrm, at(f_nrm, t - 1))
                        if t == 0:
                            v.wait_ge(ln2_ld, at(ln2_ld, 32))
                        norm_stats(r, f_ms, b)
                        stt(r, r, st[:, b:b + 1], lnp[2], ALU.subtract, ALU.mult).then_inc(f_var, 1)
                    if t >= 3:
                        v.wait_ge(x2_hi, at(x2_hi, t - 2))
                        low_part(in_part(1, t - 3), flat([PA, PB][(t - 3) % 2]).rearrange("p (k q) -> p k q", k=8), SX,
                                 in_part(0, t - 3)).then_inc(x2_cp, 1)
                for i in range(4):
                    v.wait_ge(x2_st[i], at(x2_st[i], 48))
                    v.sem_inc(passed, 1)

        @block.tensor
        def _(pe):
            mm = nc.tensor.matmul

            def transposes(dst, src, n):
                for k in range(n):
                    q = nc.tensor.transpose(flat(dst)[:, k * P:(k + 1) * P], src[:, k * P:(k + 1) * P], ident)
                return q

            pe.wait_ge(c_ld, 16)
            for t in range(NT + MT):
                pe.wait_ge(nat_ld[t], 16)
                if t >= 2:
                    pe.wait_ge(nat_a, t - 1)
                    pe.wait_ge(nat_v, t - 1)
                src = RC[:, t * D:(t + 1) * D] if t < NT else OT[:, (t - NT) * D:(t - NT + 1) * D]
                transposes([PA, PB][t % 2], src, 8).then_inc(nat_tr, 1)
            pe.wait_ge(nat_a, NT + MT)
            pe.wait_ge(nat_v, NT + MT)
            pe.wait_ge(misc_ld, 48)
            with pe.Fori(0, LAYERS) as l:
                at = lambda s, n: l * per[s.name] + n

                def product(dst, lhs, rhs, first, last):
                    mm(dst, lhs(0), rhs(0), start=first, stop=False)
                    mm(dst, lhs(0), rhs(1), start=False, stop=False)
                    return mm(dst, lhs(1), rhs(0), start=False, stop=last)

                def unit_loaded(u):
                    pe.wait_ge(w_lo, at(w_lo, 8 * (u + 1)))

                def bank_free(j):
                    if 2 <= j < 18:
                        pe.wait_ge(pj_a, at(pj_a, j - 1))
                    elif j >= 18:
                        pe.wait_ge(pj_v, at(pj_v, j - 17))

                def project(j, n, lhs, rhs):
                    bank_free(j)
                    for k in range(KD):
                        q = product(PA[:, j % 2, 0:n], lambda i: lhs(k, i), lambda i: rhs(k, i), k == 0, k == KD - 1)
                    q.then_inc(pj, 1)
                    return q

                unit_loaded(0)
                for j in range(2):
                    project(j, BW, lambda k, i: WS[0][:, k, i, j * P:(j + 1) * P], lambda k, i: memS[:, i, k, :])
                for j in range(2):
                    project(2 + j, BW, lambda k, i: memS[:, i, k, j * P:(j + 1) * P],
                            lambda k, i: WS[0][:, k, i, BW:2 * BW])
                pe.drain().then_inc(w_used, 1)
                pe.wait_ge(par_ld, at(par_ld, 96))
                pe.sem_inc(passed, 1)
                nc.tensor.transpose(PD[:, 0, 0:6 + NBR * KD], b_rows, ident[0:6 + NBR * KD, 0:6 + NBR * KD]
                                    ).then_inc(bt_tr, 1)
                for u, c0, n in ((1, 0, 4), (2, 4, 2)):
                    unit_loaded(u)
                    for c in range(n):
                        for half in range(2):
                            project(4 + (c0 + c) * 2 + half, HALF,
                                    lambda k, i: WS[u % 2][:, k, i, c * P:(c + 1) * P],
                                    lambda k, i: XS[:, i, k, half * HALF:(half + 1) * HALF])
                    pe.drain().then_inc(w_used, 1)
                unit_loaded(3)
                for t in range(NT):
                    project(16 + t, BW + H, lambda k, i: XS[:, i, k, t * P:(t + 1) * P],
                            lambda k, i: WS[1][:, k, i, 0:BW + H])
                pe.drain().then_inc(w_used, 1)

                def project_pair(first, t, which, j):
                    u = first + which
                    if t == 0:
                        unit_loaded(u)
                    project(j, HALF, lambda k, i: XS[:, i, k, t * P:(t + 1) * P], lambda k, i: WS[u % 2][:, k, i, :])
                    if t == NT - 1:
                        pe.drain().then_inc(w_used, 1)

                pe.wait_ge(z_v, at(z_v, 1))
                for t in range(NT):
                    q = nc.tensor.transpose(flat(PC)[0:H, t * P:(t + 1) * P], ZF[:, 0, t * H:(t + 1) * H], ident)
                q.then_inc(lf_tr, 1)
                project_pair(4, 0, 0, 24)
                project_pair(4, 0, 1, 25)
                pe.wait_ge(c_row, at(c_row, 1))
                for h in range(H):
                    if h >= 1:
                        pe.wait_ge(cb_cp, at(cb_cp, h))
                    for half in range(2):
                        q = mm(PC[:, half, :], ident[0:H, h:h + 1].to_broadcast([H, P]),
                               WK[0:H, 3 * T + half * HALF:3 * T + (half + 1) * HALF], start=True, stop=True)
                    q.then_inc(cb_mm, 1)
                pe.wait_ge(cb_cp, at(cb_cp, H))

                units = att_units()
                N = len(units)

                def head(c, h):
                    return slice((h % 2) * HD, (h % 2 + 1) * HD), c + h // 2

                def scores(n):
                    t, i = units[n]
                    if n >= 1 and i == 0:
                        pe.wait_ge(p_ok, at(p_ok, n))
                    elif i >= 1:
                        pe.wait_ge(s_rd, at(s_rd, t * H + i))
                    if i < H:
                        rows, cq = head(0, i)
                        ck = cq + 2
                        w = (t + 1) * P
                        for c0 in range(0, w - P, HALF):
                            c1 = min(w - P, c0 + HALF)
                            mm(flat(PB)[:, c0:c1], qkT[rows, cq, t * P:(t + 1) * P], qkT[rows, ck, c0:c1],
                               start=True, stop=True)
                        mm(flat(PB)[:, w - P:w], qkT[rows, cq, t * P:(t + 1) * P], qkT[rows, ck, w - P:w],
                           start=True, stop=False)
                        q = mm(flat(PB)[:, w - P:w], ident, co("causal"), start=False, stop=True)
                    else:
                        for h in range(H):
                            rows, cq = head(4, h)
                            q = mm(flat(PB)[:, perm(h) * N_MEM:(perm(h) + 1) * N_MEM], qkT[rows, cq, t * P:(t + 1) * P],
                                   MKV[rows, h // 2, :], start=True, stop=True)
                    q.then_inc(s_mm, 1)

                def transpose_p(n):
                    t, i = units[n]
                    pe.wait_ge(p_ok, at(p_ok, n + 1))
                    pe.wait_ge(pt_cp, at(pt_cp, n + 1))
                    transposes(PC, WK[:, (n % 2) * T:(n % 2 + 1) * T], t + 1 if i < H else 8).then_inc(pt_tr, 1)

                def times_v(n):
                    t, i = units[n]
                    pt = WK[:, (2 + n % 2) * T:(3 + n % 2) * T]
                    pe.wait_ge(pt_cp, at(pt_cp, n + 2))
                    pe.wait_ge(o_ev, at(o_ev, n + 1))
                    if i < H:
                        for kt in range(t + 1):
                            q = mm(PD[:, 0, 0:HD], pt[:, kt * P:(kt + 1) * P], FV[:, kt, i * HD:(i + 1) * HD],
                                   start=kt == 0, stop=kt == t)
                    else:
                        for h in range(H):
                            for kt in range(MT):
                                q = mm(PD[:, 0, h * HD:(h + 1) * HD], pt[:, (2 * h + kt) * P:(2 * h + kt + 1) * P],
                                       MKV[:, 2 + kt, h * HD:(h + 1) * HD], start=kt == 0, stop=kt == MT - 1)
                    q.then_inc(pv_mm, 1)

                def transpose_o(c, src, branch=0):
                    pe.wait_ge(ot_cp, at(ot_cp, c + 1))
                    for j in range(2):
                        q = nc.tensor.transpose(turned(branch)[:, j * P:(j + 1) * P], src[:, j * P:(j + 1) * P], ident)
                    q.then_inc(ot_tr, 1)

                for n in range(N + 3):
                    if n < N:
                        t, i = units[n]
                        if i == 0 and t > 0:
                            project_pair(4, t, 0, 24 + 2 * t)
                            project_pair(4, t, 1, 25 + 2 * t)
                        scores(n)
                    if 1 <= n <= N:
                        transpose_p(n - 1)
                    if 2 <= n <= N + 1:
                        times_v(n - 2)
                    if n >= 3 and units[n - 3][1] >= H - 1:
                        t, i = units[n - 3]
                        pe.wait_ge(o_ev, at(o_ev, n - 1))
                        transpose_o(2 * t + (i == H), ON[:, i - H + 1, :])

                ROT, QKT = WK[:, 1024:1536], WK[:, 1792:2304]
                KDC = [WK[:, 1536:1792], WK[:, 3584:3840]]
                QDT, STM = WK[:, 2304:2560], WK[:, 2560:3072]
                for t in range(NT):
                    pe.wait_ge(r_rot, at(r_rot, t + 1))
                    for c in range(4):
                        q = nc.tensor.transpose(PC[:, 0, c * P:(c + 1) * P], ROT[:, c * P:(c + 1) * P], ident)
                    q.then_inc(r_tr, 1)
                    project_pair(6, t, 0, 40 + 2 * t)
                    if t >= 1:
                        pe.wait_ge(r_on, at(r_on, t))
                        transpose_o(2 * NT + t - 1, ON[:, (t - 1) % 2, :])
                    pe.wait_ge(r_qk, at(r_qk, t + 1))
                    for h in range(H):
                        rows, c = head(0, h)
                        q = mm(PC[:, h % 2, c * P:(c + 1) * P], QKT[rows, (2 + c) * P:(3 + c) * P],
                               QKT[rows, c * P:(c + 1) * P], start=True, stop=True)
                    q.then_inc(r_sc, 1)
                    project_pair(6, t, 1, 41 + 2 * t)
                    pe.wait_ge(r_mk, at(r_mk, t + 1))
                    for h in range(H):
                        rows, c = head(0, h)
                        val = RN[:, t, 2 * BW + h * HD:2 * BW + (h + 1) * HD]
                        mm(PB[:, h % 2, c * HD:(c + 1) * HD], STM[:, h * P:(h + 1) * P], val, start=True, stop=False)
                        mm(PB[:, h % 2, c * HD:(c + 1) * HD], QDT[rows, c * P:(c + 1) * P], rstate[rows, c, :],
                           start=False, stop=True)
                    for h in range(H):
                        rows, c = head(0, h)
                        val = RN[:, t, 2 * BW + h * HD:2 * BW + (h + 1) * HD]
                        q = mm(PD[rows, 0, c * HD:(c + 1) * HD], KDC[t % 2][:, h * HD:(h + 1) * HD], val,
                               start=True, stop=True)
                    q.then_inc(r_o, 1)
                pe.wait_ge(r_on, at(r_on, NT))
                transpose_o(3 * NT - 1, ON[:, (NT - 1) % 2, :])

                AT = WK[:, 3072:3584]
                QM, Q2, KM, K3 = (WK[:, 1280 + 256 * i:1536 + 256 * i] for i in range(4))
                TQM, TQ2, TKM = (WK[:, 2304 + 256 * i:2560 + 256 * i] for i in range(3))

                def running_sums(t):
                    pe.wait_ge(h_lf, at(h_lf, t + 1))
                    if t >= 1:
                        pe.wait_ge(h_e, at(h_e, t))
                    for i, name in enumerate(("c_mid", "c_cum", "c_rest")):
                        mm(flat(PB)[:, i * BW:(i + 1) * BW], co(name), WK[:, 0:BW], start=True, stop=True)
                    for j in range(2):
                        q = mm(PB[:, 1, BW + 2 * j:BW + 2 * j + 2], WK[:, j * P:(j + 1) * P], co("c_end"),
                               start=True, stop=True)
                    q.then_inc(h_b, 1)

                running_sums(0)
                for t in range(NT):
                    val = HN[:, t, BW:2 * BW]
                    pe.wait_ge(h_pr, at(h_pr, t + 1))
                    pe.wait_ge(ot_cp, at(ot_cp, 3 * NT + max(t, 1)))
                    for i, src in enumerate((QM, Q2, KM)):
                        for j in range(2):
                            q = nc.tensor.transpose(flat(PC)[:, (2 * i + j) * P:(2 * i + j + 1) * P],
                                                    src[:, j * P:(j + 1) * P], ident)
                    q.then_inc(h_tr, 1)
                    for c in range(2):
                        rc = slice(c * CH, (c + 1) * CH)
                        for h in range(H):
                            rows, p = head(0, h)
                            q = mm(PA[rows, c, p * HD:(p + 1) * HD], K3[rc, h * HD:(h + 1) * HD],
                                   val[rc, h * HD:(h + 1) * HD], start=True, stop=True)
                    q.then_inc(h_kv, 1)
                    pe.wait_ge(h_tc, at(h_tc, t + 1))
                    pe.wait_ge(h_st, at(h_st, t + 1))
                    for h in range(H):
                        rows, p = head(0, h)
                        q = mm(PA[:, h % 2, (p + 1) * P:(p + 2) * P], TKM[rows, p * P:(p + 1) * P],
                               TQM[rows, p * P:(p + 1) * P], start=True, stop=True)
                    q.then_inc(h_a, 1)
                    if t + 1 < NT:
                        running_sums(t + 1)
                    if t >= 1:
                        pe.wait_ge(h_on, at(h_on, t))
                        transpose_o(3 * NT + t - 1, ON[:, (t - 1) % 2, :], 2)
                    pe.wait_ge(h_am, at(h_am, t + 1))
                    for h in range(H):
                        rows, p = head(0, h)
                        o = PD[:, h % 2, 2 * P + p * HD:2 * P + (p + 1) * HD]
                        mm(o, AT[:, h * P:(h + 1) * P], val[:, h * HD:(h + 1) * HD], start=True, stop=False,
                           skip_group_check=True)
                        for c in range(2):
                            q = mm(PD[c * CH:(c + 1) * CH, h % 2, 2 * P + p * HD:2 * P + (p + 1) * HD],
                                   TQ2[rows, p * P + c * CH:p * P + (c + 1) * CH], hstate[rows, t % 2, c, p, :],
                                   start=False, stop=c == 1, skip_group_check=True)
                    q.then_inc(h_o, 1)
                pe.wait_ge(h_on, at(h_on, NT))
                transpose_o(4 * NT - 1, ON[:, (NT - 1) % 2, :], 2)

                pe.wait_ge(ot_cp, at(ot_cp, 4 * NT + 1))
                pe.sem_inc(passed, 1)
                with pe.Fori(0, KD // 2) as dd:
                    for b in range(2):
                        pe.wait_ge(w_lo, at(w_lo, 8 * (GATE_U + 1 + b)) + dd * 16)
                        for q in range(8 * b, 8 * b + 8):
                            half, n = q // 4 % 2, q % 4
                            tok = slice(half * HALF, (half + 1) * HALF)
                            pe.wait_ge(g_sig, at(g_sig, q + 1) + dd * 16)
                            pe.wait_ge(g_mul, at(g_mul, q + 1) + dd * 16)
                            for k in range(KD):
                                z = product([PA, PB][(q % 4) // 2][:, q % 2, :],
                                            lambda i: WS[b][:, k, i, n * P:(n + 1) * P],
                                            lambda i: XS[:, i, k, tok], k == 0, k == KD - 1)
                            if q % 8 == 0:
                                pe.wait_ge(wbr_lo, at(wbr_lo, b + 3) + dd * 2)
                            for j in range(2):
                                z = product([PC, PD][(q % 4) // 2][:, q % 2, :],
                                            lambda i: WBS[b][:, i, 2 * n + j, :],
                                            lambda i: OTS[:, i, 2 * n + j, tok], j == 0, j == 1)
                            z.then_inc(g_mm, 1)
                        pe.drain().then_inc(w_used, 1)

                pe.wait_ge(mix_ok, at(mix_ok, 16))
                pe.wait_ge(g_sig, at(g_sig, 64 + 4))
                unit_loaded(OUT_U)
                X1T = WK[:, 2048:3072]
                for t in range(NT + 2):
                    if t < NT:
                        if t >= 2:
                            pe.wait_ge(o_rd, at(o_rd, t + 1))
                        for o, half in {0: ((0, 0), (1, 0), (0, 1)), 1: ((1, 1),)}.get(t, ((t, 0), (t, 1))):
                            if t == 0 and half == 1:
                                unit_loaded(OUT_U + 1)
                            for k in range(KD):
                                q = product([PA, PB][o % 2][:, half, :], lambda i: MIXS[:, i, k, o * P:(o + 1) * P],
                                            lambda i: WS[half][:, k, i, :], k == 0, k == KD - 1)
                        q.then_inc(o_mm, 1)
                        if t == NT - 1:
                            pe.drain().then_inc(w_used, 2)
                    if t >= 2:
                        pe.wait_ge(x1_cp, at(x1_cp, t - 1))
                        for k in range(KD):
                            q = mm(PD[:, 0, (t - 2) * E:(t - 1) * E], X1T[:, k * P:(k + 1) * P], wr[:, k, :],
                                   start=k == 0, stop=k == KD - 1)
                        q.then_inc(lg_mm, 1)
                    if 1 <= t <= NT:
                        pe.wait_ge(o_x1, at(o_x1, t))
                        transposes(PC, X1[:, t - 1, :], 8).then_inc(x1_tr, 1)
                pe.wait_ge(sel_ok, at(sel_ok, 1))
                both = WK[:, 3 * NT * E:4 * NT * E]
                mm(PD[:, 1, 0:NT * E], co("before"), both, start=True, stop=True)
                mm(PD[:, 1, NT * E:2 * NT * E], co("ones"), both, start=True, stop=True).then_inc(rank_mm, 1)

                pe.wait_ge(tab_ok, at(tab_ok, 1))
                pe.sem_inc(passed, 1)
                before_last = pe.value_load(tab[0:1, TILES + 2:TILES + 3], min_val=E - 2, max_val=TILES - 3)
                last = before_last + 1
                g0 = pe.value_load(tab[0:1, TILES + 1:TILES + 2], min_val=0, max_val=TILES)

                def transpose_rows(i, first=False):
                    pe.wait_ge(row_ld, (g0 + i) * 16 + (l + 1) * 16)
                    if not first:
                        pe.wait_ge(row_lo, g0 + i + l)
                    transposes(PC, ROW, 8).then_inc(row_tr, 1)

                def first_product(i, c):
                    pe.wait_ge(row_lo, g0 + i + (l + 1))
                    for k in range(KD):
                        pe.wait_ge(ei_lo, c * KD + (k + 1))
                        for a, b in ((0, 0), (0, 1), (1, 0)):
                            for half in range(2):
                                q = mm(PA[:, half, :], ROWS[:, a, k * P:(k + 1) * P],
                                       EIS[:, b, k, half * HALF:(half + 1) * HALF],
                                       start=k == 0 and a + b == 0, stop=k == KD - 1 and a == 1)
                        q.then_inc(wei_used, 1)

                def transpose_hidden(i):
                    pe.wait_ge(hid_ok, g0 + i + 1)
                    for k in range(KF):
                        q = nc.tensor.transpose(PD[:, 0, k * P:(k + 1) * P], WK[:, 512 + k * P:512 + (k + 1) * P], ident)
                    q.then_inc(hid_tr, 1)

                def second_product(i, c):
                    pe.wait_ge(hid_lo, g0 + i + 1)
                    pe.wait_ge(y_ev, g0 + i + 1)
                    for k in range(KF):
                        pe.wait_ge(eo_lo, c * KF + (k + 1))
                        for a, b in ((0, 0), (0, 1), (1, 0)):
                            for half in range(2):
                                q = mm(PB[:, half, :], HIDS[:, a, k * P:(k + 1) * P],
                                       EOS[:, b, k, half * HALF:(half + 1) * HALF],
                                       start=k == 0 and a + b == 0, stop=k == KF - 1 and a == 1)
                        q.then_inc(weo_used, 1)

                transpose_rows(0, True)
                first_product(0, loads(pe, 0))
                transpose_rows(1)
                transpose_hidden(0)
                with pe.Fori(0, last) as i:
                    c1, c2 = loads(pe, i), loads(pe, i + 1)
                    first_product(i + 1, c2)
                    transpose_rows(i + 2)
                    second_product(i, c1)
                    transpose_hidden(i + 1)
                second_product(last, loads(pe, last))

                for t in range(NT):
                    pe.wait_ge(f_x2, at(f_x2, t + 1))
                    if t >= 2:
                        pe.wait_ge(x2_cp, at(x2_cp, t - 1))
                    transposes([PA, PB][t % 2], x2[t % 4], 8).then_inc(x2_tr, 1)
                pe.wait_ge(x2_cp, at(x2_cp, NT))
                pe.wait_ge(mt_ld, at(mt_ld, 16))
                pe.sem_inc(passed, 1)


def constants():
    import numpy as np
    c = np.zeros((P, N_CONST), np.float32)

    def put(name, value):
        a, b = CONST[name]
        c[:, a:b] = np.asarray(value, np.float64).reshape(P, b - a)

    i = np.arange(P)
    gamma = np.log1p(-np.exp2(-5.0 - np.arange(H)))
    put("ident", np.eye(P))
    put("causal", np.where(i[:, None] >= i[None, :], 0.0, NEG / QK_SCALE))
    j_, i_ = i[:, None], i[None, :]
    seen = (i_ // CH) >= (j_ // CH)
    put("rmask", np.stack([np.where(seen, np.exp(g * np.abs(i_ - j_)), 0.0) * QK_SCALE for g in gamma], 1))
    put("qdec", np.stack([np.stack([np.exp(gamma[2 * j + p // HD] * (i + 1)) for p in range(P)]) for j in range(2)], 1))
    put("kdec", np.exp(gamma[None, :] * (P - 1 - i[:, None])) * QK_SCALE)
    put("gtile", np.stack([[np.exp(gamma[2 * j + p // HD] * P) for j in range(2)] for p in range(P)]))
    inv = (10000.0 ** (-2.0 * np.arange(HD // 2, dtype=np.float32) / HD)).astype(np.float32)
    pos = np.arange(T, dtype=np.float32)
    ang = (pos[:, None] * inv[None, :]).astype(np.float32).astype(np.float64).reshape(NT, P, HD // 2).transpose(1, 0, 2)
    put("cos", np.cos(ang))
    put("sin", np.concatenate([-np.sin(ang), np.sin(ang)], 2))
    same = (i_ // CH) == (j_ // CH)
    cum = same & (j_ <= i_)
    put("c_cum", cum)
    put("c_mid", cum * 1.0 - (same & (j_ % CH < CH // 2)))
    put("c_rest", same & (j_ > i_))
    put("c_end", np.stack([i < CH, i >= CH], 1))
    put("before", j_ < i_)
    put("ones", np.ones((P, P)))
    put("iota4", np.tile(np.arange(4), (P, 1)))
    put("iota16", np.tile(np.arange(16), (P, 1)))
    put("iota32", np.tile(np.arange(32), (P, 1)))
    put("thr", np.tile(np.arange(8) * P, (P, 1)))
    return c, (same & (j_ <= i_)).astype(np.int32)


_INS = ['x', 'mem', 'w_in', 'b_in', 'w_mem_kv', 'hgrn_lb', 'hgrn_norm_g', 'w_branch', 'w_out', 'ln_g', 'ln_b',
        'w_router', 'b_router', 'w_e_in', 'w_e_out']


def kernel(**inputs):
    import numpy as _np
    import concourse.bacc as _bacc
    from concourse import mybir as _mybir
    from concourse.bass_utils import run_bass_kernel_spmd as _run

    nc = _bacc.Bacc("TRN2", target_bir_lowering=False, num_devices=1, dynamic_dma_scratch_size=8192)
    arrays, args = {}, []
    tables, mask = constants()
    for name, a in [(n, _np.ascontiguousarray(inputs[n])) for n in _INS] + [("tables", tables), ("chunk_mask", mask)]:
        arrays[f"in_{name}_dram"] = a
        args.append(nc.dram_tensor(f"in_{name}_dram", a.shape, _mybir.dt.from_np(a.dtype), kind="ExternalInput").ap())
    args.append(nc.dram_tensor("out_0_dram", (1, T, D), F32, kind="ExternalOutput").ap())
    trunk(nc, *args)
    r = _run(nc, [arrays], core_ids=[0])
    return r.results[0]["out_0_dram"]
```
